# Optimizing a Trainium2 kernel written in Bass

```python
import jax
import jax.numpy as jnp
from jax import lax
import numpy as np

D_MODEL = 1024
BATCH = 1
SEQ = 256
DEPTH = 1

N_MEM = 256
D_MIX = D_MODEL
HEAD_DIM = 64
NSA_HEADS = 8
NSA_KV_HEADS = 2
NSA_WIDTH = NSA_HEADS * HEAD_DIM
NSA_KV_WIDTH = NSA_KV_HEADS * HEAD_DIM
CONV_WIDTH = D_MIX - NSA_WIDTH
CONV_K = 3
CMP_LEN = 32
CMP_STRIDE = 16
CMP_HIDDEN = 256
SEL_LEN = 64
N_SEL = 16
WINDOW = 512
Q_BLK = 128
ROPE_THETA = 10000.0
XATTN_HEADS = 4
XATTN_HEAD_DIM = D_MODEL // XATTN_HEADS
N_EXPERTS = 32
TOP_K = 4
D_FF = D_MODEL
SWIGLU_LIMIT = 7.0
SWIGLU_ALPHA = 1.702
MOE_BLK = 128
RMS_EPS = 1e-5
NEG_INF = -1e30
FORCED = 1e30
IN_SIZES = (NSA_WIDTH, NSA_KV_WIDTH, NSA_KV_WIDTH, NSA_KV_WIDTH, NSA_KV_WIDTH, NSA_KV_WIDTH, NSA_KV_WIDTH, 3 * NSA_HEADS, CONV_WIDTH, CONV_WIDTH, CONV_WIDTH)
IN_COLS = NSA_WIDTH + 6 * NSA_KV_WIDTH + 3 * NSA_HEADS + 3 * CONV_WIDTH

kernel_name = 'hymba_nsa_shortconv_moe_block'

def rmsnorm(t, g):
    tf = t.astype(jnp.float32)
    y = tf * lax.rsqrt(jnp.mean(tf * tf, axis=-1, keepdims=True) + RMS_EPS)
    return (y * g.astype(jnp.float32)).astype(t.dtype)

def rope(t, pos):
    half = HEAD_DIM // 2
    inv_freq = ROPE_THETA ** (-jnp.arange(half, dtype=jnp.float32) / half)
    ang = pos.astype(jnp.float32)[:, :, None] * inv_freq
    cos = jnp.cos(ang)[:, :, None, :]
    sin = jnp.sin(ang)[:, :, None, :]
    tf = t.astype(jnp.float32)
    t1, t2 = tf[..., :half], tf[..., half:]
    return jnp.concatenate([t1 * cos - t2 * sin, t2 * cos + t1 * sin], axis=-1).astype(t.dtype)

def masked_softmax(s, mask):
    return jax.nn.softmax(jnp.where(mask, s, NEG_INF), axis=-1)

def compress_blocks(t, pos_emb, w1, b1, w2):
    B, S, G, dh = t.shape
    nc = (S - CMP_LEN) // CMP_STRIDE + 1
    idx = jnp.arange(nc)[:, None] * CMP_STRIDE + jnp.arange(CMP_LEN)[None, :]
    blk = t[:, idx] + pos_emb[:, None, :]
    blk = jnp.moveaxis(blk, 3, 2).reshape(B, nc, G, CMP_LEN * dh)
    hid = jax.nn.gelu(blk @ w1 + b1)
    return hid @ w2

def nsa_attention(q, k_cmp, v_cmp, k_slc, v_slc, k_win, v_win, gate_logits,
                  cmp_pos_k, cmp_pos_v, cmp_w1_k, cmp_b1_k, cmp_w2_k, cmp_w1_v, cmp_b1_v, cmp_w2_v):
    B, S = q.shape[0], q.shape[1]
    G = NSA_KV_HEADS
    HPG = NSA_HEADS // NSA_KV_HEADS
    scale = HEAD_DIM ** -0.5
    f32 = jnp.float32
    qg = q.reshape(B, S, G, HPG, HEAD_DIM)
    s_idx = jnp.arange(S)

    kc = compress_blocks(k_cmp, cmp_pos_k, cmp_w1_k, cmp_b1_k, cmp_w2_k)
    vc = compress_blocks(v_cmp, cmp_pos_v, cmp_w1_v, cmp_b1_v, cmp_w2_v)
    nc = kc.shape[1]
    c_end = jnp.arange(nc) * CMP_STRIDE + CMP_LEN - 1
    cmask = c_end[None, :] <= s_idx[:, None]
    sc = jnp.einsum('bsghd,bcgd->bghsc', qg, kc, preferred_element_type=f32) * scale
    p_cmp = jnp.where(cmask, masked_softmax(sc, cmask), 0.0)
    o_cmp = jnp.einsum('bghsc,bcgd->bsghd', p_cmp.astype(vc.dtype), vc).reshape(B, S, NSA_HEADS, HEAD_DIM)

    ns = S // SEL_LEN
    cs = jnp.arange(nc) * CMP_STRIDE
    js = jnp.arange(ns) * SEL_LEN
    overlap = jnp.clip(jnp.minimum(cs[:, None] + CMP_LEN, js[None, :] + SEL_LEN)
                       - jnp.maximum(cs[:, None], js[None, :]), 0, None).astype(f32) / CMP_LEN
    imp = jnp.einsum('bghsc,cj->bgsj', p_cmp, overlap)
    cur = (s_idx // SEL_LEN)[:, None]
    jj = jnp.arange(ns)[None, :]
    forced = (jj == 0) | (jj == cur) | (jj == cur - 1)
    imp = jnp.where(forced, FORCED, jnp.where(jj > cur, NEG_INF, imp))
    n_top = min(N_SEL, ns)
    _, sel_idx = lax.top_k(imp, n_top)

    ks_blk = jnp.moveaxis(k_slc, 2, 1).reshape(B, G, ns, SEL_LEN, HEAD_DIM)
    vs_blk = jnp.moveaxis(v_slc, 2, 1).reshape(B, G, ns, SEL_LEN, HEAD_DIM)
    kw_pad = jnp.pad(k_win, ((0, 0), (WINDOW, 0), (0, 0), (0, 0)))
    vw_pad = jnp.pad(v_win, ((0, 0), (WINDOW, 0), (0, 0), (0, 0)))
    gather = jax.vmap(jax.vmap(lambda blk, ix: blk[ix]))
    offs = jnp.arange(SEL_LEN)
    kpos_rel = jnp.arange(WINDOW + Q_BLK) - WINDOW

    def query_block(ci):
        s0 = ci * Q_BLK
        qpos = s0 + jnp.arange(Q_BLK)
        qc = lax.dynamic_slice_in_dim(qg, s0, Q_BLK, axis=1)
        ix = lax.dynamic_slice_in_dim(sel_idx, s0, Q_BLK, axis=2)
        ksel = gather(ks_blk, ix).reshape(B, G, Q_BLK, n_top * SEL_LEN, HEAD_DIM)
        vsel = gather(vs_blk, ix).reshape(B, G, Q_BLK, n_top * SEL_LEN, HEAD_DIM)
        tpos = (ix[..., None] * SEL_LEN + offs).reshape(B, G, Q_BLK, n_top * SEL_LEN)
        smask = (tpos <= qpos[:, None])[:, :, None]
        ss = jnp.einsum('bqghd,bgqnd->bghqn', qc, ksel, preferred_element_type=f32) * scale
        ps = masked_softmax(ss, smask)
        o_s = jnp.einsum('bghqn,bgqnd->bqghd', ps.astype(vsel.dtype), vsel)
        kw = lax.dynamic_slice_in_dim(kw_pad, s0, WINDOW + Q_BLK, axis=1)
        vw = lax.dynamic_slice_in_dim(vw_pad, s0, WINDOW + Q_BLK, axis=1)
        kpos = s0 + kpos_rel
        wmask = ((kpos[None, :] <= qpos[:, None]) & (qpos[:, None] - kpos[None, :] < WINDOW)
                 & (kpos[None, :] >= 0))
        sw = jnp.einsum('bqghd,bkgd->bghqk', qc, kw, preferred_element_type=f32) * scale
        pw = masked_softmax(sw, wmask)
        o_w = jnp.einsum('bghqk,bkgd->bqghd', pw.astype(vw.dtype), vw)
        return o_s, o_w

    o_slc, o_win = lax.map(query_block, jnp.arange(S // Q_BLK))
    o_slc = jnp.moveaxis(o_slc, 0, 1).reshape(B, S, NSA_HEADS, HEAD_DIM)
    o_win = jnp.moveaxis(o_win, 0, 1).reshape(B, S, NSA_HEADS, HEAD_DIM)

    g = jax.nn.sigmoid(gate_logits.astype(f32)).astype(q.dtype)
    o = g[..., 0:1] * o_cmp + g[..., 1:2] * o_slc + g[..., 2:3] * o_win
    return o.reshape(B, S, NSA_WIDTH)

def short_gated_conv(h, b_gate, c_gate, conv_w):
    u = c_gate * h
    y = lax.conv_general_dilated(u, conv_w[:, None, :].astype(u.dtype), window_strides=(1,),
                                 padding=[(CONV_K - 1, 0)], dimension_numbers=('NWC', 'WIO', 'NWC'),
                                 feature_group_count=u.shape[-1])
    return b_gate * y

def hybrid_mixer(xn, positions, w_mix_in, cmp_pos_k, cmp_pos_v, cmp_w1_k, cmp_b1_k, cmp_w2_k,
                 cmp_w1_v, cmp_b1_v, cmp_w2_v, conv_w, g_nsa_out, g_conv_out, w_mix_out):
    B, S, _ = xn.shape
    proj = xn @ w_mix_in
    splits = np.cumsum(IN_SIZES)[:-1].tolist()
    q, kc, vc, ks, vs, kw, vw, gl, ch, cb, cc = jnp.split(proj, splits, axis=-1)
    kvshape = (B, S, NSA_KV_HEADS, HEAD_DIM)
    q = rope(q.reshape(B, S, NSA_HEADS, HEAD_DIM), positions)
    kc = rope(kc.reshape(kvshape), positions)
    ks = rope(ks.reshape(kvshape), positions)
    kw = rope(kw.reshape(kvshape), positions)
    o_nsa = nsa_attention(q, kc, vc.reshape(kvshape), ks, vs.reshape(kvshape), kw, vw.reshape(kvshape),
                          gl.reshape(B, S, NSA_HEADS, 3), cmp_pos_k, cmp_pos_v,
                          cmp_w1_k, cmp_b1_k, cmp_w2_k, cmp_w1_v, cmp_b1_v, cmp_w2_v)
    o_conv = short_gated_conv(ch, cb, cc, conv_w)
    o = jnp.concatenate([rmsnorm(o_nsa, g_nsa_out), rmsnorm(o_conv, g_conv_out)], axis=-1)
    return o @ w_mix_out

def memory_cross_attention(hn, memn, w_xq, w_xkv, w_xo):
    B, S, D = hn.shape
    M = memn.shape[1]
    q = (hn @ w_xq).reshape(B, S, XATTN_HEADS, XATTN_HEAD_DIM)
    k, v = jnp.split(memn @ w_xkv, 2, axis=-1)
    k = k.reshape(B, M, XATTN_HEADS, XATTN_HEAD_DIM)
    v = v.reshape(B, M, XATTN_HEADS, XATTN_HEAD_DIM)
    s = jnp.einsum('bshd,bmhd->bhsm', q, k, preferred_element_type=jnp.float32) * XATTN_HEAD_DIM ** -0.5
    p = jax.nn.softmax(s, axis=-1)
    o = jnp.einsum('bhsm,bmhd->bshd', p.astype(v.dtype), v).reshape(B, S, D)
    return o @ w_xo

def moe_ffn(xn, w_router, b_router, w_gate_up, b_gate_up, w_down, b_down):
    B, S, D = xn.shape
    T = B * S
    A = T * TOP_K
    xt = xn.reshape(T, D)
    logits = (xt @ w_router + b_router).astype(jnp.float32)
    top_v, top_e = lax.top_k(logits, TOP_K)
    gate = jax.nn.softmax(top_v, axis=-1)
    e_flat = top_e.reshape(A).astype(jnp.int32)
    tok_flat = jnp.repeat(jnp.arange(T, dtype=jnp.int32), TOP_K)
    w_flat = gate.reshape(A)
    order = jnp.argsort(e_flat)
    e_sorted = e_flat[order]
    counts = jnp.bincount(e_flat, length=N_EXPERTS).astype(jnp.int32)
    padded = (counts + MOE_BLK - 1) // MOE_BLK * MOE_BLK
    start = jnp.cumsum(counts) - counts
    pend = jnp.cumsum(padded)
    pstart = pend - padded
    dest = pstart[e_sorted] + (jnp.arange(A, dtype=jnp.int32) - start[e_sorted])
    P = A + N_EXPERTS * MOE_BLK
    nblk = P // MOE_BLK
    tok_buf = jnp.zeros((P,), jnp.int32).at[dest].set(tok_flat[order])
    w_buf = jnp.zeros((P,), jnp.float32).at[dest].set(w_flat[order])
    blk_e = jnp.minimum(jnp.searchsorted(pend, jnp.arange(nblk, dtype=jnp.int32) * MOE_BLK, side='right'),
                        N_EXPERTS - 1).astype(jnp.int32)

    def expert_block(args):
        tok, e = args
        xb = xt[tok]
        gu = xb @ w_gate_up[e] + b_gate_up[e]
        g, u = gu[:, :D_FF], gu[:, D_FF:]
        g = jnp.minimum(g, SWIGLU_LIMIT)
        u = jnp.clip(u, -SWIGLU_LIMIT, SWIGLU_LIMIT)
        hmid = (u + 1.0) * (g * jax.nn.sigmoid(SWIGLU_ALPHA * g))
        return hmid @ w_down[e] + b_down[e]

    out = lax.map(expert_block, (tok_buf.reshape(nblk, MOE_BLK), blk_e))
    y = jnp.zeros((T, D), jnp.float32).at[tok_buf].add(out.reshape(P, D).astype(jnp.float32) * w_buf[:, None])
    return y.astype(xn.dtype).reshape(B, S, D)

def setup_inputs(seed: int = 0) -> dict:
    key = jax.random.key(seed)
    ks = jax.random.split(key, 32)
    L, D = DEPTH, D_MODEL

    def nrm(k, shape, scale):
        return jax.random.normal(k, shape, jnp.float32) * scale

    def gain(k, shape):
        return 1.0 + 0.02 * jax.random.normal(k, shape, jnp.float32)

    positions = (jax.random.randint(ks[2], (BATCH, 1), 0, 4096, dtype=jnp.int32)
                 + jnp.arange(SEQ, dtype=jnp.int32)[None, :])
    return {
        'x': nrm(ks[0], (BATCH, SEQ, D), 1.0),
        'mem': nrm(ks[1], (BATCH, N_MEM, D), 1.0),
        'positions': positions,
        'g_mix_norm': gain(ks[3], (L, D)),
        'w_mix_in': nrm(ks[4], (L, D, IN_COLS), D ** -0.5),
        'cmp_pos_k': nrm(ks[5], (L, CMP_LEN, HEAD_DIM), 0.1),
        'cmp_pos_v': nrm(ks[6], (L, CMP_LEN, HEAD_DIM), 0.1),
        'cmp_w1_k': nrm(ks[7], (L, CMP_LEN * HEAD_DIM, CMP_HIDDEN), (CMP_LEN * HEAD_DIM) ** -0.5),
        'cmp_b1_k': nrm(ks[8], (L, CMP_HIDDEN), 0.01),
        'cmp_w2_k': nrm(ks[9], (L, CMP_HIDDEN, HEAD_DIM), CMP_HIDDEN ** -0.5),
        'cmp_w1_v': nrm(ks[10], (L, CMP_LEN * HEAD_DIM, CMP_HIDDEN), (CMP_LEN * HEAD_DIM) ** -0.5),
        'cmp_b1_v': nrm(ks[11], (L, CMP_HIDDEN), 0.01),
        'cmp_w2_v': nrm(ks[12], (L, CMP_HIDDEN, HEAD_DIM), CMP_HIDDEN ** -0.5),
        'conv_w': nrm(ks[13], (L, CONV_K, CONV_WIDTH), CONV_K ** -0.5),
        'g_nsa_out': gain(ks[14], (L, NSA_WIDTH)),
        'g_conv_out': gain(ks[15], (L, CONV_WIDTH)),
        'w_mix_out': nrm(ks[16], (L, D_MIX, D), D_MIX ** -0.5),
        'g_xattn_norm': gain(ks[17], (L, D)),
        'g_mem_norm': gain(ks[18], (L, D)),
        'w_xq': nrm(ks[19], (L, D, D), D ** -0.5),
        'w_xkv': nrm(ks[20], (L, D, 2 * D), D ** -0.5),
        'w_xo': nrm(ks[21], (L, D, D), D ** -0.5),
        'g_moe_norm': gain(ks[22], (L, D)),
        'w_router': nrm(ks[23], (L, D, N_EXPERTS), D ** -0.5),
        'b_router': nrm(ks[24], (L, N_EXPERTS), 0.01),
        'w_gate_up': nrm(ks[25], (L, N_EXPERTS, D, 2 * D_FF), D ** -0.5),
        'b_gate_up': nrm(ks[26], (L, N_EXPERTS, 2 * D_FF), 0.01),
        'w_down': nrm(ks[27], (L, N_EXPERTS, D_FF, D), D_FF ** -0.5),
        'b_down': nrm(ks[28], (L, N_EXPERTS, D), 0.01),
        'g_final': gain(ks[29], (D,)),
    }

def reference(x, mem, positions, g_mix_norm, w_mix_in, cmp_pos_k, cmp_pos_v, cmp_w1_k, cmp_b1_k, cmp_w2_k,
              cmp_w1_v, cmp_b1_v, cmp_w2_v, conv_w, g_nsa_out, g_conv_out, w_mix_out, g_xattn_norm,
              g_mem_norm, w_xq, w_xkv, w_xo, g_moe_norm, w_router, b_router, w_gate_up, b_gate_up,
              w_down, b_down, g_final):
    h = x
    for l in range(DEPTH):
        h = h + hybrid_mixer(rmsnorm(h, g_mix_norm[l]), positions, w_mix_in[l], cmp_pos_k[l], cmp_pos_v[l],
                             cmp_w1_k[l], cmp_b1_k[l], cmp_w2_k[l], cmp_w1_v[l], cmp_b1_v[l], cmp_w2_v[l],
                             conv_w[l], g_nsa_out[l], g_conv_out[l], w_mix_out[l])
        h = h + memory_cross_attention(rmsnorm(h, g_xattn_norm[l]), rmsnorm(mem, g_mem_norm[l]),
                                       w_xq[l], w_xkv[l], w_xo[l])
        h = h + moe_ffn(rmsnorm(h, g_moe_norm[l]), w_router[l], b_router[l], w_gate_up[l], b_gate_up[l],
                        w_down[l], b_down[l])
    return rmsnorm(h, g_final)


_drawn_inputs = setup_inputs


def setup_inputs(seed=0):
    import zlib

    import numpy as np

    out = dict(_drawn_inputs(seed))
    spreads = {}
    factors = {'cmp_pos_k': 2.892,
     'cmp_b1_k': 8.0,
     'cmp_b1_v': 8.0,
     'g_nsa_out': 2.99,
     'g_conv_out': 3.137,
     'g_xattn_norm': 8.0,
     'g_mem_norm': 6.708,
     'b_gate_up': 64.0,
     'b_down': 64.0,
     'g_final': 8.571,
     'g_moe_norm': 7.382,
     'b_router': 8.0}
    for name, (base, spread) in spreads.items():
        noise = np.random.default_rng([zlib.crc32(name.encode()), seed]).standard_normal(out[name].shape)
        drawn = base * np.exp(spread * noise) if base else spread * noise
        out[name] = jnp.asarray(drawn.astype(out[name].dtype))
    for name, factor in factors.items():
        out[name] = (out[name] * factor).astype(out[name].dtype)
    return out
```

```python
import numpy as np
import concourse.bass as bass
from concourse import mybir
from contextlib import ExitStack

F32 = mybir.dt.float32
BF16 = mybir.dt.bfloat16
I32 = mybir.dt.int32
ALU = mybir.AluOpType
ACT = mybir.ActivationFunctionType
AX = mybir.AxisListType.X

P = 128
BANK = 512
D = 1024
S = 256
T = S // P
KC = D // P
HD = 64
G, J = 2, 4
NSA = G * J * HD
ROWC = 1304
CONVW = 512
CC = CONVW // P
NCMP, CSTR, CLEN, CHID = 15, 16, 32, 256
MC = CLEN * HD // P
XH, XD = 4, 256
E = 32
FF = 1024
LIM, ALPHA = 7.0, 1.702
SLOTS = 64
PAIRS = E // 2
ROUNDS = S // SLOTS
FILLS = 12
RING = 6
EPS = 1e-5
NEG = -1e30
R_MIX, R_XA, R_MEM, R_MOE, R_NSA, R_CNV, R_B1, R_CW, R_POS, R_END = 0, 8, 16, 24, 32, 36, 40, 44, 56, 88


def links(eng, default):
    count = {}

    def link(ins, sem=None):
        sem = default if sem is None else sem
        key = id(sem)
        count[key] = count.get(key, 0) + 1
        ins.then_inc(sem, 1)
        eng.wait_ge(sem, count[key])

    return link


def trunk(nc, x, mem, positions, g_mix_norm, w_mix_in, cmp_pos_k, cmp_pos_v, cmp_w1_k, cmp_b1_k,
          cmp_w2_k, cmp_w1_v, cmp_b1_v, cmp_w2_v, conv_w, g_nsa_out, g_conv_out, w_mix_out,
          g_xattn_norm, g_mem_norm, w_xq, w_xkv, w_xo, g_moe_norm, w_router, b_router, w_gate_up,
          b_gate_up, w_down, b_down, g_final, inv_freq, out):
    ctx = ExitStack()
    with ctx:
        def sb(name, shape, dt=F32):
            return ctx.enter_context(nc.sbuf_tensor(name, shape, dt))

        def sem(name):
            return ctx.enter_context(nc.semaphore(name))

        R = sb("R", [P, RING * 4096])
        A = sb("A", [P, 8192])
        H = sb("H", [P, T, D])
        XS = sb("XS", [P, T, D])
        XT = sb("XT", [P, KC, S])
        MT = sb("MT", [P, KC, S])
        MK = sb("MK", [P, KC, S])
        MV = sb("MV", [P, T, D])
        w_row = R[:, 0:KC * ROWC].rearrange("p (k n) -> p k n", k=KC)
        w_cnv = R[:, KC * ROWC:KC * (ROWC + 3 * CONVW)].rearrange("p (k n) -> p k n", k=KC)
        w_out = R[:, 0:8192].rearrange("p (k n) -> p k n", k=KC)
        w_q2 = R[:, 8192:16384].rearrange("p (k n) -> p k n", k=KC)
        w_o2 = R[:, 16384:24576].rearrange("p (k n) -> p k n", k=KC)
        ring = R[:, :].rearrange("p (f s n) -> p f s n", f=RING, s=2)
        tail = R[:, 16384:24576]
        w_a = A[:, :].rearrange("p (k n) -> p k n", k=KC)
        w_c1 = A[:, :].rearrange("p (v m n) -> p v m n", v=2, m=MC)

        ident = sb("ident", [P, P])
        prm_rows = sb("prm_rows", [R_END, P])
        prm = sb("prm", [P, R_END])
        ones = sb("ones", [P, 1])
        eps = sb("eps", [P, 1])
        zero1 = sb("zero1", [P, 1])
        ss = sb("ss", [P, 4])
        rst = sb("rst", [P, 4])
        pos_i = sb("pos_i", [P, T], I32)
        pos_f = sb("pos_f", [P, T])
        invf = sb("invf", [P, 32])
        ang = sb("ang", [P, T, 32])
        turn = sb("turn", [P, T, 32])
        rem = sb("rem", [P, 2, T, 32])
        trig = sb("trig", [P, 2, T, 32])
        qrot = sb("qrot", [P, T, NSA])
        krot = sb("krot", [P, T, 3, G * HD])
        vrow = sb("vrow", [P, T, 3, G * HD])
        gates = sb("gates", [P, T, 24])
        ra = sb("ra", [P, 256])
        rb = sb("rb", [P, 256])
        qT = sb("qT", [P, J, S])
        kT = sb("kT", [P, 2, S])
        convT = sb("convT", [P, CC, S])
        mask = sb("mask", [P, S])
        cmask = sb("cmask", [P, T, NCMP])
        valid = sb("valid", [P, T])
        w_c2 = sb("w_c2", [P, 2, 2, HD])
        kcT = sb("kcT", [P, NCMP])
        vc = sb("vc", [NCMP, G, HD])
        nmx = sb("nmx", [P, 2, 4])
        smx = sb("smx", [P, 2, 4])
        cof = sb("cof", [P, 2, 4])
        cnm = sb("cnm", [P, 16])
        csm = sb("csm", [P, 16])
        w_rt = sb("w_rt", [P, KC, E])
        b_rt = sb("b_rt", [P, E])

        xsf = XS[:, :, :].rearrange("p t n -> p (t n)")
        ch_sb = xsf[:, 0:512].rearrange("p (b n) -> p b n", b=2)
        u_pad = xsf[:, 512:512 + S + 2]
        cy = xsf[:, 800:800 + S]
        cy2 = xsf[:, 1056:1056 + S]
        Pb = tail[:, 0:2048].rearrange("p (b g k n) -> p b g k n", b=2, g=2, k=2)
        oT = tail[:, 2048:3072].rearrange("p (j n) -> p j n", j=J)
        sq = tail[:, 3072:5120].rearrange("p (c n) -> p c n", c=8)
        blk = tail[:, 5120:6080].rearrange("p (v m g c) -> p v m g c", v=2, m=MC, g=G)
        hid = tail[0:2 * NCMP, 6080:6592]
        hx = tail[:, 6592:6712]
        hy = tail[:, 6712:6832]
        hT = tail[:, 6832:6952].rearrange("p (v c n) -> p v c n", v=2, c=2)
        Pc = tail[:, 6952:7192].rearrange("p (g t j c) -> p g t j c", g=G, t=T, j=J)
        PTc = tail[0:NCMP, 3072:5120].rearrange("p (g t n) -> p g t n", g=G, t=T)
        PT = [MT[:, :, :].rearrange("p a b -> p (a b)").rearrange("p (b j n) -> p b j n", b=4, j=J),
              XT[:, :, :].rearrange("p a b -> p (a b)").rearrange("p (b j n) -> p b j n", b=4, j=J)]
        q2T = MT
        P2 = xsf.rearrange("p (h t n) -> p h t n", h=XH, t=T)
        P2T = XT[:, :, :].rearrange("p a b -> p (a b)").rearrange("p (h m n) -> p h m n", h=XH, m=2)
        o2T = MT
        xgT = A[:, 0:1024].rearrange("p (k n) -> p k n", k=KC)
        gcl = A[:, 1024:2048]
        ucl = A[:, 2048:3072]
        sgm = A[:, 3072:4096]
        hTm = A[:, 4096:5120].rearrange("p (k n) -> p k n", k=KC)
        orow = A[:, 5120:6144]
        b_raw = A[0:96, 0:2 * FF]
        b_res = A[0:96, 2 * FF:4 * FF]
        b_prt = A[0:96, 6144:7168].bitcast(BF16)
        mkf = MK[:, :, :].rearrange("p a b -> p (a b)")
        ROW = ROUNDS * E
        keys = mkf[:, 0:T * (ROW + 2)].rearrange("p (t c) -> p t c", t=T)
        gtab = mkf[:, 260:260 + T * (ROW + 2)].rearrange("p (t c) -> p t c", t=T)
        sel1 = mkf[:, 520:776].rearrange("p (t n) -> p t n", t=T)
        selg = mkf[:, 776:1032].rearrange("p (t n) -> p t n", t=T)
        selgT = mkf[:, 1032:1288].rearrange("p (t n) -> p t n", t=T)
        iot = mkf[:, 1288:1288 + SLOTS]
        bdiff = mkf[0:96, 1352:1352 + P]
        bsel = mkf[0:96, 1480:1480 + P // 2].bitcast(BF16)
        lg = mkf[:, 1552:1616].rearrange("p (t e) -> p t e", t=T)
        top = mkf[:, 1616:1632].rearrange("p (t e) -> p t e", t=T)
        gt = mkf[:, 1632:1696].rearrange("p (t e) -> p t e", t=T)
        eq = mkf[:, 1696:1760].rearrange("p (t e) -> p t e", t=T)
        cum = mkf[:, 1760:1824].rearrange("p (t e) -> p t e", t=T)
        need = mkf[:, 1824:1826]
        gex = mkf[:, 1826:1890].rearrange("p (t e) -> p t e", t=T)
        gsum = mkf[:, 1890:1892]
        gneg = mkf[:, 1892:1894]
        zer = mkf[:, 1894:1926]
        first = mkf[0:96, 1959:1959 + ROUNDS * PAIRS + 1]
        cmx = mkf[0:1, 1958:1959]
        flg = sb("flg", [1, ROUNDS], I32)
        tri = sb("tri", [P, P])
        mvf = MV[:, :, :].rearrange("p t n -> p (t n)")
        gfin = mvf[:, 0:D]
        bdn = mvf[0:E, D:2 * D]
        gTe = XT[0:E, 1, :]

        ps = ctx.enter_context(nc.psum_tensor("ps", [P, 8 * BANK], F32))

        def bank(i, n=1):
            return ps[:, i * BANK:(i + n) * BANK]

        ld_x, ld_mem, ld_prm, ld_misc, ld_pos = sem("ld_x"), sem("ld_mem"), sem("ld_prm"), sem("ld_misc"), sem("ld_pos")
        ld_a = [sem(f"ld_a{i}") for i in range(KC)]
        ld_row = [sem(f"ld_row{i}") for i in range(KC)]
        ld_cnv, ld_c1, ld_out, ld_q2, ld_o2 = sem("ld_cnv"), sem("ld_c1"), sem("ld_out"), sem("ld_q2"), sem("ld_o2")
        ld_bias, ld_end = sem("ld_bias"), sem("ld_end")
        a_used = sem("a_used")
        pool_seq, pool_id, pool_cst, pool_moe = sem("pool_seq"), sem("pool_id"), sem("pool_cst"), sem("pool_moe")
        dve_seq, act_seq = sem("dve_seq"), sem("act_seq")
        act_ssq, act_sqrt, dve_rstd = sem("act_ssq"), sem("act_sqrt"), sem("dve_rstd")
        dve_norm = sem("dve_norm")
        pe_prm, dve_prm = sem("pe_prm"), sem("dve_prm")
        pe_tr, dve_tr = sem("pe_tr"), sem("dve_tr")
        act_k, act_v = sem("act_k"), sem("act_v")
        pe_row, dve_rope, act_rows = sem("pe_row"), sem("dve_rope"), sem("act_rows")
        dve_rem, act_trig = sem("dve_rem"), sem("act_trig")
        pe_cnv, act_ch, dve_cnv = sem("pe_cnv"), sem("act_ch"), sem("dve_cnv")
        pe_qkT, act_qkT = sem("pe_qkT"), sem("act_qkT")
        pe_cT, dve_blk = sem("pe_cT"), sem("dve_blk")
        pe_hid, act_hid, pe_hidT, dve_hx, act_hs, dve_hT = (sem("pe_hid"), sem("act_hid"), sem("pe_hidT"),
                                                           sem("dve_hx"), sem("act_hs"), sem("dve_hT"))
        pe_ckv, dve_ckv = sem("pe_ckv"), sem("dve_ckv")
        pe_cs, dve_cx, act_ce, dve_cp, pe_cpt, act_cpt = (sem("pe_cs"), sem("dve_cx"), sem("act_ce"),
                                                         sem("dve_cp"), sem("pe_cpt"), sem("act_cpt"))
        pe_sc, dve_sx, act_e, dve_p, pe_pt, act_pt = (sem("pe_sc"), sem("dve_sx"), sem("act_e"), sem("dve_p"),
                                                     sem("pe_pt"), sem("act_pt"))
        pe_pv, dve_sq, pe_ss, act_sst, dve_o = sem("pe_pv"), sem("dve_sq"), sem("pe_ss"), sem("act_sst"), sem("dve_o")
        pe_mo, dve_h1 = sem("pe_mo"), sem("dve_h1")
        pe_q2, act_q2 = sem("pe_q2"), sem("act_q2")
        pe_s2, dve_m2, act_e2, dve_p2, pe_p2t, act_p2t = (sem("pe_s2"), sem("dve_m2"), sem("act_e2"),
                                                         sem("dve_p2"), sem("pe_p2t"), sem("act_p2t"))
        pe_o2, act_o2, pe_xo, dve_h2 = sem("pe_o2"), sem("act_o2"), sem("pe_xo"), sem("dve_h2")
        pe_lg, dve_ng, act_gx, dve_g, pe_cnt, dve_flg = (sem("pe_lg"), sem("dve_ng"), sem("act_gx"), sem("dve_g"),
                                                        sem("pe_cnt"), sem("dve_flg"))
        dve_one, pe_gT, dve_gT, pe_bd, dve_bd, dve_bp = (sem("dve_one"), sem("pe_gT"), sem("dve_gT"), sem("pe_bd"),
                                                        sem("dve_bd"), sem("dve_bp"))
        arrived = [sem(f"arrived{i}") for i in range(RING)]
        freed = sem("freed")
        m_seq = sem("m_seq")
        m_sel, m_selg, m_gath, m_xg = sem("m_sel"), sem("m_selg"), sem("m_gath"), sem("m_xg")
        m_bsel, m_bias = sem("m_bsel"), sem("m_bias")
        m_gcl, m_sg, m_h = sem("m_gcl"), sem("m_sg"), sem("m_h")
        m_tr, m_trD, m_trA, m_sgT, m_sgTc = sem("m_tr"), sem("m_trD"), sem("m_trA"), sem("m_sgT"), sem("m_sgTc")
        m_oA, m_oD, m_y, m_add = sem("m_oA"), sem("m_oD"), sem("m_y"), sem("m_add")
        f_ss, f_sq, f_out, st_out = sem("f_ss"), sem("f_sq"), sem("f_out"), sem("st_out")

        x_v = x.rearrange("o (t p) n -> p (o t) n", p=P)
        mem_v = mem.rearrange("o (t p) n -> p (o t) n", p=P)
        out_v = out.rearrange("o (t p) n -> p (o t) n", p=P)

        def chunked(w):
            return w.rearrange("(k p) n -> p k n", p=P)

        with nc.Block() as block:

            @block.sync
            def _(sp):
                for t in range(T):
                    sp.dma_start(MV[:, t, :], mem_v[:, t, :]).then_inc(ld_mem, 16)
                for kc in range(KC):
                    sp.dma_start(w_a[:, kc, :], w_xkv[0, kc * P:(kc + 1) * P, 0:D]).then_inc(ld_a[kc], 16)
                for kc in range(KC):
                    sp.dma_start(w_row[:, kc, :], w_mix_in[0, kc * P:(kc + 1) * P, 0:ROWC]).then_inc(ld_row[kc], 16)
                for kc in range(KC):
                    sp.wait_ge(a_used, kc + 1)
                    sp.dma_start(w_a[:, kc, :], w_xkv[0, kc * P:(kc + 1) * P, D:2 * D]).then_inc(ld_a[kc], 16)
                for kc in range(KC):
                    sp.dma_start(w_cnv[:, kc, :], w_mix_in[0, kc * P:(kc + 1) * P, ROWC:ROWC + 3 * CONVW]
                                 ).then_inc(ld_cnv, 16)
                sp.wait_ge(a_used, 2 * KC)
                for v, w in enumerate((cmp_w1_k, cmp_w1_v)):
                    sp.dma_start(w_c1[:, v, :, :], w[0].rearrange("(m p) n -> p m n", p=P)).then_inc(ld_c1, 16)
                sp.wait_ge(pe_cnv, CC)
                nsa = w_mix_out[0, 0:NSA, :].rearrange("(g j d) n -> g j d n", g=G, j=J)
                for g in range(G):
                    for j in range(J):
                        sp.dma_start(w_out[g * HD:(g + 1) * HD, j, :], nsa[g, j]).then_inc(ld_out, 16)
                sp.dma_start(w_out[:, J:J + CC, :], chunked(w_mix_out[0, NSA:D, :])).then_inc(ld_out, 16)
                sp.dma_start(w_q2, chunked(w_xq[0])).then_inc(ld_q2, 16)
                sp.wait_ge(pe_hid, 2)
                for part in range(3):
                    sp.dma_start(A[part * E:(part + 1) * E, 0:2 * FF], b_gate_up[0]).then_inc(ld_bias, 16)
                sp.wait_ge(pe_mo, T)
                sp.wait_ge(dve_h1, 1)
                sp.dma_start(w_o2, chunked(w_xo[0])).then_inc(ld_o2, 16)

                def fill(p, j):
                    for s in range(2):
                        e = p * 2 + s
                        if j < KC:
                            src = w_gate_up[0, bass.ds(e, 1), j * P:(j + 1) * P, :].rearrange("o p n -> p (o n)")
                            dst = ring[:, j % RING, s, :]
                        else:
                            f = (j - KC) * 2 * P
                            src = w_down[0, bass.ds(e, 1), f:f + 2 * P, :].rearrange("o (c p) n -> p (o c) n", p=P)
                            dst = ring[:, j % RING, s, :].rearrange("p (c n) -> p c n", c=2)
                        sp.dma_start(dst, src).then_inc(arrived[j % RING], 16)

                for j in range(FILLS):
                    if j == 2:
                        sp.wait_ge(pe_q2, XH)
                    if j == 4:
                        sp.wait_ge(pe_xo, T)
                    if j >= RING:
                        sp.wait_ge(freed, j - RING + 1)
                    fill(0, j)
                with sp.Fori(1, PAIRS) as p:
                    for j in range(FILLS):
                        sp.wait_ge(freed, p * FILLS + (j - RING + 1))
                        fill(p, j)
                sp.wait_ge(dve_flg, 1)
                with sp.Fori(1, ROUNDS) as r:
                    on = sp.value_load(flg[0:1, bass.ds(r, 1)], min_val=0, max_val=1)
                    with sp.If(on > 0):
                        with sp.Fori(0, PAIRS) as p:
                            for j in range(FILLS):
                                sp.wait_ge(freed, r * (PAIRS * FILLS) + p * FILLS + (j - RING + 1))
                                fill(p, j)

            @block.gpsimd
            def _(pool):
                link = links(pool, pool_seq)
                link(nc.gpsimd.memset(ident[:], 0.0))
                nc.gpsimd.affine_select(out=ident[:], in_=ident[:], compare_op=ALU.not_equal, fill=1.0, base=0,
                                        pattern=[[-1, P]], channel_multiplier=1).then_inc(pool_id, 1)
                nc.gpsimd.memset(ones[:], 1.0).then_inc(pool_cst, 1)
                nc.gpsimd.memset(zero1[:], 0.0).then_inc(pool_cst, 1)
                link(nc.gpsimd.memset(mask[:], 0.0))
                nc.gpsimd.affine_select(out=mask[:], in_=mask[:], compare_op=ALU.is_ge, fill=NEG, base=P,
                                        pattern=[[-1, S]], channel_multiplier=1).then_inc(pool_cst, 1)
                link(nc.gpsimd.memset(cmask[:], 0.0))
                nc.gpsimd.affine_select(out=cmask[:], in_=cmask[:], compare_op=ALU.is_ge, fill=NEG,
                                        base=-(CLEN - 1), pattern=[[P, T], [-CSTR, NCMP]],
                                        channel_multiplier=1).then_inc(pool_cst, 1)
                link(nc.gpsimd.memset(valid[:], 1.0))
                nc.gpsimd.affine_select(out=valid[:], in_=valid[:], compare_op=ALU.is_ge, fill=0.0,
                                        base=-(CLEN - 1), pattern=[[P, T]], channel_multiplier=1).then_inc(pool_cst, 1)
                link(nc.gpsimd.memset(tri[:], 0.0))
                nc.gpsimd.affine_select(out=tri[:], in_=tri[:], compare_op=ALU.is_ge, fill=1.0, base=0,
                                        pattern=[[-1, P]], channel_multiplier=1).then_inc(pool_cst, 1)
                pool.wait_ge(pe_s2, XH)
                link(nc.gpsimd.iota(iot, pattern=[[1, SLOTS]], base=0, channel_multiplier=0,
                               allow_small_or_imprecise_dtypes=True), pool_moe)
                for part in range(3):
                    link(nc.gpsimd.iota(mkf[part * E:(part + 1) * E, 1352:1352 + P].rearrange("p (s n) -> p s n", s=2),
                                   pattern=[[-1, 2], [0, SLOTS]], base=0, channel_multiplier=1,
                                   allow_small_or_imprecise_dtypes=True), pool_moe)
                link(nc.gpsimd.iota(first[:, 0:ROUNDS * PAIRS], pattern=[[0, ROUNDS], [2, PAIRS]], base=0, channel_multiplier=0,
                               allow_small_or_imprecise_dtypes=True), pool_moe)
                link(nc.gpsimd.memset(first[:, ROUNDS * PAIRS:ROUNDS * PAIRS + 1], 0.0), pool_moe)
                link(nc.gpsimd.memset(zer, 0.0), pool_moe)
                link(nc.gpsimd.memset(mkf[:, 0:520], -1.0), pool_moe)

            @block.scalar
            def _(act):
                link = links(act, act_seq)
                for t in range(T):
                    act.dma_start(H[:, t, :], x_v[:, t, :]).then_inc(ld_x, 16)
                rows = [(R_MIX, g_mix_norm[0]), (R_XA, g_xattn_norm[0]), (R_MEM, g_mem_norm[0]),
                        (R_MOE, g_moe_norm[0]), (R_CNV, g_conv_out[0]), (R_B1, cmp_b1_k[0]), (R_B1 + 2, cmp_b1_v[0])]
                for r, v in rows:
                    n = v.shape[0] // P
                    act.dma_start(prm_rows[r:r + n, :], v.rearrange("(r n) -> r n", n=P)).then_inc(ld_prm, 16)
                for g in range(G):
                    act.dma_start(prm_rows[R_NSA:R_NSA + J, g * HD:(g + 1) * HD],
                                  g_nsa_out[0, g * J * HD:(g + 1) * J * HD].rearrange("(j d) -> j d", j=J)
                                  ).then_inc(ld_prm, 16)
                act.dma_start(prm_rows[R_CW:R_CW + 12, :], conv_w[0].rearrange("k (c n) -> (k c) n", n=P)
                              ).then_inc(ld_prm, 16)
                for v, w in enumerate((cmp_pos_k, cmp_pos_v)):
                    act.dma_start(prm_rows[R_POS + 16 * v:R_POS + 16 * (v + 1), :],
                                  w[0].rearrange("(m i) d -> m (i d)", i=2)).then_inc(ld_prm, 16)
                act.dma_start(pos_i[:], positions.rearrange("o (t p) -> p (o t)", p=P), allow_slow_non_contiguous=True).then_inc(ld_pos, 16)
                act.dma_start(invf[:], inv_freq.to_broadcast([P, 32])).then_inc(ld_pos, 16)
                act.dma_start(b_rt[:], b_router.to_broadcast([P, E])).then_inc(ld_misc, 16)
                act.dma_start(w_rt[:], chunked(w_router[0])).then_inc(ld_misc, 16)
                for v, w in enumerate((cmp_w2_k, cmp_w2_v)):
                    act.dma_start(w_c2[:, v, :, :], w[0].rearrange("(c p) n -> p c n", p=P)).then_inc(ld_misc, 16)

                def rms(src, junk):
                    for t in range(T):
                        last = nc.scalar.activation(junk[:, t, :], src[:, t, :], ACT.Square, accum_out=ss[:, t:t + 1])
                        link(last)
                    nc.scalar.activation(rst[:, 0:T], ss[:, 0:T], ACT.Sqrt, bias=eps[:], scale=1.0 / D
                                         ).then_inc(act_sqrt, 1)

                act.wait_ge(ld_mem, 32)
                act.wait_ge(dve_one, 1)
                rms(MV, XS)
                act.wait_ge(dve_rstd, 1)
                act.wait_ge(ld_x, 32)
                act.wait_ge(dve_norm, 2)
                rms(H, MK[:, :, :].rearrange("p a b -> p (a b)").rearrange("p (t n) -> p t n", t=T))
                act.wait_ge(dve_rem, 1)
                nc.scalar.activation(trig[:].rearrange("p a t n -> p (a t n)"), rem[:].rearrange("p a t n -> p (a t n)"),
                                     ACT.Sin).then_inc(act_trig, 1)
                act.wait_ge(a_used, KC)
                for b in range(4):
                    nc.scalar.copy(MK[:, 2 * b:2 * b + 2, :].rearrange("p a n -> p (a n)"), bank(b)).then_inc(act_k, 1)
                for t in range(T):
                    if t == 1:
                        act.wait_ge(a_used, 2 * KC)
                        for b in range(4):
                            nc.scalar.copy(MV[:, b // 2, (b % 2) * BANK:(b % 2 + 1) * BANK], bank(b)).then_inc(act_v, 1)
                    act.wait_ge(pe_row, t + 1)
                    pr = bank(4, 3)
                    nc.scalar.copy(vrow[:, t, :, :],
                                   pr[:, 640:1408].rearrange("p (k n) -> p k n", k=3)[:, :, 0:P]).then_inc(act_rows, 1)
                    nc.scalar.activation(gates[:, t, :], pr[:, 1280:ROWC], ACT.Sigmoid).then_inc(act_rows, 1)
                for i in range(CC):
                    act.wait_ge(pe_cnv, i + 1)
                    if i >= 2:
                        act.wait_ge(dve_cnv, i - 1)
                    nc.scalar.copy(ch_sb[:, i % 2, :], bank(2 * (i % 2))[:, 0:S]).then_inc(act_ch, 1)
                act.wait_ge(pe_qkT, 1)
                nc.scalar.copy(qT[:, 0:2, :].rearrange("p a n -> p (a n)"), bank(4)).then_inc(act_qkT, 1)
                nc.scalar.copy(qT[:, 2:4, :].rearrange("p a n -> p (a n)"), bank(5)).then_inc(act_qkT, 1)
                nc.scalar.copy(kT[:].rearrange("p a n -> p (a n)"), bank(6)).then_inc(act_qkT, 1)
                for v in range(2):
                    act.wait_ge(pe_hid, v + 1)
                    nc.scalar.copy(hid[:, v * CHID:(v + 1) * CHID], bank(1 + v)[0:2 * NCMP, 0:CHID]).then_inc(act_hid, 1)
                act.wait_ge(dve_hx, 1)
                nc.scalar.activation(hy, hy, ACT.Sigmoid, scale=2.0 * 0.7978845608028654).then_inc(act_hs, 1)
                act.wait_ge(dve_cx, 1)
                pcf = tail[:, 6952:7192]
                nc.scalar.activation(pcf, pcf, ACT.Exp).then_inc(act_ce, 1)
                for i in range(4):
                    act.wait_ge(pe_cpt, 1)
                    nc.scalar.copy(PTc[:, i % 2, i // 2, :], bank(4 + i)[0:NCMP, :]).then_inc(act_cpt, 1)

                def exps(n):
                    t = n // J
                    nk = P * (t + 1)
                    act.wait_ge(dve_sx, n + 1)
                    for g in range(G):
                        for k in range(2):
                            nc.scalar.activation(Pb[:, n % 2, g, k, 0:nk], Pb[:, n % 2, g, k, 0:nk], ACT.Exp,
                                                 bias=nmx[:, n % 2, 2 * g + k:2 * g + k + 1],
                                                 accum_out=smx[:, n % 2, 2 * g + k:2 * g + k + 1]).then_inc(act_e, 1)

                def pt_out(n):
                    t, j = n // J, n % J
                    act.wait_ge(pe_pt, n + 1)
                    if t == 1:
                        act.wait_ge(pe_pv, 1)
                    for g in range(G):
                        nb = 2 * (t + 1)
                        nc.scalar.copy(PT[g][:, 0:nb, j, :], bank(4 + g)[:, 0:nb * P].rearrange("p (b n) -> p b n", b=nb)
                                       ).then_inc(act_pt, 1)

                for n in range(T * J):
                    exps(n)
                    if n >= 1:
                        pt_out(n - 1)
                pt_out(T * J - 1)
                act.wait_ge(pe_ss, 1)
                act.wait_ge(dve_norm, 4)
                nc.scalar.activation(rst[:, 0:4], bank(4)[:, 0:4], ACT.Sqrt, bias=eps[:], scale=1.0 / NSA
                                     ).then_inc(act_sst, 1)
                act.wait_ge(dve_h1, 1)
                rms(H, XS)
                for c in range(4):
                    act.wait_ge(pe_q2, c + 1)
                    nc.scalar.copy(q2T[:, 2 * c:2 * c + 2, :].rearrange("p a n -> p (a n)"), bank(4 + c)
                                   ).then_inc(act_q2, 1)
                for h in range(XH):
                    act.wait_ge(dve_m2, h + 1)
                    for t in range(T):
                        nc.scalar.activation(P2[:, h, t, :], bank(h)[:, t * S:(t + 1) * S], ACT.Exp,
                                             bias=cnm[:, 2 * h + t:2 * h + t + 1], scale=XD ** -0.5,
                                             accum_out=csm[:, 2 * h + t:2 * h + t + 1]).then_inc(act_e2, 1)
                for h in range(XH):
                    act.wait_ge(pe_p2t, h + 1)
                    nc.scalar.copy(P2T[:, h, :, :].rearrange("p m n -> p (m n)"), bank(4 + h)).then_inc(act_p2t, 1)
                for h in range(XH):
                    act.wait_ge(pe_o2, h + 1)
                    nc.scalar.copy(o2T[:, 2 * h:2 * h + 2, :].rearrange("p a n -> p (a n)"), bank(h)).then_inc(act_o2, 1)
                act.dma_start(bdn, b_down[0]).then_inc(ld_end, 16)
                act.dma_start(gfin, g_final.rearrange("(a n) -> a n", a=1).to_broadcast([P, D])).then_inc(ld_end, 16)
                act.wait_ge(dve_h2, 1)
                rms(H, XS)
                act.wait_ge(dve_ng, 1)
                for t in range(T):
                    nc.scalar.activation(gex[:, t, :], lg[:, t, :], ACT.Exp, bias=gneg[:, t:t + 1]).then_inc(act_gx, 1)

                act.wait_ge(dve_flg, 1)
                with act.Fori(0, ROUNDS) as r:
                    on = act.value_load(flg[0:1, bass.ds(r, 1)], min_val=0, max_val=1)
                    with act.If(on > 0):
                        with act.Fori(0, PAIRS) as p:
                            k = r * PAIRS + p
                            act.wait_ge(m_gcl, k + 1)
                            nc.scalar.activation(sgm, gcl, ACT.Sigmoid, scale=ALPHA).then_inc(m_sg, 1)
                            act.wait_ge(m_tr, k + 1)
                            nc.scalar.copy(hTm[:, 4:8, :].rearrange("p k n -> p (k n)"), bank(5)).then_inc(m_trA, 1)
                            act.wait_ge(freed, k * FILLS + FILLS)
                            nc.scalar.copy(orow[:, BANK:D], bank(5)).then_inc(m_oA, 1)

            @block.vector
            def _(dve):
                V = nc.vector
                link = links(dve, dve_seq)
                V.memset(eps[:], EPS).then_inc(dve_one, 1)

                def norm(src, dst, i):
                    dve.wait_ge(act_sqrt, i + 1)
                    link(V.reciprocal(rst[:, 0:T], rst[:, 0:T]), dve_rstd)
                    for t in range(T):
                        link(V.tensor_scalar(dst[:, t, :], src[:, t, :], rst[:, t:t + 1], None, ALU.mult), dve_norm)

                def tr_out(i, dst, b0, row):
                    for b in range(4):
                        dve.wait_ge(pe_tr, 4 * i + b + 1)
                        V.tensor_tensor(dst[:, 2 * b:2 * b + 2, :], bank(b0 + b).rearrange("p (a n) -> p a n", a=2),
                                        prm[:, row + 2 * b:row + 2 * b + 2].unsqueeze(2).to_broadcast([P, 2, S]),
                                        ALU.mult).then_inc(dve_tr, 1)

                norm(MV, XS, 0)
                dve.wait_ge(pe_prm, 1)
                link(V.tensor_copy(prm[:], bank(7)[:, 0:R_END]), dve_prm)
                tr_out(0, MT, 0, R_MEM)
                dve.wait_ge(pe_tr, 4)
                norm(H, XS, 1)
                tr_out(1, XT, 4, R_MIX)

                dve.wait_ge(ld_pos, 32)
                link(V.tensor_copy(pos_f[:], pos_i[:]))
                for t in range(T):
                    link(V.tensor_scalar(ang[:, t, :], invf[:], pos_f[:, t:t + 1], None, ALU.mult))
                big = 12582912.0
                link(V.tensor_scalar(turn[:], ang[:], 0.15915494309189535, None, ALU.mult))
                link(V.tensor_scalar(turn[:], turn[:], big, None, ALU.add))
                link(V.tensor_scalar(turn[:], turn[:], big, None, ALU.subtract))
                c1, c2 = 6.28125, 0.0019350051879882812
                c3 = 2.0 * np.pi - c1 - c2
                for c in (c1, c2, c3):
                    link(V.scalar_tensor_tensor(ang[:].rearrange("p t n -> p (t n)"), turn[:].rearrange("p t n -> p (t n)"),
                                                -float(c), ang[:].rearrange("p t n -> p (t n)"), ALU.mult, ALU.add))
                pi = 3.1415925
                link(V.tensor_scalar(rem[:, 0], ang[:], pi, -pi, ALU.min, ALU.max))
                link(V.tensor_scalar(ang[:], ang[:], float(np.pi / 2), None, ALU.add))
                link(V.tensor_scalar(turn[:], ang[:], pi, 2.0 * float(np.pi), ALU.is_gt, ALU.mult))
                link(V.tensor_tensor(ang[:], ang[:], turn[:], ALU.subtract))
                link(V.tensor_scalar(rem[:, 1], ang[:], pi, -pi, ALU.min, ALU.max), dve_rem)
                dve.wait_ge(act_trig, 1)

                def rope(a1, a2, o1, o2, t, n, shape, sem_last):
                    sin, cos = trig[:, 0, t, :], trig[:, 1, t, :]
                    def bc(w):
                        return w.unsqueeze(1).unsqueeze(1).to_broadcast([P] + shape + [32])
                    def tmp(b):
                        return b[:, 0:n].rearrange("p (a b d) -> p a b d", a=shape[0], b=shape[1])
                    V.tensor_tensor(tmp(ra), a1, bc(cos), ALU.mult)
                    link(V.tensor_tensor(tmp(rb), a2, bc(sin), ALU.mult))
                    link(V.tensor_tensor(o1, tmp(ra), tmp(rb), ALU.subtract))
                    V.tensor_tensor(tmp(ra), a2, bc(cos), ALU.mult)
                    link(V.tensor_tensor(tmp(rb), a1, bc(sin), ALU.mult))
                    link(V.tensor_tensor(o2, tmp(ra), tmp(rb), ALU.add), sem_last)

                for t in range(T):
                    dve.wait_ge(pe_row, t + 1)
                    pr = bank(4, 3)
                    q4 = pr[:, 0:NSA].rearrange("p (g j d) -> p g j d", g=G, j=J)
                    o4 = qrot[:, t, :].rearrange("p (j g d) -> p g j d", g=G, j=J)
                    rope(q4[:, :, :, 0:32], q4[:, :, :, 32:64], o4[:, :, :, 0:32], o4[:, :, :, 32:64], t, 256, [G, J], None)
                    dve.wait_ge(act_rows, 2 * (t + 1))
                    k4 = pr[:, NSA:NSA + 768].rearrange("p (k w g d) -> p k w g d", k=3, w=2, g=G)[:, :, 0]
                    r4 = krot[:, t, :, :].rearrange("p k (g d) -> p k g d", g=G)
                    rope(k4[:, :, :, 0:32], k4[:, :, :, 32:64], r4[:, :, :, 0:32], r4[:, :, :, 32:64], t, 192, [3, G], dve_rope)

                link(V.memset(u_pad[:, 0:2], 0.0))
                for i in range(CC):
                    dve.wait_ge(act_ch, i + 1)
                    b0 = 2 * (i % 2)
                    link(V.tensor_tensor(u_pad[:, 2:S + 2], bank(b0)[:, S:2 * S], ch_sb[:, i % 2, :], ALU.mult))
                    tap = [prm[:, R_CW + 4 * w + i:R_CW + 4 * w + i + 1] for w in range(3)]
                    link(V.tensor_scalar(cy, u_pad[:, 0:S], tap[0], None, ALU.mult))
                    link(V.scalar_tensor_tensor(cy2, u_pad[:, 1:S + 1], tap[1], cy, ALU.mult, ALU.add))
                    link(V.scalar_tensor_tensor(cy, u_pad[:, 2:S + 2], tap[2], cy2, ALU.mult, ALU.add))
                    link(V.tensor_tensor(convT[:, i, :], bank(b0 + 1)[:, 0:S], cy, ALU.mult), dve_cnv)

                for v in range(2):
                    dve.wait_ge(pe_cT, v + 1)
                    for i in range(2):
                        src = (bank(7) if v == 0 else bank(0))[i * HD:(i + 1) * HD, :].rearrange(
                            "p (g c m i) -> p g c m i", g=G, m=8, i=2)
                        for mh in range(2):
                            for g in range(G):
                                link(V.tensor_tensor(
                                    blk[i * HD:(i + 1) * HD, v, 8 * mh:8 * mh + 8, g, :].rearrange("p m c -> p c m"),
                                    src[:, g, mh:mh + NCMP, :, i],
                                    prm[i * HD:(i + 1) * HD, R_POS + 16 * v + 8 * mh:R_POS + 16 * v + 8 * mh + 8
                                        ].unsqueeze(1).to_broadcast([HD, NCMP, 8]), ALU.add), dve_blk)

                dve.wait_ge(pe_hidT, 1)
                link(V.tensor_tensor(hx.rearrange("p (a n) -> p a n", a=4),
                                     bank(3)[:, 0:120].rearrange("p (a n) -> p a n", a=4),
                                     prm[:, R_B1:R_B1 + 4].unsqueeze(2).to_broadcast([P, 4, 2 * NCMP]), ALU.add))
                link(V.tensor_tensor(hy, hx, hx, ALU.mult))
                link(V.tensor_scalar(hy, hy, 0.044715, 1.0, ALU.mult, ALU.add))
                link(V.tensor_tensor(hy, hy, hx, ALU.mult), dve_hx)
                dve.wait_ge(act_hs, 1)
                link(V.tensor_tensor(tail[:, 6832:6952], hx, hy, ALU.mult), dve_hT)
                dve.wait_ge(pe_ckv, 1)
                link(V.tensor_copy(kcT[:], bank(2)[:, 0:NCMP]), dve_ckv)
                link(V.tensor_copy(vc[:].rearrange("p g d -> p (g d)"), bank(2)[0:NCMP, 128:256]), dve_ckv)

                dve.wait_ge(pe_cs, 1)
                dve.wait_ge(pool_cst, 6)
                for g in range(G):
                    for t in range(T):
                        link(V.scalar_tensor_tensor(Pc[:, g, t], bank(4 + g)[:, t * 60:t * 60 + 60].rearrange(
                            "p (j c) -> p j c", j=J), HD ** -0.5,
                            cmask[:, t, :].unsqueeze(1).to_broadcast([P, J, NCMP]), ALU.mult, ALU.add))
                pc16 = tail[:, 6952:7192].rearrange("p (a c) -> p a c", c=NCMP)
                link(V.tensor_reduce(cnm[:], pc16, AX, ALU.max))
                link(V.tensor_tensor(pc16, pc16, cnm[:].unsqueeze(2).to_broadcast([P, 16, NCMP]), ALU.subtract), dve_cx)
                dve.wait_ge(act_ce, 1)
                link(V.tensor_reduce(csm[:], pc16, AX, ALU.add))
                link(V.reciprocal(csm[:], csm[:]))
                c4 = csm[:].rearrange("p (g t j) -> p g t j", g=G, t=T)
                for t in range(T):
                    gt0 = gates[:, t, :].rearrange("p (g j b) -> p g j b", g=G, j=J)[:, :, :, 0]
                    link(V.tensor_tensor(c4[:, :, t, :], c4[:, :, t, :], gt0, ALU.mult))
                    link(V.tensor_scalar(c4[:, :, t, :], c4[:, :, t, :], valid[:, t:t + 1], None, ALU.mult))
                link(V.tensor_tensor(pc16, pc16, csm[:].unsqueeze(2).to_broadcast([P, 16, NCMP]), ALU.mult), dve_cp)

                def mask_max(n):
                    t, b = n // J, n % 2
                    nk = P * (t + 1)
                    dve.wait_ge(pe_sc, n + 1)
                    if n >= 2:
                        dve.wait_ge(pe_pt, n - 1)
                    sc = bank(2 * b, 2).rearrange("p (a n) -> p a n", a=4)[:, :, 0:nk]
                    pb = Pb[:, b].rearrange("p g k n -> p (g k) n")[:, :, 0:nk]
                    mk = mask[:, S - nk:S].unsqueeze(1).to_broadcast([P, 4, nk])
                    link(V.scalar_tensor_tensor(pb, sc, HD ** -0.5, mk, ALU.mult, ALU.add))
                    link(V.tensor_reduce(nmx[:, b, :], pb, AX, ALU.max, negate=True), dve_sx)

                def weigh(n):
                    t, j, b = n // J, n % J, n % 2
                    nk = P * (t + 1)
                    dve.wait_ge(act_e, 4 * (n + 1))
                    link(V.reciprocal(cof[:, b, :], smx[:, b, :]))
                    gt2 = gates[:, t, :].rearrange("p (g j b) -> p g j b", g=G, j=J)[:, :, j, 1:3]
                    c2 = cof[:, b, :].rearrange("p (g k) -> p g k", g=G)
                    link(V.tensor_tensor(c2, c2, gt2, ALU.mult))
                    pb = Pb[:, b].rearrange("p g k n -> p (g k) n")[:, :, 0:nk]
                    link(V.tensor_tensor(pb, pb, cof[:, b, :].unsqueeze(2).to_broadcast([P, 4, nk]), ALU.mult), dve_p)

                for n in range(T * J):
                    mask_max(n)
                    if n >= 1:
                        weigh(n - 1)
                weigh(T * J - 1)

                for t in range(T):
                    dve.wait_ge(pe_pv, t + 1)
                    link(V.tensor_copy(oT[:, :, t * P:(t + 1) * P], bank(6 + t).rearrange("p (j n) -> p j n", j=J)))
                link(V.tensor_tensor(sq[:, 0:4, :], oT, oT, ALU.mult))
                link(V.tensor_tensor(sq[:, 4:8, :], convT[:], convT[:], ALU.mult), dve_sq)
                link(V.tensor_tensor(oT, oT, prm[:, R_NSA:R_NSA + J].unsqueeze(2).to_broadcast([P, J, S]), ALU.mult), dve_o)
                link(V.tensor_tensor(convT[:], convT[:], prm[:, R_CNV:R_CNV + CC].unsqueeze(2).to_broadcast([P, CC, S]),
                                     ALU.mult), dve_o)
                dve.wait_ge(act_sst, 1)
                link(V.reciprocal(rst[:, 0:4], rst[:, 0:4]), dve_seq)
                for t in range(T):
                    dve.wait_ge(pe_mo, t + 1)
                    for part in range(2):
                        ins = V.scalar_tensor_tensor(H[:, t, :], bank(4 * t + 2 * part, 2), rst[:, 2 * t + part:2 * t + part + 1],
                                                     H[:, t, :], ALU.mult, ALU.add)
                        link(ins, dve_h1 if t == 1 and part == 1 else None)
                norm(H, XS, 2)
                tr_out(2, XT, 0, R_XA)

                for h in range(XH):
                    dve.wait_ge(pe_s2, h + 1)
                    link(V.tensor_reduce(cnm[:, 2 * h:2 * h + 2], bank(h).rearrange("p (t n) -> p t n", t=T), AX, ALU.max,
                                         negate=True))
                    link(V.tensor_scalar(cnm[:, 2 * h:2 * h + 2], cnm[:, 2 * h:2 * h + 2], XD ** -0.5, None, ALU.mult), dve_m2)
                for h in range(XH):
                    dve.wait_ge(act_e2, 2 * (h + 1))
                    link(V.reciprocal(csm[:, 2 * h:2 * h + 2], csm[:, 2 * h:2 * h + 2]))
                    link(V.tensor_tensor(P2[:, h], P2[:, h], csm[:, 2 * h:2 * h + 2].unsqueeze(2).to_broadcast([P, T, S]),
                                         ALU.mult), dve_p2)
                for t in range(T):
                    dve.wait_ge(pe_xo, t + 1)
                    link(V.tensor_tensor(H[:, t, :], H[:, t, :], bank(4 + 2 * t, 2), ALU.add), dve_h2 if t == 1 else None)
                norm(H, XS, 3)
                tr_out(3, XT, 0, R_MOE)

                dve.wait_ge(pe_lg, 1)
                dve.wait_ge(pool_moe, 8)
                dve.wait_ge(ld_misc, 64)
                link(V.tensor_tensor(lg, bank(4)[:, 0:2 * E].rearrange("p (t e) -> p t e", t=T),
                                     b_rt[:].unsqueeze(1).to_broadcast([P, T, E]), ALU.add))
                for t in range(T):
                    link(V.max(top[:, t, :], lg[:, t, :]))
                link(V.tensor_scalar(gneg, top[:, :, 0], -1.0, None, ALU.mult), dve_ng)
                for t in range(T):
                    fourth = top[:, t, 3:4]
                    link(V.tensor_scalar(gt[:, t, :], lg[:, t, :], fourth, None, ALU.is_gt))
                    link(V.tensor_scalar(eq[:, t, :], lg[:, t, :], fourth, None, ALU.is_equal))
                    link(V.tensor_tensor_scan(cum[:, t, :], eq[:, t, :], zer, 0.0, ALU.add, ALU.add))
                link(V.tensor_reduce(need, gt, AX, ALU.add))
                link(V.tensor_scalar(need, need, -1.0, 4.0, ALU.mult, ALU.add))
                for t in range(T):
                    link(V.tensor_scalar(cum[:, t, :], cum[:, t, :], need[:, t:t + 1], None, ALU.is_le))
                link(V.tensor_tensor(eq, eq, cum, ALU.mult))
                link(V.tensor_tensor(gt, gt, eq, ALU.add), dve_g)
                dve.wait_ge(act_gx, 2)
                link(V.tensor_tensor(gex, gex, gt, ALU.mult))
                link(V.tensor_reduce(gsum, gex, AX, ALU.add))
                link(V.reciprocal(gsum, gsum))
                for t in range(T):
                    for r in range(ROUNDS):
                        ins = V.tensor_scalar(gtab[:, t, r * E:(r + 1) * E], gex[:, t, :], gsum[:, t:t + 1], None, ALU.mult)
                        link(ins, dve_g if (t, r) == (T - 1, ROUNDS - 1) else None)
                dve.wait_ge(pe_cnt, 1)
                for t in range(T):
                    place = bank(5)[:, t * E:(t + 1) * E]
                    link(V.scalar_tensor_tensor(lg[:, t, :], place, 1.0, gt[:, t, :], ALU.add, ALU.mult))
                    for r in range(ROUNDS):
                        link(V.tensor_scalar(keys[:, t, r * E:(r + 1) * E], lg[:, t, :], -1.0 - SLOTS * r, None, ALU.add))
                link(V.tensor_reduce(cmx, bank(5)[0:1, 2 * E:3 * E], AX, ALU.max))
                for r in range(ROUNDS):
                    link(V.tensor_scalar(flg[0:1, r:r + 1], cmx, float(SLOTS * r), None, ALU.is_gt),
                         dve_flg if r == ROUNDS - 1 else None)
                dve.wait_ge(pe_gT, 1)
                link(V.tensor_copy(gTe, bank(6)[0:E, 0:S]), dve_gT)
                dve.wait_ge(ld_bias, 48)
                link(V.tensor_copy(b_prt, b_raw))
                for part, src in ((1, b_raw), (2, b_res)):
                    for q in range(part * E, 96, E):
                        link(V.tensor_tensor(b_res[q:q + E], src[q:q + E], b_prt[q:q + E], ALU.subtract))
                        link(V.tensor_copy(b_prt[q:q + E], b_res[q:q + E]), dve_bp if part == 2 else None)
                dve.wait_ge(pe_bd, 1)
                for t in range(T):
                    link(V.tensor_tensor(H[:, t, :], H[:, t, :], bank(2 * t, 2), ALU.add), dve_bd)

                def build_sel(c):
                    for t in range(T):
                        yield V.tensor_tensor(sel1[:, t, :].rearrange("p (s n) -> p s n", s=2),
                                              iot.unsqueeze(1).to_broadcast([P, 2, SLOTS]),
                                              keys[:, t, bass.ds(c, 2)].unsqueeze(2).to_broadcast([P, 2, SLOTS]),
                                              ALU.is_equal)

                def build_selg(c):
                    for t in range(T):
                        yield V.tensor_tensor(selg[:, t, :].rearrange("p (s n) -> p s n", s=2),
                                              sel1[:, t, :].rearrange("p (s n) -> p s n", s=2),
                                              gtab[:, t, bass.ds(c, 2)].unsqueeze(2).to_broadcast([P, 2, SLOTS]),
                                              ALU.mult)

                def build_bsel(i):
                    return V.tensor_tensor(bsel, bdiff, first[:, bass.ds(i, 1)].to_broadcast([96, P]), ALU.is_equal)

                def xg_out():
                    return V.tensor_tensor(xgT, bank(6, 2).rearrange("p (k n) -> p k n", k=KC),
                                           prm[:, R_MOE:R_MOE + KC].unsqueeze(2).to_broadcast([P, KC, P]), ALU.mult)

                for ins in build_sel(0):
                    link(ins, m_sel)
                for ins in build_selg(0):
                    link(ins, m_selg)
                link(build_bsel(0), m_bsel)
                link(V.memset(cmx, 0.0), m_add)
                dve.wait_ge(m_gath, 1)
                link(xg_out(), m_xg)
                with dve.Fori(0, ROUNDS) as r:
                    on = dve.value_load(flg[0:1, bass.ds(r, 1)], min_val=0, max_val=1)
                    with dve.If(on > 0):
                        with dve.Fori(0, PAIRS) as p:
                            k = r * PAIRS + p
                            dve.wait_ge(m_gath, k + 1)
                            dve.wait_ge(m_selg, 2 * k + 2)
                            for ins in build_sel(k * 2 + 2):
                                ins.then_inc(m_sel, 1)
                            dve.wait_ge(m_bias, k + 1)
                            build_bsel(k + 1).then_inc(m_bsel, 1)
                            dve.wait_ge(freed, k * FILLS + KC)
                            V.tensor_scalar(gcl, bank(0, 2), LIM, None, ALU.min).then_inc(m_gcl, 1)
                            V.tensor_scalar(ucl, bank(2, 2), LIM, -LIM, ALU.min, ALU.max).then_inc(m_seq, 1)
                            dve.wait_ge(m_gcl, k + 1)
                            dve.wait_ge(m_seq, k * 2 + 1)
                            V.scalar_tensor_tensor(ucl, ucl, 1.0, gcl, ALU.add, ALU.mult).then_inc(m_seq, 1)
                            dve.wait_ge(m_seq, k * 2 + 2)
                            dve.wait_ge(m_sg, k + 1)
                            V.tensor_tensor(ucl, ucl, sgm, ALU.mult).then_inc(m_h, 1)
                            dve.wait_ge(m_gath, k + 2)
                            xg_out().then_inc(m_xg, 1)
                            dve.wait_ge(m_tr, k + 1)
                            V.tensor_copy(hTm[:, 0:4, :].rearrange("p k n -> p (k n)"), bank(4)).then_inc(m_trD, 1)
                            dve.wait_ge(m_sgT, k + 1)
                            V.tensor_copy(selgT.rearrange("p t n -> p (t n)"), bank(6)[:, 0:S]).then_inc(m_sgTc, 1)
                            dve.wait_ge(freed, k * FILLS + FILLS)
                            V.tensor_copy(orow[:, 0:BANK], bank(4)).then_inc(m_oD, 1)
                            dve.wait_ge(m_sel, 2 * k + 4)
                            for ins in build_selg(k * 2 + 2):
                                ins.then_inc(m_selg, 1)
                            for q in range(4):
                                t, n = q // 2, q % 2
                                hh = H[:, t, n * BANK:(n + 1) * BANK]
                                dve.wait_ge(m_y, k * 4 + q + 1)
                                V.tensor_tensor(hh, hh, bank(6 + n), ALU.add).then_inc(m_add, 1)
                            dve.wait_ge(m_add, k * 4 + 5)

            @block.tensor
            def _(pe):
                mm = nc.tensor.matmul

                def tr(dst, src):
                    k = src.shape[0]
                    return nc.tensor.transpose(dst, src, ident[0:k, 0:k])

                def transpose_rows(i, b0, waits):
                    pe.wait_ge(dve_norm, 2 * (i + 1))
                    for b in range(4):
                        for s, v in waits(b):
                            pe.wait_ge(s, v)
                        for a in range(2):
                            for t in range(T):
                                c = 2 * b + a
                                last = tr(bank(b0 + b)[:, a * S + t * P:a * S + (t + 1) * P], XS[:, t, c * P:(c + 1) * P])
                        last.then_inc(pe_tr, 1)

                pe.wait_ge(pool_id, 1)
                pe.wait_ge(ld_prm, 16 * 12)
                tr(bank(7)[:, 0:R_END], prm_rows[:]).then_inc(pe_prm, 1)
                transpose_rows(0, 0, lambda b: [])
                pe.wait_ge(dve_tr, 4)
                for kc in range(KC):
                    pe.wait_ge(ld_a[kc], 16)
                    for c in range(KC):
                        last = mm(bank(c // 2)[:, (c % 2) * S:(c % 2 + 1) * S], w_a[:, kc, c * P:(c + 1) * P], MT[:, kc, :],
                                  start=(kc == 0 and c % 2 == 0), stop=(kc == KC - 1), skip_group_check=True)
                    last.then_inc(a_used, 1)
                transpose_rows(1, 4, lambda b: [(dve_prm, 1)])

                def rows(t):
                    for kc in range(KC):
                        pe.wait_ge(ld_row[kc], 16)
                        for n, w in ((0, BANK), (1, BANK), (2, ROWC - 2 * BANK)):
                            last = mm(bank(4 + n)[:, 0:w], XT[:, kc, t * P:(t + 1) * P], w_row[:, kc, n * BANK:n * BANK + w],
                                      start=(kc == 0), stop=(kc == KC - 1))
                    last.then_inc(pe_row, 1)

                pe.wait_ge(dve_tr, 8)
                rows(0)
                pe.wait_ge(act_k, 4)
                for kc in range(KC):
                    pe.wait_ge(ld_a[kc], 32)
                    for t in range(T):
                        for n in range(2):
                            last = mm(bank(2 * t + n), MT[:, kc, t * P:(t + 1) * P], w_a[:, kc, n * BANK:(n + 1) * BANK],
                                      start=(kc == 0), stop=(kc == KC - 1))
                    last.then_inc(a_used, 1)
                pe.wait_ge(dve_rope, 1)
                pe.wait_ge(act_rows, 2)
                rows(1)
                pe.wait_ge(act_v, 4)
                pe.wait_ge(ld_cnv, 16 * KC)
                for i in range(CC):
                    if i >= 2:
                        pe.wait_ge(dve_cnv, i - 1)
                    for which, (b, half) in enumerate(((0, 0), (1, 0), (0, 1))):
                        for kc in range(KC):
                            last = mm(bank(2 * (i % 2) + b)[:, half * S:(half + 1) * S],
                                      w_cnv[:, kc, which * CONVW + i * P:which * CONVW + (i + 1) * P], XT[:, kc, :],
                                      start=(kc == 0), stop=(kc == KC - 1))
                    last.then_inc(pe_cnv, 1)
                pe.wait_ge(dve_rope, 2)
                pe.wait_ge(act_rows, 4)
                for j in range(J):
                    for t in range(T):
                        tr(bank(4 + j // 2)[:, (j % 2) * S + t * P:(j % 2) * S + (t + 1) * P], qrot[:, t, j * P:(j + 1) * P])
                for kd in range(2):
                    for t in range(T):
                        last = tr(bank(6)[:, kd * S + t * P:kd * S + (t + 1) * P], krot[:, t, 1 + kd, :])
                last.then_inc(pe_qkT, 1)
                for v, src in enumerate((krot, vrow)):
                    if v == 1:
                        pe.wait_ge(dve_cnv, CC)
                    for g in range(G):
                        for t in range(T):
                            for i in range(2):
                                last = mm((bank(7) if v == 0 else bank(0))[i * HD:(i + 1) * HD, g * S + t * P:g * S + (t + 1) * P],
                                          src[:, t, 0, g * HD:(g + 1) * HD], ident[:], start=True, stop=True)
                    last.then_inc(pe_cT, 1)
                pe.wait_ge(dve_cnv, CC)
                pe.wait_ge(ld_c1, 32)
                for v in range(2):
                    pe.wait_ge(dve_blk, 8 * (v + 1))
                    for m in range(MC):
                        last = mm(bank(1 + v)[0:2 * NCMP, 0:CHID], blk[:, v, m].rearrange("p g c -> p (g c)"),
                                  w_c1[:, v, m, :], start=(m == 0), stop=(m == MC - 1))
                    last.then_inc(pe_hid, 1)
                for v in range(2):
                    pe.wait_ge(act_hid, v + 1)
                    for c in range(2):
                        last = tr(bank(3)[:, (2 * v + c) * 30:(2 * v + c + 1) * 30], hid[:, v * CHID + c * P:v * CHID + (c + 1) * P])
                last.then_inc(pe_hidT, 1)
                pe.wait_ge(dve_hT, 1)
                pe.wait_ge(ld_misc, 64)
                for g in range(G):
                    for c in range(2):
                        mm(bank(2)[g * HD:(g + 1) * HD, 0:NCMP], w_c2[:, 0, c, :], hT[:, 0, c, g * NCMP:(g + 1) * NCMP],
                           start=(c == 0), stop=(c == 1))
                for g in range(G):
                    for c in range(2):
                        last = mm(bank(2)[0:NCMP, 128 + g * HD:128 + (g + 1) * HD], hT[:, 1, c, g * NCMP:(g + 1) * NCMP],
                                  w_c2[:, 1, c, :], start=(c == 0), stop=(c == 1))
                last.then_inc(pe_ckv, 1)
                pe.wait_ge(dve_ckv, 2)
                pe.wait_ge(act_qkT, 3)
                for t in range(T):
                    for j in range(J):
                        for g in range(G):
                            gp = slice(g * HD, (g + 1) * HD)
                            last = mm(bank(4 + g)[:, t * 60 + j * 15:t * 60 + j * 15 + 15], qT[gp, j, t * P:(t + 1) * P],
                                      kcT[gp, :], start=True, stop=True)
                last.then_inc(pe_cs, 1)

                def scores(n):
                    t, j = n // J, n % J
                    nk = P * (t + 1)
                    if n >= 2:
                        pe.wait_ge(dve_sx, n - 1)
                    for g in range(G):
                        gp = slice(g * HD, (g + 1) * HD)
                        last = mm(bank(2 * (n % 2) + g).rearrange("p (k n) -> p k n", k=2)[:, :, 0:nk],
                                  qT[gp, j, t * P:(t + 1) * P], kT[gp, :, 0:nk], start=True, stop=True)
                    last.then_inc(pe_sc, 1)

                scores(0)
                pe.wait_ge(dve_cp, 1)
                for t in range(T):
                    for g in range(G):
                        for j in range(J):
                            last = tr(bank(4 + 2 * t + g)[0:NCMP, j * P:(j + 1) * P], Pc[:, g, t, j, :])
                last.then_inc(pe_cpt, 1)

                def p_transposes(n):
                    t = n // J
                    pe.wait_ge(dve_p, n + 1)
                    pe.wait_ge(act_cpt, 4)
                    if n >= 1:
                        pe.wait_ge(act_pt, 2 * n)
                    for g in range(G):
                        for k in range(2):
                            for b in range(t + 1):
                                i = k * (t + 1) + b
                                last = tr(bank(4 + g)[:, i * P:(i + 1) * P], Pb[:, n % 2, g, k, b * P:(b + 1) * P])
                    last.then_inc(pe_pt, 1)

                for n in range(T * J):
                    if n + 1 < T * J:
                        scores(n + 1)
                    p_transposes(n)
                    if n % J == J - 1:
                        t = n // J
                        pe.wait_ge(act_pt, 2 * (n + 1))
                        nb = 2 * (t + 1)
                        for i in range(nb + 1):
                            for g in range(G):
                                o = bank(6 + t)[g * HD:(g + 1) * HD, :]
                                if i < nb:
                                    k, b = i // (t + 1), i % (t + 1)
                                    last = mm(o, vrow[:, b, 1 + k, g * HD:(g + 1) * HD], PT[g][:, i, :, :],
                                              start=(i == 0), stop=False)
                                else:
                                    last = mm(o, vc[:, g, :], PTc[:, g, t, :], start=False, stop=True)
                        last.then_inc(pe_pv, 1)
                pe.wait_ge(dve_sq, 1)
                pe.wait_ge(pool_cst, 6)
                for t in range(T):
                    for part in range(2):
                        for c in range(4):
                            last = mm(bank(4)[:, 2 * t + part:2 * t + part + 1], sq[:, 4 * part + c, t * P:(t + 1) * P],
                                      ones[:, 0:1], start=(c == 0), stop=(c == 3))
                last.then_inc(pe_ss, 1)
                pe.wait_ge(dve_o, 2)
                pe.wait_ge(ld_out, 16 * 9)
                for t in range(T):
                    if t == 1:
                        pe.wait_ge(act_sst, 1)
                    for part, src in enumerate((oT, convT)):
                        for n in range(2):
                            for c in range(4):
                                last = mm(bank(4 * t + 2 * part + n), src[:, c, t * P:(t + 1) * P],
                                          w_out[:, 4 * part + c, n * BANK:(n + 1) * BANK], start=(c == 0), stop=(c == 3))
                    last.then_inc(pe_mo, 1)
                transpose_rows(2, 0, lambda b: [])
                pe.wait_ge(dve_tr, 12)
                pe.wait_ge(ld_q2, 16)
                for c in range(KC):
                    for kc in range(KC):
                        last = mm(bank(4 + c // 2)[:, (c % 2) * S:(c % 2 + 1) * S], w_q2[:, kc, c * P:(c + 1) * P], XT[:, kc, :],
                                  start=(kc == 0), stop=(kc == KC - 1))
                    if c % 2 == 1:
                        last.then_inc(pe_q2, 1)
                for h in range(XH):
                    pe.wait_ge(act_q2, h + 1)
                    for t in range(T):
                        for c in range(2):
                            last = mm(bank(h)[:, t * S:(t + 1) * S], q2T[:, 2 * h + c, t * P:(t + 1) * P], MK[:, 2 * h + c, :],
                                      start=(c == 0), stop=(c == 1))
                    last.then_inc(pe_s2, 1)
                for h in range(XH):
                    pe.wait_ge(dve_p2, h + 1)
                    for m in range(2):
                        for t in range(T):
                            last = tr(bank(4 + h)[:, m * S + t * P:m * S + (t + 1) * P], P2[:, h, t, m * P:(m + 1) * P])
                    last.then_inc(pe_p2t, 1)
                for h in range(XH):
                    pe.wait_ge(act_p2t, h + 1)
                    for c in range(2):
                        for m in range(2):
                            last = mm(bank(h)[:, c * S:(c + 1) * S], MV[:, m, h * XD + c * P:h * XD + (c + 1) * P],
                                      P2T[:, h, m, :], start=(m == 0), stop=(m == 1))
                    last.then_inc(pe_o2, 1)
                pe.wait_ge(act_o2, XH)
                pe.wait_ge(ld_o2, 16)
                for t in range(T):
                    for n in range(2):
                        for c in range(KC):
                            last = mm(bank(4 + 2 * t + n), o2T[:, c, t * P:(t + 1) * P], w_o2[:, c, n * BANK:(n + 1) * BANK],
                                      start=(c == 0), stop=(c == KC - 1))
                    last.then_inc(pe_xo, 1)
                transpose_rows(3, 0, lambda b: [])
                pe.wait_ge(dve_tr, 16)
                for t in range(T):
                    for kc in range(KC):
                        last = mm(bank(4)[:, t * E:(t + 1) * E], XT[:, kc, t * P:(t + 1) * P], w_rt[:, kc, :],
                                  start=(kc == 0), stop=(kc == KC - 1))
                last.then_inc(pe_lg, 1)
                pe.wait_ge(dve_g, 1)
                mm(bank(5)[:, 0:E], tri[:], gt[:, 0, :], start=True, stop=True)
                mm(bank(5)[:, E:2 * E], tri[:], gt[:, 1, :], start=True, stop=False)
                mm(bank(5)[:, E:2 * E], ones[:, 0:1].to_broadcast([P, P]), gt[:, 0, :], start=False, stop=True)
                for t in range(T):
                    last = mm(bank(5)[0:1, 2 * E:3 * E], ones[:, 0:1], gt[:, t, :], start=(t == 0), stop=(t == 1))
                last.then_inc(pe_cnt, 1)
                pe.wait_ge(dve_g, 2)
                for t in range(T):
                    last = tr(bank(6)[0:E, t * P:(t + 1) * P], gtab[:, t, 0:E])
                last.then_inc(pe_gT, 1)
                pe.wait_ge(dve_gT, 1)
                pe.wait_ge(ld_end, 32)
                for t in range(T):
                    for n in range(2):
                        last = mm(bank(2 * t + n), gTe[:, t * P:(t + 1) * P], bdn[:, n * BANK:(n + 1) * BANK],
                                  start=True, stop=True)
                last.then_inc(pe_bd, 1)

                def gather():
                    for c in range(KC):
                        for t in range(T):
                            last = mm(bank(6 + c // 4)[:, (c % 4) * P:(c % 4 + 1) * P], XS[:, t, c * P:(c + 1) * P],
                                      sel1[:, t, :], start=(t == 0), stop=(t == 1))
                    return last

                pe.wait_ge(m_sel, 2)
                gather().then_inc(m_gath, 1)
                pe.wait_ge(dve_bp, 1)
                pe.wait_ge(dve_bd, 2)
                with pe.Fori(0, ROUNDS) as r:
                    on = pe.value_load(flg[0:1, bass.ds(r, 1)], min_val=0, max_val=1)
                    with pe.If(on > 0):
                        with pe.Fori(0, PAIRS) as p:
                            k = r * PAIRS + p
                            pe.wait_ge(m_bsel, k + 1)
                            for n in range(4):
                                last = mm(bank(n), bsel, b_prt[:, n * BANK:(n + 1) * BANK], start=True, stop=False,
                                          skip_group_check=True)
                            last.then_inc(m_bias, 1)
                            pe.wait_ge(m_xg, k + 1)
                            for j in range(KC):
                                pe.wait_ge(arrived[j % RING], k * 64 + 32 * (j // RING + 1))
                                for n in range(4):
                                    for s in range(2):
                                        last = mm(bank(n)[s * SLOTS:(s + 1) * SLOTS, :], xgT[:, j, s * SLOTS:(s + 1) * SLOTS],
                                                  ring[:, j % RING, s, n * BANK:(n + 1) * BANK], start=False,
                                                  stop=(j == KC - 1), skip_group_check=True)
                                last.then_inc(freed, 1)
                            pe.wait_ge(m_sel, 2 * k + 4)
                            pe.wait_ge(m_add, k * 4 + 1)
                            gather().then_inc(m_gath, 1)
                            pe.wait_ge(m_h, k + 1)
                            for f in range(KC):
                                last = tr(bank(4 + f // 4)[:, (f % 4) * P:(f % 4 + 1) * P], ucl[:, f * P:(f + 1) * P])
                            last.then_inc(m_tr, 1)
                            pe.wait_ge(m_selg, 2 * k + 2)
                            pe.wait_ge(m_xg, k + 2)
                            for t in range(T):
                                last = tr(bank(6)[:, t * P:(t + 1) * P], selg[:, t, :])
                            last.then_inc(m_sgT, 1)
                            pe.wait_ge(m_trD, k + 1)
                            pe.wait_ge(m_trA, k + 1)
                            for j in range(KC, FILLS):
                                pe.wait_ge(arrived[j % RING], k * 64 + 32 * (j // RING + 1))
                                for c in range(2):
                                    f = 2 * (j - KC) + c
                                    for n in range(2):
                                        for s in range(2):
                                            last = mm(bank(4 + n)[s * SLOTS:(s + 1) * SLOTS, :],
                                                      hTm[:, f, s * SLOTS:(s + 1) * SLOTS],
                                                      ring[:, j % RING, s, c * D + n * BANK:c * D + (n + 1) * BANK],
                                                      start=(f == 0), stop=(f == KC - 1))
                                last.then_inc(freed, 1)
                            pe.wait_ge(m_oD, k + 1)
                            pe.wait_ge(m_oA, k + 1)
                            pe.wait_ge(m_sgTc, k + 1)
                            for q in range(4):
                                t, n = q // 2, q % 2
                                if q >= 2:
                                    pe.wait_ge(m_add, k * 4 + q)
                                mm(bank(6 + n), selgT[:, t, :], orow[:, n * BANK:(n + 1) * BANK],
                                   start=True, stop=True).then_inc(m_y, 1)

        with nc.Block() as block:

            @block.scalar
            def _(act):
                for t in range(T):
                    nc.scalar.activation(XS[:, t, :], H[:, t, :], ACT.Square, accum_out=ss[:, t:t + 1]).then_inc(f_ss, 1)
                act.wait_ge(f_ss, T)
                nc.scalar.activation(rst[:, 0:T], ss[:, 0:T], ACT.Sqrt, bias=eps[:], scale=1.0 / D).then_inc(f_sq, 1)

            @block.vector
            def _(dve):
                dve.wait_ge(f_sq, 1)
                nc.vector.reciprocal(rst[:, 0:T], rst[:, 0:T]).then_inc(f_sq, 1)
                dve.wait_ge(f_sq, 2)
                for t in range(T):
                    nc.vector.scalar_tensor_tensor(H[:, t, :], H[:, t, :], rst[:, t:t + 1], gfin, ALU.mult, ALU.mult
                                                   ).then_inc(f_out, 1)

            @block.sync
            def _(sp):
                for t in range(T):
                    sp.wait_ge(f_out, t + 1)
                    sp.dma_start(out_v[:, t, :], H[:, t, :]).then_inc(st_out, 16)
                sp.wait_ge(st_out, 16 * T)


_INS = ['x', 'mem', 'positions', 'g_mix_norm', 'w_mix_in', 'cmp_pos_k', 'cmp_pos_v', 'cmp_w1_k', 'cmp_b1_k',
        'cmp_w2_k', 'cmp_w1_v', 'cmp_b1_v', 'cmp_w2_v', 'conv_w', 'g_nsa_out', 'g_conv_out', 'w_mix_out',
        'g_xattn_norm', 'g_mem_norm', 'w_xq', 'w_xkv', 'w_xo', 'g_moe_norm', 'w_router', 'b_router', 'w_gate_up',
        'b_gate_up', 'w_down', 'b_down', 'g_final']


def kernel(**inputs):
    import concourse.bacc as _bacc
    from concourse.bass_utils import run_bass_kernel_spmd as _run

    nc = _bacc.Bacc("TRN2", target_bir_lowering=False, num_devices=1)
    arrays, args = {}, []
    half = HD // 2
    freq = (10000.0 ** (-np.arange(half) / half)).astype(np.float32).reshape(1, half)
    for name in _INS + ['inv_freq']:
        a = freq if name == 'inv_freq' else np.ascontiguousarray(inputs[name])
        arrays[f"in_{name}"] = a
        args.append(nc.dram_tensor(f"in_{name}", a.shape, mybir.dt.from_np(a.dtype), kind="ExternalInput").ap())
    args.append(nc.dram_tensor("out_0", (1, S, D), F32, kind="ExternalOutput").ap())
    trunk(nc, *args)
    r = _run(nc, [arrays], core_ids=[0])
    return r.results[0]["out_0"]
```

```python
import numpy as np
import concourse.bass as bass
from concourse import mybir
from contextlib import ExitStack

F32 = mybir.dt.float32
BF16 = mybir.dt.bfloat16
I32 = mybir.dt.int32
ALU = mybir.AluOpType
ACT = mybir.ActivationFunctionType
AX = mybir.AxisListType.X

P = 128
BANK = 512
D = 1024
S = 256
T = S // P
KC = D // P
HD = 64
G, J = 2, 4
NSA = G * J * HD
ROWC = 1304
CONVW = 512
CC = CONVW // P
NCMP, CSTR, CLEN, CHID = 15, 16, 32, 256
MC = CLEN * HD // P
XH, XD = 4, 256
E = 32
FF = 1024
LIM, ALPHA = 7.0, 1.702
SLOTS = 64
PAIRS = E // 2
ROUNDS = S // SLOTS
FILLS = 12
RING = 8
HALF = 2
EPS = 1e-5
NEG = -1e30
R_MIX, R_XA, R_MEM, R_MOE, R_NSA, R_CNV, R_B1, R_CW, R_POS, R_END = 0, 8, 16, 24, 32, 36, 40, 44, 56, 88


def links(eng, default):
    count = {}

    def link(ins, sem=None):
        sem = default if sem is None else sem
        key = id(sem)
        count[key] = count.get(key, 0) + 1
        ins.then_inc(sem, 1)
        eng.wait_ge(sem, count[key])

    return link


def trunk(nc, x, mem, positions, g_mix_norm, w_mix_in, cmp_pos_k, cmp_pos_v, cmp_w1_k, cmp_b1_k,
          cmp_w2_k, cmp_w1_v, cmp_b1_v, cmp_w2_v, conv_w, g_nsa_out, g_conv_out, w_mix_out,
          g_xattn_norm, g_mem_norm, w_xq, w_xkv, w_xo, g_moe_norm, w_router, b_router, w_gate_up,
          b_gate_up, w_down, b_down, g_final, inv_freq, out):
    ctx = ExitStack()
    with ctx:
        def sb(name, shape, dt=F32):
            return ctx.enter_context(nc.sbuf_tensor(name, shape, dt))

        def sem(name):
            return ctx.enter_context(nc.semaphore(name))

        R = sb("R", [P, 24576])
        A = sb("A", [P, 8192])
        H = sb("H", [P, T, D])
        XS = sb("XS", [P, T, D])
        XT = sb("XT", [P, KC, S])
        MT = sb("MT", [P, KC, S])
        MK = sb("MK", [P, KC, S])
        MV = sb("MV", [P, T, D])
        w_row = R[:, 0:KC * ROWC].rearrange("p (k n) -> p k n", k=KC)
        w_cnv = R[:, KC * ROWC:KC * (ROWC + 3 * CONVW)].rearrange("p (k n) -> p k n", k=KC)
        w_out = R[:, 0:8192].rearrange("p (k n) -> p k n", k=KC)
        w_xv = R[:, 8192:16384].rearrange("p (k n) -> p k n", k=KC)
        w_o2 = R[:, 16384:24576].rearrange("p (k n) -> p k n", k=KC)
        tail = R[:, 16384:24576]
        w_a = A[:, :].rearrange("p (k n) -> p k n", k=KC)
        w_c1 = A[:, :].rearrange("p (v m n) -> p v m n", v=2, m=MC)

        ident = sb("ident", [P, P])
        prm_rows = sb("prm_rows", [R_END, P])
        prm = sb("prm", [P, R_END])
        ones = sb("ones", [P, 1])
        eps = sb("eps", [P, 1])
        ss = sb("ss", [P, 4])
        rst = sb("rst", [P, 4])
        pos_i = sb("pos_i", [P, T], I32)
        pos_f = sb("pos_f", [P, T])
        invf = sb("invf", [P, 32])
        ang = sb("ang", [P, T, 32])
        turn = sb("turn", [P, T, 32])
        rem = sb("rem", [P, 2, T, 32])
        trig = sb("trig", [P, 2, T, 32])
        QA = sb("QA", [P, 2048])
        KA = sb("KA", [P, 2048])
        qrot = QA[:, 0:1024].rearrange("p (t n) -> p t n", t=T)
        krot = KA[:, 0:768].rearrange("p (t k n) -> p t k n", t=T, k=3)
        vrow = KA[:, 768:1536].rearrange("p (t k n) -> p t k n", t=T, k=3)
        gates = sb("gates", [P, T, 24])
        ra = sb("ra", [P, 256])
        rb = sb("rb", [P, 256])
        qT = QA[:, 1024:2048].rearrange("p (j n) -> p j n", j=J)
        kT = KA[:, 1536:2048].rearrange("p (k n) -> p k n", k=2)
        convT = sb("convT", [P, CC, S])
        mask = sb("mask", [P, S])
        cmask = sb("cmask", [P, T, NCMP])
        valid = sb("valid", [P, T])
        w_c2 = sb("w_c2", [P, 2, 2, HD])
        kcT = sb("kcT", [P, NCMP])
        vc = sb("vc", [NCMP, G, HD])
        nmx = sb("nmx", [P, 2, 4])
        smx = sb("smx", [P, 2, 4])
        cof = sb("cof", [P, 2, 4])
        cnm = sb("cnm", [P, 16])
        csm = sb("csm", [P, 16])
        w_rt = sb("w_rt", [P, KC, E])
        b_rt = sb("b_rt", [P, E])

        xsf = XS[:, :, :].rearrange("p t n -> p (t n)")
        ch_sb = xsf[:, 0:512].rearrange("p (b n) -> p b n", b=2)
        u_pad = xsf[:, 512:512 + S + 2]
        cy = xsf[:, 800:800 + S]
        cy2 = xsf[:, 1056:1056 + S]
        mkf = MK[:, :, :].rearrange("p a b -> p (a b)")
        mtf = MT[:, :, :].rearrange("p a b -> p (a b)")
        xtf = XT[:, :, :].rearrange("p a b -> p (a b)")
        kraw = mkf[:, 0:384].rearrange("p (k n) -> p k n", k=3)
        blk = mkf[:, 0:960].rearrange("p (v m g c) -> p v m g c", v=2, m=MC, g=G)
        hid = mkf[0:64, 960:960 + CHID]
        hx = mkf[:, 1472:1592]
        hy = mkf[:, 1592:1712]
        hTf = mkf[:, 1712:1832]
        hT = hTf.rearrange("p (v c n) -> p v c n", v=2, c=2)
        Pb = tail[:, 0:2048].rearrange("p (b g k n) -> p b g k n", b=2, g=2, k=2)
        oT = tail[:, 2048:3072].rearrange("p (j n) -> p j n", j=J)
        sqn = tail[:, 3072:4096].rearrange("p (t j n) -> p t j n", t=T, j=J)
        PTc = tail[0:NCMP, 3072:5120].rearrange("p (g t n) -> p g t n", g=G, t=T)
        Pcf = tail[:, 7168:7408]
        Pc = Pcf.rearrange("p (g t j c) -> p g t j c", g=G, t=T, j=J)
        PT = [tail[:, 5120:7168].rearrange("p (b j n) -> p b j n", b=4, j=J),
              xtf.rearrange("p (b j n) -> p b j n", b=4, j=J)]
        gsr = sb("gsr", [P, 4])
        sqs = sb("sqs", [P, 2, S])
        P2 = xsf.rearrange("p (t h n) -> p t h n", t=T, h=XH)
        qo2 = mtf.rearrange("p (t c n) -> p t c n", t=T, c=KC)
        P2T = xtf.rearrange("p (t h m n) -> p t h m n", t=T, h=XH, m=2)
        ring = [[R[:, (2 * f + h) * 2048:(2 * f + h + 1) * 2048] for h in range(2)] for f in range(6)]
        ring += [[QA[:, :], KA[:, :]], [mtf, xtf]]
        xgT = A[:, 0:1024].rearrange("p (k n) -> p k n", k=KC)
        gcl = A[:, 1024:2048]
        ucl = A[:, 2048:3072]
        sgm = A[:, 3072:4096]
        hTm = A[:, 4096:5120].rearrange("p (k n) -> p k n", k=KC)
        orow = A[:, 5120:6144]
        BW = 2 * FF + D
        b_raw = A[0:96, 0:BW]
        b_res = A[0:96, BW:2 * BW]
        b_prt = A[0:96, 2 * BW:2 * BW + BW // 2].bitcast(BF16)
        ROW = ROUNDS * E
        keys = mkf[:, 0:T * (ROW + 2)].rearrange("p (t c) -> p t c", t=T)
        gtab = mkf[:, 260:260 + T * (ROW + 2)].rearrange("p (t c) -> p t c", t=T)
        sel1 = mkf[:, 520:776].rearrange("p (t n) -> p t n", t=T)
        selg = mkf[:, 776:1032].rearrange("p (t n) -> p t n", t=T)
        selgT = mkf[:, 1032:1288].rearrange("p (t n) -> p t n", t=T)
        iot = mkf[:, 1288:1288 + SLOTS]
        bdiff = mkf[0:96, 1352:1352 + P]
        bsel = mkf[0:96, 1480:1480 + P // 2].bitcast(BF16)
        lg = mkf[:, 1552:1616].rearrange("p (t e) -> p t e", t=T)
        top = mkf[:, 1616:1632].rearrange("p (t e) -> p t e", t=T)
        gt = mkf[:, 1632:1696].rearrange("p (t e) -> p t e", t=T)
        eq = mkf[:, 1696:1760].rearrange("p (t e) -> p t e", t=T)
        cum = mkf[:, 1760:1824].rearrange("p (t e) -> p t e", t=T)
        need = mkf[:, 1824:1826]
        gex = mkf[:, 1826:1890].rearrange("p (t e) -> p t e", t=T)
        gsum = mkf[:, 1890:1892]
        gneg = mkf[:, 1892:1894]
        zer = mkf[:, 1894:1926]
        lead = mkf[0:96, 1959:1959 + ROUNDS * PAIRS + 1]
        cmx = mkf[0:1, 1958:1959]
        koff = mkf[:, 2030:2030 + ROUNDS]
        flg = sb("flg", [1, ROUNDS], I32)
        tri = ra[:, 0:P]
        mvf = MV[:, :, :].rearrange("p t n -> p (t n)")
        gfin = mvf[:, 0:D]

        ps = ctx.enter_context(nc.psum_tensor("ps", [P, 8 * BANK], F32))

        def bank(i, n=1):
            return ps[:, i * BANK:(i + n) * BANK]

        ld_x, ld_mem, ld_prm, ld_misc, ld_pos = sem("ld_x"), sem("ld_mem"), sem("ld_prm"), sem("ld_misc"), sem("ld_pos")
        ld_row = [sem(f"ld_row{i}") for i in range(KC)]
        ld_cnv, ld_c1, ld_out, ld_xv, ld_xk, ld_q2, ld_o2 = (sem("ld_cnv"), sem("ld_c1"), sem("ld_out"), sem("ld_xv"),
                                                            sem("ld_xk"), sem("ld_q2"), sem("ld_o2"))
        ld_bias, ld_end = sem("ld_bias"), sem("ld_end")
        pool_seq, pool_id, pool_cst, pool_moe = sem("pool_seq"), sem("pool_id"), sem("pool_cst"), sem("pool_moe")
        pool_bias = sem("pool_bias")
        dve_seq, act_seq = sem("dve_seq"), sem("act_seq")
        act_sqrt, dve_rstd, dve_norm = sem("act_sqrt"), sem("dve_rstd"), sem("dve_norm")
        pe_prm, dve_prm, dve_eps = sem("pe_prm"), sem("dve_prm"), sem("dve_eps")
        pe_tr, dve_tr = sem("pe_tr"), sem("dve_tr")
        dve_q = sem("dve_q")
        pe_row, dve_rope, act_rows = sem("pe_row"), sem("dve_rope"), sem("act_rows")
        dve_rem, act_trig = sem("dve_rem"), sem("act_trig")
        pe_cnv, act_ch, dve_cnv, dve_csq = sem("pe_cnv"), sem("act_ch"), sem("dve_cnv"), sem("dve_csq")
        pe_qkT, act_qkT = sem("pe_qkT"), sem("act_qkT")
        pe_cT, dve_blk = sem("pe_cT"), sem("dve_blk")
        pe_hid, act_hid, pe_hidT, dve_hx, act_hs, dve_hT = (sem("pe_hid"), sem("act_hid"), sem("pe_hidT"),
                                                           sem("dve_hx"), sem("act_hs"), sem("dve_hT"))
        pe_ckv, dve_ckv = sem("pe_ckv"), sem("dve_ckv")
        pe_cs, dve_cx, act_ce, dve_cp, pe_cpt, act_cpt = (sem("pe_cs"), sem("dve_cx"), sem("act_ce"),
                                                         sem("dve_cp"), sem("pe_cpt"), sem("act_cpt"))
        pe_kv, act_kv = sem("pe_kv"), sem("act_kv")
        pe_sc, dve_sx, act_e, dve_p, pe_pt, act_pt = (sem("pe_sc"), sem("dve_sx"), sem("act_e"), sem("dve_p"),
                                                     sem("pe_pt"), sem("act_pt"))
        dve_sm = sem("dve_sm")
        pe_pv, dve_o, act_osq, dve_osq = sem("pe_pv"), sem("dve_o"), sem("act_osq"), sem("dve_osq")
        pe_ss, act_sst, pe_mo, dve_h1 = sem("pe_ss"), sem("act_sst"), sem("pe_mo"), sem("dve_h1")
        pe_two, dve_two, act_two = sem("pe_two"), sem("dve_two"), sem("act_two")
        act_rt, dve_rt = sem("act_rt"), sem("dve_rt")
        pe_s2, dve_m2, act_e2, dve_sum2 = sem("pe_s2"), sem("dve_m2"), sem("act_e2"), sem("dve_sum2")
        pe_xo, dve_h2, act_xs = sem("pe_xo"), sem("dve_h2"), sem("act_xs")
        pe_lg, dve_ng, act_gx, dve_g, pe_cnt, dve_flg = (sem("pe_lg"), sem("dve_ng"), sem("act_gx"), sem("dve_g"),
                                                        sem("pe_cnt"), sem("dve_flg"))
        arrived = [sem(f"arrived{i}") for i in range(RING)]
        freed = sem("freed")
        m_seq = sem("m_seq")
        m_sel, m_selg, m_gath, m_xg = sem("m_sel"), sem("m_selg"), sem("m_gath"), sem("m_xg")
        m_bsel, m_bias = sem("m_bsel"), sem("m_bias")
        m_gcl, m_sg, m_h = sem("m_gcl"), sem("m_sg"), sem("m_h")
        m_tr, m_trD, m_trA, m_sgT, m_sgTc = sem("m_tr"), sem("m_trD"), sem("m_trA"), sem("m_sgT"), sem("m_sgTc")
        m_oA, m_oD, m_y, m_add = sem("m_oA"), sem("m_oD"), sem("m_y"), sem("m_add")
        f_go = sem("f_go")
        f_ss, f_root, f_rst, f_out, st_out = sem("f_ss"), sem("f_root"), sem("f_rst"), sem("f_out"), sem("st_out")

        x_v = x.rearrange("o (t p) n -> p (o t) n", p=P)
        mem_v = mem.rearrange("o (t p) n -> p (o t) n", p=P)
        out_v = out.rearrange("o (t p) n -> p (o t) n", p=P)

        KV_BANK = [7, 0, 3, 2, 3, 7, 2, 3]
        KV_AT = {1: 4, 3: 5, 4: 6, 6: 7}

        TWO = {x: n + 1 for n, x in enumerate([
            ("h1T", 0), ("h1T", 1), ("q", 0), ("qT", 0), ("q", 1), ("qT", 1), ("pT", 0), ("pT", 1),
            ("pv", 0), ("pv", 1), ("oT", 0), ("oT", 1), ("h2T", 0), ("h2T", 1)])}

        def chunked(w):
            return w.rearrange("(k p) n -> p k n", p=P)

        with nc.Block() as block:

            @block.sync
            def _(sp):
                for t in range(T):
                    sp.dma_start(H[:, t, :], x_v[:, t, :]).then_inc(ld_x, 16)
                rows = [(R_MIX, g_mix_norm[0]), (R_XA, g_xattn_norm[0]), (R_MEM, g_mem_norm[0]),
                        (R_MOE, g_moe_norm[0]), (R_CNV, g_conv_out[0]), (R_B1, cmp_b1_k[0]), (R_B1 + 2, cmp_b1_v[0])]
                for r, v in rows:
                    n = v.shape[0] // P
                    sp.dma_start(prm_rows[r:r + n, :], v.rearrange("(r n) -> r n", n=P)).then_inc(ld_prm, 16)
                for g in range(G):
                    sp.dma_start(prm_rows[R_NSA:R_NSA + J, g * HD:(g + 1) * HD],
                                  g_nsa_out[0, g * J * HD:(g + 1) * J * HD].rearrange("(j d) -> j d", j=J)
                                  ).then_inc(ld_prm, 16)
                sp.dma_start(prm_rows[R_CW:R_CW + 12, :], conv_w[0].rearrange("k (c n) -> (k c) n", n=P)
                              ).then_inc(ld_prm, 16)
                for v, w in enumerate((cmp_pos_k, cmp_pos_v)):
                    sp.dma_start(prm_rows[R_POS + 16 * v:R_POS + 16 * (v + 1), :],
                                  w[0].rearrange("(m i) d -> m (i d)", i=2)).then_inc(ld_prm, 16)
                for kc in range(KC):
                    sp.dma_start(w_row[:, kc, :], w_mix_in[0, kc * P:(kc + 1) * P, 0:ROWC]).then_inc(ld_row[kc], 16)
                for t in range(T):
                    sp.dma_start(MV[:, t, :], mem_v[:, t, :]).then_inc(ld_mem, 16)
                for kc in range(KC):
                    sp.dma_start(w_cnv[:, kc, :], w_mix_in[0, kc * P:(kc + 1) * P, ROWC:ROWC + 3 * CONVW]
                                 ).then_inc(ld_cnv, 16)
                for v, w in enumerate((cmp_w1_k, cmp_w1_v)):
                    sp.dma_start(w_c1[:, v, :, :], w[0].rearrange("(m p) n -> p m n", p=P)).then_inc(ld_c1, 16)
                sp.wait_ge(pe_cnv, CC)
                sp.dma_start(w_xv, chunked(w_xkv[0, :, D:2 * D])).then_inc(ld_xv, 16)
                sp.wait_ge(pe_hid, 1)
                sp.dma_start(w_a, chunked(w_xkv[0, :, 0:D])).then_inc(ld_xk, 16)
                nsa = w_mix_out[0, 0:NSA, :].rearrange("(g j d) n -> g j d n", g=G, j=J)
                for g in range(G):
                    for j in range(J):
                        sp.dma_start(w_out[g * HD:(g + 1) * HD, j, :], nsa[g, j]).then_inc(ld_out, 16)
                sp.dma_start(w_out[:, J:J + CC, :], chunked(w_mix_out[0, NSA:D, :])).then_inc(ld_out, 16)
                sp.wait_ge(pe_kv, 8)
                sp.dma_start(w_a, chunked(w_xq[0])).then_inc(ld_q2, 16)
                sp.wait_ge(pe_ss, 1)
                sp.wait_ge(pe_mo, T)
                sp.dma_start(w_o2, chunked(w_xo[0])).then_inc(ld_o2, 16)
                sp.wait_ge(pe_two, TWO["q", 1])
                for part in range(3):
                    sp.dma_start(A[part * E:(part + 1) * E, 0:2 * FF], b_gate_up[0]).then_inc(ld_bias, 16)
                    sp.dma_start(A[part * E:(part + 1) * E, 2 * FF:BW], b_down[0]).then_inc(ld_bias, 16)

                def fill(p, h, j):
                    slot = (FILLS * h + j) % RING
                    for side in range(2):
                        e = p * (2 * HALF) + (2 * h + side)
                        if j < KC:
                            src = w_gate_up[0, bass.ds(e, 1), j * P:(j + 1) * P, :].rearrange("o p n -> p (o n)")
                            dst = ring[slot][side]
                        else:
                            f = (j - KC) * 2 * P
                            src = w_down[0, bass.ds(e, 1), f:f + 2 * P, :].rearrange("o (c p) n -> p (o c) n", p=P)
                            dst = ring[slot][side].rearrange("p (c n) -> p c n", c=2)
                        sp.dma_start(dst, src).then_inc(arrived[slot], 16)

                for h in range(HALF):
                    for j in range(FILLS):
                        n = FILLS * h + j
                        if n == 4:
                            sp.wait_ge(pe_xo, 2 * T)
                        if n == 7:
                            sp.wait_ge(pe_lg, T)
                        if n >= RING:
                            sp.wait_ge(freed, n - RING + 1)
                        fill(0, h, j)
                with sp.Fori(1, PAIRS // HALF) as p:
                    for h in range(HALF):
                        for j in range(FILLS):
                            sp.wait_ge(freed, p * (HALF * FILLS) + (FILLS * h + j - RING + 1))
                            fill(p, h, j)
                sp.wait_ge(dve_flg, 1)
                with sp.Fori(1, ROUNDS) as r:
                    on = sp.value_load(flg[0:1, bass.ds(r, 1)], min_val=0, max_val=1)
                    with sp.If(on > 0):
                        with sp.Fori(0, PAIRS // HALF) as p:
                            for h in range(HALF):
                                for j in range(FILLS):
                                    sp.wait_ge(freed, r * (PAIRS * FILLS) + p * (HALF * FILLS) + (FILLS * h + j - RING + 1))
                                    fill(p, h, j)
                for t in range(T):
                    sp.wait_ge(f_out, t + 1)
                    sp.dma_start(out_v[:, t, :], H[:, t, :]).then_inc(st_out, 16)
                sp.wait_ge(st_out, 16 * T)

            @block.gpsimd
            def _(pool):
                link = links(pool, pool_seq)
                link(nc.gpsimd.memset(ident[:], 0.0))
                nc.gpsimd.affine_select(out=ident[:], in_=ident[:], compare_op=ALU.not_equal, fill=1.0, base=0,
                                        pattern=[[-1, P]], channel_multiplier=1).then_inc(pool_id, 1)
                nc.gpsimd.memset(ones[:], 1.0).then_inc(pool_cst, 1)
                link(nc.gpsimd.memset(mask[:], 0.0))
                nc.gpsimd.affine_select(out=mask[:], in_=mask[:], compare_op=ALU.is_ge, fill=NEG, base=P,
                                        pattern=[[-1, S]], channel_multiplier=1).then_inc(pool_cst, 1)
                link(nc.gpsimd.memset(cmask[:], 0.0))
                nc.gpsimd.affine_select(out=cmask[:], in_=cmask[:], compare_op=ALU.is_ge, fill=NEG,
                                        base=-(CLEN - 1), pattern=[[P, T], [-CSTR, NCMP]],
                                        channel_multiplier=1).then_inc(pool_cst, 1)
                link(nc.gpsimd.memset(valid[:], 1.0))
                nc.gpsimd.affine_select(out=valid[:], in_=valid[:], compare_op=ALU.is_ge, fill=0.0,
                                        base=-(CLEN - 1), pattern=[[P, T]], channel_multiplier=1).then_inc(pool_cst, 1)
                pool.wait_ge(pe_s2, T)
                link(nc.gpsimd.iota(iot, pattern=[[1, SLOTS]], base=0, channel_multiplier=0,
                               allow_small_or_imprecise_dtypes=True), pool_moe)
                for part in range(3):
                    link(nc.gpsimd.iota(mkf[part * E:(part + 1) * E, 1352:1352 + P].rearrange("p (s n) -> p s n", s=2),
                                   pattern=[[-1, 2], [0, SLOTS]], base=0, channel_multiplier=1,
                                   allow_small_or_imprecise_dtypes=True), pool_moe)
                link(nc.gpsimd.iota(lead[:, 0:ROUNDS * PAIRS], pattern=[[0, ROUNDS], [2, PAIRS]], base=0, channel_multiplier=0,
                               allow_small_or_imprecise_dtypes=True), pool_moe)
                link(nc.gpsimd.memset(lead[:, ROUNDS * PAIRS:ROUNDS * PAIRS + 1], 0.0), pool_moe)
                link(nc.gpsimd.memset(zer, 0.0), pool_moe)
                link(nc.gpsimd.iota(koff, pattern=[[-SLOTS, ROUNDS]], base=-1, channel_multiplier=0,
                                    allow_small_or_imprecise_dtypes=True), pool_moe)
                link(nc.gpsimd.memset(mkf[:, 0:520], -1.0), pool_moe)
                link(nc.gpsimd.memset(tri, 0.0))
                link(nc.gpsimd.affine_select(out=tri, in_=tri, compare_op=ALU.is_ge, fill=1.0, base=0,
                                             pattern=[[-1, P]], channel_multiplier=1), pool_moe)
                pool.wait_ge(ld_bias, 16 * 6)
                link(nc.gpsimd.tensor_copy(b_prt, b_raw))
                for part, src in ((1, b_raw), (2, b_res)):
                    for q in range(part * E, 96, E):
                        link(nc.gpsimd.tensor_tensor(b_res[q:q + E], src[q:q + E], b_prt[q:q + E], ALU.subtract))
                        link(nc.gpsimd.tensor_copy(b_prt[q:q + E], b_res[q:q + E]), pool_bias if part == 2 else None)

            @block.scalar
            def _(act):
                link = links(act, act_seq)
                def root(t, src, junk):
                    link(nc.scalar.activation(junk, src, ACT.Square, accum_out=ss[:, t:t + 1]))
                    return nc.scalar.activation(rst[:, t:t + 1], ss[:, t:t + 1], ACT.Sqrt, bias=eps[:], scale=1.0 / D)

                act.wait_ge(dve_eps, 1)
                act.wait_ge(ld_x, 32)
                for t in range(T):
                    root(t, H[:, t, :], XS[:, t, :]).then_inc(act_sqrt, 1)
                act.dma_start(pos_i[:], positions.rearrange("o (t p) -> p (o t)", p=P), allow_slow_non_contiguous=True).then_inc(ld_pos, 16)
                act.dma_start(invf[:], inv_freq.to_broadcast([P, 32])).then_inc(ld_pos, 16)
                act.dma_start(b_rt[:], b_router.to_broadcast([P, E])).then_inc(ld_misc, 16)
                act.dma_start(w_rt[:], chunked(w_router[0])).then_inc(ld_misc, 16)
                for v, w in enumerate((cmp_w2_k, cmp_w2_v)):
                    act.dma_start(w_c2[:, v, :, :], w[0].rearrange("(c p) n -> p c n", p=P)).then_inc(ld_misc, 16)
                act.wait_ge(dve_rem, 1)
                nc.scalar.activation(trig[:].rearrange("p a t n -> p (a t n)"), rem[:].rearrange("p a t n -> p (a t n)"),
                                     ACT.Sin).then_inc(act_trig, 1)
                act.wait_ge(dve_norm, 2)
                act.wait_ge(ld_mem, 32)
                for t in range(T):
                    root(t, MV[:, t, :], mkf[:, t * D:(t + 1) * D]).then_inc(act_sqrt, 1)
                for t in range(T):
                    act.wait_ge(pe_row, t + 1)
                    if t == 1:
                        act.wait_ge(dve_rope, 1)
                    pr = bank(4, 3)
                    nc.scalar.copy(kraw, pr[:, NSA:NSA + 768].rearrange("p (k n) -> p k n", k=3)[:, :, 0:P]).then_inc(act_rows, 1)
                    nc.scalar.copy(vrow[:, t, :, :],
                                   pr[:, 640:1408].rearrange("p (k n) -> p k n", k=3)[:, :, 0:P]).then_inc(act_rows, 1)
                    nc.scalar.activation(gates[:, t, :], pr[:, 1280:ROWC], ACT.Sigmoid).then_inc(act_rows, 1)

                def conv_h(i):
                    act.wait_ge(pe_cnv, i + 1)
                    if i >= 2:
                        act.wait_ge(dve_cnv, i - 1)
                    nc.scalar.copy(ch_sb[:, i % 2, :], bank(2 * (i % 2))[:, 0:S]).then_inc(act_ch, 1)

                for i in range(CC - 1):
                    conv_h(i)
                act.wait_ge(pe_qkT, 1)
                nc.scalar.copy(qT[:, 0:2, :].rearrange("p a n -> p (a n)"), bank(4)).then_inc(act_qkT, 1)
                nc.scalar.copy(qT[:, 2:4, :].rearrange("p a n -> p (a n)"), bank(5)).then_inc(act_qkT, 1)
                nc.scalar.copy(kT.rearrange("p a n -> p (a n)"), bank(6)).then_inc(act_qkT, 1)
                conv_h(CC - 1)

                def kv_out(i):
                    act.wait_ge(pe_kv, i + 1)
                    dst = MV[:, i // 2, (i % 2) * BANK:(i % 2 + 1) * BANK] if i < 4 else mkf[:, (i - 4) * BANK:(i - 3) * BANK]
                    nc.scalar.copy(dst, bank(KV_BANK[i])).then_inc(act_kv, 1)

                act.wait_ge(pe_hid, 1)
                for v in range(2):
                    nc.scalar.copy(hid[32 * v:32 * v + 2 * NCMP, :], bank(1 + v)[32 * v:32 * v + 2 * NCMP, 0:CHID]
                                   ).then_inc(act_hid, 1)
                kv_out(0)
                act.wait_ge(dve_hx, 1)
                nc.scalar.activation(hy, hy, ACT.Sigmoid, scale=2.0 * 0.7978845608028654).then_inc(act_hs, 1)
                kv_out(1)
                kv_out(2)
                act.wait_ge(dve_cx, 1)
                nc.scalar.activation(Pcf, Pcf, ACT.Exp).then_inc(act_ce, 1)

                def exps(n):
                    t = n // J
                    nk = P * (t + 1)
                    act.wait_ge(dve_sx, n + 1)
                    for g in range(G):
                        for k in range(2):
                            nc.scalar.activation(Pb[:, n % 2, g, k, 0:nk], Pb[:, n % 2, g, k, 0:nk], ACT.Exp,
                                                 bias=nmx[:, n % 2, 2 * g + k:2 * g + k + 1],
                                                 accum_out=smx[:, n % 2, 2 * g + k:2 * g + k + 1]).then_inc(act_e, 1)

                def pt_out(n):
                    t, j = n // J, n % J
                    act.wait_ge(pe_pt, n + 1)
                    if t == 1:
                        act.wait_ge(pe_pv, 1)
                    for g in range(G):
                        nb = 2 * (t + 1)
                        nc.scalar.copy(PT[g][:, 0:nb, j, :], bank(4 + g)[:, 0:nb * P].rearrange("p (b n) -> p b n", b=nb)
                                       ).then_inc(act_pt, 1)

                exps(0)
                kv_out(3)
                for i in range(4):
                    act.wait_ge(pe_cpt, 1)
                    nc.scalar.copy(PTc[:, i % 2, i // 2, :], bank(4 + i)[0:NCMP, :]).then_inc(act_cpt, 1)

                def o_squares(t):
                    act.wait_ge(dve_o, t + 1)
                    act.wait_ge(pe_pv, T)
                    nc.scalar.activation(sqn[:, t].rearrange("p j n -> p (j n)"), bank(6 if t == 0 else 7), ACT.Square
                                         ).then_inc(act_osq, 1)

                for n in range(T * J):
                    if n >= 1:
                        exps(n)
                        pt_out(n - 1)
                    if n in KV_AT:
                        kv_out(KV_AT[n])
                pt_out(T * J - 1)
                for t in range(T):
                    o_squares(t)
                act.wait_ge(pe_ss, 1)
                nc.scalar.activation(gsr[:], bank(4)[:, 0:4], ACT.Sqrt, bias=eps[:], scale=1.0 / NSA).then_inc(act_sst, 1)

                def second(what, t, b, dst, scale=None):
                    act.wait_ge(pe_two, TWO[what, t])
                    nc.scalar.activation(dst, bank(b), ACT.Copy, scale=1.0 if scale is None else scale).then_inc(act_two, 1)

                def second_gain(what, t, row):
                    act.wait_ge(pe_two, TWO[what, t])
                    for c in range(4, KC):
                        ins = nc.scalar.activation(XT[:, c, t * P:(t + 1) * P], bank(4 * t + 1)[:, (c - 4) * P:(c - 3) * P],
                                                   ACT.Copy, scale=prm[:, row + c:row + c + 1])
                    ins.then_inc(act_two, 1)

                def qo_second(t):
                    return qo2[:, t, 4:8, :].rearrange("p c n -> p (c n)")

                for t in range(T):
                    act.wait_ge(dve_h1, t + 1)
                    root(t, H[:, t, :], XS[:, t, :]).then_inc(act_rt, 1)
                    second_gain("h1T", t, R_XA)
                act.wait_ge(dve_rt, 1)
                second("q", 0, 3, XS[:, 0, BANK:D], rst[:, 0:1])
                second("qT", 0, 1, qo_second(0))
                act.wait_ge(dve_rt, 2)
                second("q", 1, 7, XS[:, 1, BANK:D], rst[:, 1:2])

                def exps2(t):
                    act.wait_ge(dve_m2, t + 1)
                    act.wait_ge(pe_two, TWO["qT", t])
                    for h in range(XH):
                        nc.scalar.activation(P2[:, t, h, :], bank(4 * t + 2, 2)[:, h * S:(h + 1) * S], ACT.Exp,
                                             bias=cnm[:, XH * t + h:XH * t + h + 1], scale=XD ** -0.5,
                                             accum_out=csm[:, XH * t + h:XH * t + h + 1]).then_inc(act_e2, 1)

                second("qT", 1, 5, qo_second(1))
                exps2(0)
                exps2(1)
                second("pT", 0, 1, P2T[:, 0, 2:4].rearrange("p h m n -> p (h m n)"))
                second("pT", 1, 5, P2T[:, 1, 2:4].rearrange("p h m n -> p (h m n)"))
                for t in range(T):
                    act.wait_ge(pe_two, TWO["pv", t])
                    act.wait_ge(dve_sum2, t + 1)
                    for h in (2, 3):
                        ins = nc.scalar.activation(XS[:, t, h * XD:(h + 1) * XD], bank(4 * t + 3)[:, (h - 2) * XD:(h - 1) * XD],
                                                   ACT.Copy, scale=csm[:, XH * t + h:XH * t + h + 1])
                    ins.then_inc(act_two, 1)
                for t in range(T):
                    second("oT", t, 4 * t + 1, qo_second(t))
                act.wait_ge(pe_two, TWO["pv", 1])
                act.dma_start(gfin, g_final.rearrange("(a n) -> a n", a=1).to_broadcast([P, D])).then_inc(ld_end, 16)
                for t in range(T):
                    act.wait_ge(dve_h2, 2 * t + 2)
                    act.wait_ge(pe_two, TWO["oT", t])
                    root(t, H[:, t, :], XS[:, t, :]).then_inc(act_rt, 1)
                    second_gain("h2T", t, R_MOE)
                    act.wait_ge(dve_rt, T + t + 1)
                    nc.scalar.activation(XS[:, t, :], H[:, t, :], ACT.Copy, scale=rst[:, t:t + 1]).then_inc(act_xs, 1)
                for t in range(T):
                    act.wait_ge(dve_ng, t + 1)
                    nc.scalar.activation(gex[:, t, :], lg[:, t, :], ACT.Exp, bias=gneg[:, t:t + 1]).then_inc(act_gx, 1)

                act.wait_ge(dve_flg, 1)
                with act.Fori(0, ROUNDS) as r:
                    on = act.value_load(flg[0:1, bass.ds(r, 1)], min_val=0, max_val=1)
                    with act.If(on > 0):
                        with act.Fori(0, PAIRS // HALF) as p:
                            for h in range(HALF):
                                k = r * PAIRS + p * HALF + h
                                act.wait_ge(m_gcl, k + 1)
                                nc.scalar.activation(sgm, gcl, ACT.Sigmoid, scale=ALPHA).then_inc(m_sg, 1)
                                act.wait_ge(m_tr, k + 1)
                                nc.scalar.copy(hTm[:, 4:8, :].rearrange("p k n -> p (k n)"), bank(5)).then_inc(m_trA, 1)
                                act.wait_ge(freed, k * FILLS + FILLS)
                                nc.scalar.copy(orow[:, BANK:D], bank(5)).then_inc(m_oA, 1)
                act.wait_ge(f_go, 1)
                for t in range(T):
                    link(nc.scalar.activation(XS[:, t, :], H[:, t, :], ACT.Square, accum_out=ss[:, t:t + 1]), f_ss)
                    nc.scalar.activation(rst[:, t:t + 1], ss[:, t:t + 1], ACT.Sqrt, bias=eps[:], scale=1.0 / D
                                         ).then_inc(f_root, 1)

            @block.vector
            def _(dve):
                V = nc.vector
                link = links(dve, dve_seq)
                V.memset(eps[:], EPS).then_inc(dve_eps, 1)

                def tr_out(i, dst, b0, row):
                    for b in range(4):
                        dve.wait_ge(pe_tr, 4 * i + b + 1)
                        V.tensor_tensor(dst[:, 2 * b:2 * b + 2, :], bank(b0 + b).rearrange("p (a n) -> p a n", a=2),
                                        prm[:, row + 2 * b:row + 2 * b + 2].unsqueeze(2).to_broadcast([P, 2, S]),
                                        ALU.mult).then_inc(dve_tr, 1)

                def norm(src, dst, i):
                    for t in range(T):
                        dve.wait_ge(act_sqrt, T * i + t + 1)
                        link(V.reciprocal(rst[:, t:t + 1], rst[:, t:t + 1]), dve_rstd)
                        link(V.tensor_scalar(dst[:, t, :], src[:, t, :], rst[:, t:t + 1], None, ALU.mult), dve_norm)

                norm(H, XS, 0)
                dve.wait_ge(pe_prm, 1)
                link(V.tensor_copy(prm[:], bank(7)[:, 0:R_END]), dve_prm)
                tr_out(0, XT, 0, R_MIX)
                dve.wait_ge(ld_pos, 32)
                link(V.tensor_copy(pos_f[:], pos_i[:]))
                for t in range(T):
                    link(V.tensor_scalar(ang[:, t, :], invf[:], pos_f[:, t:t + 1], None, ALU.mult))
                big = 12582912.0
                link(V.tensor_scalar(turn[:], ang[:], 0.15915494309189535, None, ALU.mult))
                link(V.tensor_scalar(turn[:], turn[:], big, None, ALU.add))
                link(V.tensor_scalar(turn[:], turn[:], big, None, ALU.subtract))
                c1, c2 = 6.28125, 0.0019350051879882812
                c3 = 2.0 * np.pi - c1 - c2
                for c in (c1, c2, c3):
                    link(V.scalar_tensor_tensor(ang[:].rearrange("p t n -> p (t n)"), turn[:].rearrange("p t n -> p (t n)"),
                                                -float(c), ang[:].rearrange("p t n -> p (t n)"), ALU.mult, ALU.add))
                pi = 3.1415925
                link(V.tensor_scalar(rem[:, 0], ang[:], pi, -pi, ALU.min, ALU.max))
                link(V.tensor_scalar(ang[:], ang[:], float(np.pi / 2), None, ALU.add))
                link(V.tensor_scalar(turn[:], ang[:], pi, 2.0 * float(np.pi), ALU.is_gt, ALU.mult))
                link(V.tensor_tensor(ang[:], ang[:], turn[:], ALU.subtract))
                link(V.tensor_scalar(rem[:, 1], ang[:], pi, -pi, ALU.min, ALU.max), dve_rem)
                norm(MV, MV, 1)
                dve.wait_ge(act_trig, 1)

                def rope(a1, a2, o1, o2, t, n, shape, sem_last):
                    sin, cos = trig[:, 0, t, :], trig[:, 1, t, :]
                    def bc(w):
                        return w.unsqueeze(1).unsqueeze(1).to_broadcast([P] + shape + [32])
                    def tmp(b):
                        return b[:, 0:n].rearrange("p (a b d) -> p a b d", a=shape[0], b=shape[1])
                    V.tensor_tensor(tmp(ra), a1, bc(cos), ALU.mult)
                    link(V.tensor_tensor(tmp(rb), a2, bc(sin), ALU.mult))
                    link(V.tensor_tensor(o1, tmp(ra), tmp(rb), ALU.subtract))
                    V.tensor_tensor(tmp(ra), a2, bc(cos), ALU.mult)
                    link(V.tensor_tensor(tmp(rb), a1, bc(sin), ALU.mult))
                    link(V.tensor_tensor(o2, tmp(ra), tmp(rb), ALU.add), sem_last)

                for t in range(T):
                    if t == 1:
                        tr_out(1, MT, 0, R_MEM)
                    dve.wait_ge(pe_row, t + 1)
                    pr = bank(4, 3)
                    q4 = pr[:, 0:NSA].rearrange("p (g j d) -> p g j d", g=G, j=J)
                    o4 = qrot[:, t, :].rearrange("p (j g d) -> p g j d", g=G, j=J)
                    rope(q4[:, :, :, 0:32], q4[:, :, :, 32:64], o4[:, :, :, 0:32], o4[:, :, :, 32:64], t, 256, [G, J], dve_q)
                    dve.wait_ge(act_rows, 3 * t + 1)
                    k4 = kraw.rearrange("p k (g d) -> p k g d", g=G)
                    r4 = krot[:, t, :, :].rearrange("p k (g d) -> p k g d", g=G)
                    rope(k4[:, :, :, 0:32], k4[:, :, :, 32:64], r4[:, :, :, 0:32], r4[:, :, :, 32:64], t, 192, [3, G], dve_rope)

                link(V.memset(u_pad[:, 0:2], 0.0))
                def conv(i):
                    dve.wait_ge(act_ch, i + 1)
                    b0 = 2 * (i % 2)
                    link(V.tensor_tensor(u_pad[:, 2:S + 2], bank(b0)[:, S:2 * S], ch_sb[:, i % 2, :], ALU.mult))
                    tap = [prm[:, R_CW + 4 * w + i:R_CW + 4 * w + i + 1] for w in range(3)]
                    link(V.tensor_scalar(cy, u_pad[:, 0:S], tap[0], None, ALU.mult))
                    link(V.scalar_tensor_tensor(cy2, u_pad[:, 1:S + 1], tap[1], cy, ALU.mult, ALU.add))
                    link(V.scalar_tensor_tensor(cy, u_pad[:, 2:S + 2], tap[2], cy2, ALU.mult, ALU.add))
                    link(V.tensor_tensor(convT[:, i, :], bank(b0 + 1)[:, 0:S], cy, ALU.mult), dve_cnv)

                def conv_end():
                    sqc = xsf[:, 0:1024].rearrange("p (c n) -> p c n", c=CC)
                    link(V.tensor_tensor(sqc, convT[:], convT[:], ALU.mult))
                    link(V.tensor_reduce(sqs[:, 1, :], sqc.rearrange("p c n -> p n c"), AX, ALU.add))
                    link(V.tensor_tensor(convT[:], convT[:], prm[:, R_CNV:R_CNV + CC].unsqueeze(2).to_broadcast([P, CC, S]),
                                         ALU.mult), dve_csq)

                for i in range(CC - 1):
                    conv(i)
                for v in range(2):
                    dve.wait_ge(pe_cT, v + 1)
                    for i in range(2):
                        src = (bank(7) if v == 0 else bank(0))[i * HD:(i + 1) * HD, :].rearrange(
                            "p (g c m i) -> p g c m i", g=G, m=8, i=2)
                        for mh in range(2):
                            for g in range(G):
                                link(V.tensor_tensor(
                                    blk[i * HD:(i + 1) * HD, v, 8 * mh:8 * mh + 8, g, :].rearrange("p m c -> p c m"),
                                    src[:, g, mh:mh + NCMP, :, i],
                                    prm[i * HD:(i + 1) * HD, R_POS + 16 * v + 8 * mh:R_POS + 16 * v + 8 * mh + 8
                                        ].unsqueeze(1).to_broadcast([HD, NCMP, 8]), ALU.add), dve_blk)
                conv(CC - 1)

                dve.wait_ge(pe_hidT, 1)
                for v in range(2):
                    link(V.tensor_tensor(hx[:, 60 * v:60 * v + 60].rearrange("p (a n) -> p a n", a=2),
                                         bank(3 - 2 * v)[:, 0:60].rearrange("p (a n) -> p a n", a=2),
                                         prm[:, R_B1 + 2 * v:R_B1 + 2 * v + 2].unsqueeze(2).to_broadcast([P, 2, 2 * NCMP]),
                                         ALU.add))
                link(V.tensor_tensor(hy, hx, hx, ALU.mult))
                link(V.tensor_scalar(hy, hy, 0.044715, 1.0, ALU.mult, ALU.add))
                link(V.tensor_tensor(hy, hy, hx, ALU.mult), dve_hx)
                dve.wait_ge(act_hs, 1)
                link(V.tensor_tensor(hTf, hx, hy, ALU.mult), dve_hT)
                conv_end()
                dve.wait_ge(pe_ckv, 1)
                link(V.tensor_copy(kcT[:], bank(2)[:, 0:NCMP]), dve_ckv)
                link(V.tensor_copy(vc[:].rearrange("p g d -> p (g d)"), bank(2)[0:NCMP, 128:256]), dve_ckv)

                dve.wait_ge(pe_cs, 1)
                dve.wait_ge(pool_cst, 4)
                for g in range(G):
                    for t in range(T):
                        link(V.scalar_tensor_tensor(Pc[:, g, t], bank(4 + g)[:, t * 60:t * 60 + 60].rearrange(
                            "p (j c) -> p j c", j=J), HD ** -0.5,
                            cmask[:, t, :].unsqueeze(1).to_broadcast([P, J, NCMP]), ALU.mult, ALU.add))
                pc16 = Pcf.rearrange("p (a c) -> p a c", c=NCMP)
                link(V.tensor_reduce(cnm[:], pc16, AX, ALU.max))
                link(V.tensor_tensor(pc16, pc16, cnm[:].unsqueeze(2).to_broadcast([P, 16, NCMP]), ALU.subtract), dve_cx)
                dve.wait_ge(act_ce, 1)
                link(V.tensor_reduce(csm[:], pc16, AX, ALU.add))
                link(V.reciprocal(csm[:], csm[:]))
                c4 = csm[:].rearrange("p (g t j) -> p g t j", g=G, t=T)
                for t in range(T):
                    gt0 = gates[:, t, :].rearrange("p (g j b) -> p g j b", g=G, j=J)[:, :, :, 0]
                    link(V.tensor_tensor(c4[:, :, t, :], c4[:, :, t, :], gt0, ALU.mult))
                    link(V.tensor_scalar(c4[:, :, t, :], c4[:, :, t, :], valid[:, t:t + 1], None, ALU.mult))
                link(V.tensor_tensor(pc16, pc16, csm[:].unsqueeze(2).to_broadcast([P, 16, NCMP]), ALU.mult), dve_cp)

                def mask_max(n):
                    t, b = n // J, n % 2
                    nk = P * (t + 1)
                    dve.wait_ge(pe_sc, n + 1)
                    if n >= 2:
                        dve.wait_ge(pe_pt, n - 1)
                    sc = bank(0, 2).rearrange("p (a n) -> p a n", a=4)[:, :, 0:nk]
                    pb = Pb[:, b].rearrange("p g k n -> p (g k) n")[:, :, 0:nk]
                    mk = mask[:, S - nk:S].unsqueeze(1).to_broadcast([P, 4, nk])
                    link(V.scalar_tensor_tensor(pb, sc, HD ** -0.5, mk, ALU.mult, ALU.add), dve_sm)
                    link(V.tensor_reduce(nmx[:, b, :], pb, AX, ALU.max, negate=True), dve_sx)

                def weigh(n):
                    t, j, b = n // J, n % J, n % 2
                    nk = P * (t + 1)
                    dve.wait_ge(act_e, 4 * (n + 1))
                    link(V.reciprocal(cof[:, b, :], smx[:, b, :]))
                    gt2 = gates[:, t, :].rearrange("p (g j b) -> p g j b", g=G, j=J)[:, :, j, 1:3]
                    c2 = cof[:, b, :].rearrange("p (g k) -> p g k", g=G)
                    link(V.tensor_tensor(c2, c2, gt2, ALU.mult))
                    pb = Pb[:, b].rearrange("p g k n -> p (g k) n")[:, :, 0:nk]
                    link(V.tensor_tensor(pb, pb, cof[:, b, :].unsqueeze(2).to_broadcast([P, 4, nk]), ALU.mult), dve_p)

                def o_out(t):
                    dve.wait_ge(pe_pv, t + 1)
                    link(V.tensor_tensor(oT[:, :, t * P:(t + 1) * P], bank(6 if t == 0 else 7).rearrange("p (j n) -> p j n", j=J),
                                         prm[:, R_NSA:R_NSA + J].unsqueeze(2).to_broadcast([P, J, P]), ALU.mult), dve_o)

                for n in range(T * J):
                    mask_max(n)
                    if n >= 1:
                        weigh(n - 1)
                    if n == J + 1:
                        o_out(0)
                weigh(T * J - 1)
                o_out(1)
                dve.wait_ge(act_osq, T)
                link(V.tensor_reduce(sqs[:, 0, :].rearrange("p (t n) -> p t n", t=T), sqn.rearrange("p t j n -> p t n j"),
                                     AX, ALU.add), dve_osq)
                dve.wait_ge(act_sst, 1)
                link(V.reciprocal(gsr[:], gsr[:]))

                def first_gain(what, t, row):
                    dve.wait_ge(pe_two, TWO[what, t])
                    V.tensor_tensor(XT[:, 0:4, t * P:(t + 1) * P], bank(4 * t).rearrange("p (c n) -> p c n", c=4),
                                    prm[:, row:row + 4].unsqueeze(2).to_broadcast([P, 4, P]), ALU.mult).then_inc(dve_two, 1)

                def first(what, t, b, dst):
                    dve.wait_ge(pe_two, TWO[what, t])
                    V.tensor_copy(dst, bank(b)).then_inc(dve_two, 1)

                def reciprocal_root(t, i):
                    dve.wait_ge(act_rt, T * i + t + 1)
                    link(V.reciprocal(rst[:, t:t + 1], rst[:, t:t + 1]), dve_rt)

                def qo_first(t):
                    return qo2[:, t, 0:4, :].rearrange("p c n -> p (c n)")

                def q_rows(t):
                    dve.wait_ge(pe_two, TWO["q", t])
                    V.tensor_scalar(XS[:, t, 0:BANK], bank(4 * t + 2), rst[:, t:t + 1], None, ALU.mult).then_inc(dve_two, 1)

                def max2(t):
                    dve.wait_ge(pe_s2, t + 1)
                    c = slice(XH * t, XH * (t + 1))
                    link(V.tensor_reduce(cnm[:, c], bank(4 * t + 2, 2).rearrange("p (h n) -> p h n", h=XH), AX, ALU.max,
                                         negate=True))
                    link(V.tensor_scalar(cnm[:, c], cnm[:, c], XD ** -0.5, None, ALU.mult), dve_m2)

                for t in range(T):
                    dve.wait_ge(pe_mo, t + 1)
                    for part in range(2):
                        link(V.scalar_tensor_tensor(H[:, t, :], bank(4 * t + 2 * part, 2), gsr[:, 2 * t + part:2 * t + part + 1],
                                                    H[:, t, :], ALU.mult, ALU.add), dve_h1 if part == 1 else None)
                    first_gain("h1T", t, R_XA)
                    reciprocal_root(t, 0)
                q_rows(0)
                first("qT", 0, 0, qo_first(0))
                q_rows(1)
                max2(0)
                first("qT", 1, 4, qo_first(1))
                max2(1)
                first("pT", 0, 0, P2T[:, 0, 0:2].rearrange("p h m n -> p (h m n)"))
                first("pT", 1, 4, P2T[:, 1, 0:2].rearrange("p h m n -> p (h m n)"))
                for t in range(T):
                    dve.wait_ge(act_e2, XH * (t + 1))
                    c = slice(XH * t, XH * (t + 1))
                    link(V.reciprocal(csm[:, c], csm[:, c]), dve_sum2)
                    dve.wait_ge(pe_two, TWO["pv", t])
                    V.tensor_tensor(XS[:, t, 0:BANK].rearrange("p (h n) -> p h n", h=2),
                                    bank(4 * t + 2).rearrange("p (h n) -> p h n", h=2),
                                    csm[:, XH * t:XH * t + 2].unsqueeze(2).to_broadcast([P, 2, XD]), ALU.mult
                                    ).then_inc(dve_two, 1)
                for t in range(T):
                    first("oT", t, 4 * t, qo_first(t))
                for t in range(T):
                    for n in range(2):
                        dve.wait_ge(pe_xo, 2 * t + n + 1)
                        hn = H[:, t, n * BANK:(n + 1) * BANK]
                        link(V.tensor_tensor(hn, hn, bank(4 * t + 2 + n), ALU.add), dve_h2)
                    first_gain("h2T", t, R_MOE)
                    reciprocal_root(t, 1)

                dve.wait_ge(pool_moe, 10)
                dve.wait_ge(ld_misc, 64)
                for t in range(T):
                    dve.wait_ge(pe_lg, t + 1)
                    link(V.scalar_tensor_tensor(lg[:, t, :], bank(4 * t + 2)[:, 0:E], rst[:, t:t + 1], b_rt[:], ALU.mult, ALU.add))
                    link(V.max(top[:, t, :], lg[:, t, :]))
                    link(V.tensor_scalar(gneg[:, t:t + 1], top[:, t, 0:1], -1.0, None, ALU.mult), dve_ng)
                    fourth = top[:, t, 3:4]
                    V.tensor_scalar(gt[:, t, :], lg[:, t, :], fourth, None, ALU.is_gt)
                    link(V.tensor_scalar(eq[:, t, :], lg[:, t, :], fourth, None, ALU.is_equal))
                    link(V.tensor_tensor_scan(cum[:, t, :], eq[:, t, :], zer, 0.0, ALU.add, ALU.add))
                link(V.tensor_reduce(need, gt, AX, ALU.add))
                link(V.tensor_scalar(need, need, -1.0, 4.0, ALU.mult, ALU.add))
                for t in range(T):
                    link(V.tensor_scalar(cum[:, t, :], cum[:, t, :], need[:, t:t + 1], None, ALU.is_le))
                link(V.tensor_tensor(eq, eq, cum, ALU.mult))
                link(V.tensor_tensor(gt, gt, eq, ALU.add), dve_g)
                dve.wait_ge(act_gx, 2)
                link(V.tensor_tensor(gex, gex, gt, ALU.mult))
                link(V.tensor_reduce(gsum, gex, AX, ALU.add))
                link(V.reciprocal(gsum, gsum))
                for t in range(T):
                    link(V.tensor_scalar(gtab[:, t, 0:ROW].rearrange("p (r e) -> p r e", r=ROUNDS),
                                         gex[:, t, :].unsqueeze(1).to_broadcast([P, ROUNDS, E]), gsum[:, t:t + 1], None, ALU.mult))
                dve.wait_ge(pe_cnt, 1)
                for t in range(T):
                    place = bank(3)[:, t * E:(t + 1) * E]
                    link(V.scalar_tensor_tensor(lg[:, t, :], place, 1.0, gt[:, t, :], ALU.add, ALU.mult))
                    link(V.tensor_tensor(keys[:, t, 0:ROW].rearrange("p (r e) -> p r e", r=ROUNDS),
                                         lg[:, t, :].unsqueeze(1).to_broadcast([P, ROUNDS, E]),
                                         koff.unsqueeze(2).to_broadcast([P, ROUNDS, E]), ALU.add))
                link(V.tensor_reduce(cmx, bank(3)[0:1, 2 * E:3 * E], AX, ALU.max))
                for r in range(ROUNDS):
                    link(V.tensor_scalar(flg[0:1, r:r + 1], cmx, float(SLOTS * r), None, ALU.is_gt),
                         dve_flg if r == ROUNDS - 1 else None)
                def build_sel(c):
                    for t in range(T):
                        yield V.tensor_tensor(sel1[:, t, :].rearrange("p (s n) -> p s n", s=2),
                                              iot.unsqueeze(1).to_broadcast([P, 2, SLOTS]),
                                              keys[:, t, bass.ds(c, 2)].unsqueeze(2).to_broadcast([P, 2, SLOTS]),
                                              ALU.is_equal)

                def build_selg(c):
                    for t in range(T):
                        yield V.tensor_tensor(selg[:, t, :].rearrange("p (s n) -> p s n", s=2),
                                              sel1[:, t, :].rearrange("p (s n) -> p s n", s=2),
                                              gtab[:, t, bass.ds(c, 2)].unsqueeze(2).to_broadcast([P, 2, SLOTS]),
                                              ALU.mult)

                def build_bsel(i):
                    return V.tensor_tensor(bsel, bdiff, lead[:, bass.ds(i, 1)].to_broadcast([96, P]), ALU.is_equal)

                def xg_out():
                    return V.tensor_tensor(xgT, bank(6, 2).rearrange("p (k n) -> p k n", k=KC),
                                           prm[:, R_MOE:R_MOE + KC].unsqueeze(2).to_broadcast([P, KC, P]), ALU.mult)

                for ins in build_sel(0):
                    link(ins, m_sel)
                for ins in build_selg(0):
                    link(ins, m_selg)
                link(build_bsel(0), m_bsel)
                link(V.memset(cmx, 0.0), m_add)
                dve.wait_ge(pool_bias, 1)
                dve.wait_ge(m_gath, 1)
                link(xg_out(), m_xg)
                with dve.Fori(0, ROUNDS) as r:
                    on = dve.value_load(flg[0:1, bass.ds(r, 1)], min_val=0, max_val=1)
                    with dve.If(on > 0):
                        with dve.Fori(0, PAIRS // HALF) as p:
                            for h in range(HALF):
                                k = r * PAIRS + p * HALF + h
                                dve.wait_ge(m_gath, k + 1)
                                dve.wait_ge(m_selg, 2 * k + 2)
                                for ins in build_sel(k * 2 + 2):
                                    ins.then_inc(m_sel, 1)
                                dve.wait_ge(freed, k * FILLS + KC)
                                V.tensor_scalar(gcl, bank(0, 2), LIM, None, ALU.min).then_inc(m_gcl, 1)
                                V.tensor_scalar(ucl, bank(2, 2), LIM, -LIM, ALU.min, ALU.max).then_inc(m_seq, 1)
                                dve.wait_ge(m_gcl, k + 1)
                                dve.wait_ge(m_seq, k * 2 + 1)
                                V.scalar_tensor_tensor(ucl, ucl, 1.0, gcl, ALU.add, ALU.mult).then_inc(m_seq, 1)
                                dve.wait_ge(m_seq, k * 2 + 2)
                                dve.wait_ge(m_sg, k + 1)
                                V.tensor_tensor(ucl, ucl, sgm, ALU.mult).then_inc(m_h, 1)
                                dve.wait_ge(m_gath, k + 2)
                                xg_out().then_inc(m_xg, 1)
                                dve.wait_ge(m_tr, k + 1)
                                V.tensor_copy(hTm[:, 0:4, :].rearrange("p k n -> p (k n)"), bank(4)).then_inc(m_trD, 1)
                                dve.wait_ge(m_sgT, k + 1)
                                V.tensor_copy(selgT.rearrange("p t n -> p (t n)"), bank(6)[:, 0:S]).then_inc(m_sgTc, 1)
                                dve.wait_ge(freed, k * FILLS + FILLS)
                                V.tensor_copy(orow[:, 0:BANK], bank(4)).then_inc(m_oD, 1)
                                dve.wait_ge(m_bias, k + 1)
                                build_bsel(k + 1).then_inc(m_bsel, 1)
                                dve.wait_ge(m_sel, 2 * k + 4)
                                for ins in build_selg(k * 2 + 2):
                                    ins.then_inc(m_selg, 1)
                                for q in range(4):
                                    t, n = q // 2, q % 2
                                    hh = H[:, t, n * BANK:(n + 1) * BANK]
                                    dve.wait_ge(m_y, k * 4 + q + 1)
                                    V.tensor_tensor(hh, hh, bank(6 + n), ALU.add).then_inc(m_add, 1)
                                dve.wait_ge(m_add, k * 4 + 5)
                V.memset(cmx, 0.0).then_inc(f_go, 1)
                dve.wait_ge(ld_end, 16)
                for t in range(T):
                    dve.wait_ge(f_root, t + 1)
                    link(V.reciprocal(rst[:, t:t + 1], rst[:, t:t + 1]), f_rst)
                    V.scalar_tensor_tensor(H[:, t, :], H[:, t, :], rst[:, t:t + 1], gfin, ALU.mult, ALU.mult
                                           ).then_inc(f_out, 1)

            @block.tensor
            def _(pe):
                mm = nc.tensor.matmul

                def tr(dst, src):
                    k = src.shape[0]
                    return nc.tensor.transpose(dst, src, ident[0:k, 0:k])

                def transpose_rows(i, src, b0):
                    pe.wait_ge(dve_norm, 2 * (i + 1))
                    for b in range(4):
                        for a in range(2):
                            for t in range(T):
                                c = 2 * b + a
                                last = tr(bank(b0 + b)[:, a * S + t * P:a * S + (t + 1) * P], src[:, t, c * P:(c + 1) * P])
                        last.then_inc(pe_tr, 1)

                pe.wait_ge(pool_id, 1)
                pe.wait_ge(ld_prm, 16 * 12)
                tr(bank(7)[:, 0:R_END], prm_rows[:]).then_inc(pe_prm, 1)
                transpose_rows(0, XS, 0)

                def rows(t):
                    for kc in range(KC):
                        pe.wait_ge(ld_row[kc], 16)
                        for n, w in ((0, BANK), (1, BANK), (2, ROWC - 2 * BANK)):
                            last = mm(bank(4 + n)[:, 0:w], XT[:, kc, t * P:(t + 1) * P], w_row[:, kc, n * BANK:n * BANK + w],
                                      start=(kc == 0), stop=(kc == KC - 1))
                    last.then_inc(pe_row, 1)

                pe.wait_ge(dve_tr, 4)
                rows(0)
                transpose_rows(1, MV, 0)
                pe.wait_ge(dve_q, 1)
                pe.wait_ge(act_rows, 3)
                rows(1)

                pe.wait_ge(dve_tr, 8)
                pe.wait_ge(ld_cnv, 16 * KC)

                def conv(i):
                    if i >= 2:
                        pe.wait_ge(dve_cnv, i - 1)
                    for which, (b, half) in enumerate(((0, 0), (1, 0), (0, 1))):
                        for kc in range(KC):
                            last = mm(bank(2 * (i % 2) + b)[:, half * S:(half + 1) * S],
                                      w_cnv[:, kc, which * CONVW + i * P:which * CONVW + (i + 1) * P], XT[:, kc, :],
                                      start=(kc == 0), stop=(kc == KC - 1))
                    last.then_inc(pe_cnv, 1)

                for i in range(CC - 1):
                    conv(i)
                pe.wait_ge(dve_rope, 2)
                pe.wait_ge(act_rows, 6)
                for j in range(J):
                    for t in range(T):
                        tr(bank(4 + j // 2)[:, (j % 2) * S + t * P:(j % 2) * S + (t + 1) * P], qrot[:, t, j * P:(j + 1) * P])
                for kd in range(2):
                    for t in range(T):
                        last = tr(bank(6)[:, kd * S + t * P:kd * S + (t + 1) * P], krot[:, t, 1 + kd, :])
                last.then_inc(pe_qkT, 1)
                for v, src in enumerate((krot, vrow)):
                    if v == 1:
                        pe.wait_ge(dve_cnv, CC - 1)
                    for g in range(G):
                        for t in range(T):
                            for i in range(2):
                                last = mm((bank(7) if v == 0 else bank(0))[i * HD:(i + 1) * HD, g * S + t * P:g * S + (t + 1) * P],
                                          src[:, t, 0, g * HD:(g + 1) * HD], ident[:], start=True, stop=True)
                    last.then_inc(pe_cT, 1)
                conv(CC - 1)
                pe.wait_ge(ld_c1, 32)
                pe.wait_ge(dve_cnv, CC - 1)
                pe.wait_ge(dve_blk, 16)
                pe.wait_ge(dve_cnv, CC)
                for m in range(MC):
                    for v in range(2):
                        last = mm(bank(1 + v)[32 * v:32 * v + 2 * NCMP, 0:CHID], blk[:, v, m].rearrange("p g c -> p (g c)"),
                                  w_c1[:, v, m, :], start=(m == 0), stop=(m == MC - 1))
                last.then_inc(pe_hid, 1)

                def kv(i):
                    o = bank(KV_BANK[i])
                    if i < 4:
                        t, n = i // 2, i % 2
                        for kc in range(KC):
                            last = mm(o, MT[:, kc, t * P:(t + 1) * P], w_xv[:, kc, n * BANK:(n + 1) * BANK],
                                      start=(kc == 0), stop=(kc == KC - 1))
                    else:
                        for c in range(2):
                            m = 2 * (i - 4) + c
                            for kc in range(KC):
                                last = mm(o[:, c * S:(c + 1) * S], w_a[:, kc, m * P:(m + 1) * P], MT[:, kc, :],
                                          start=(kc == 0), stop=(kc == KC - 1))
                    last.then_inc(pe_kv, 1)

                pe.wait_ge(ld_xv, 16)
                kv(0)
                for v in range(2):
                    pe.wait_ge(act_hid, v + 1)
                    for c in range(2):
                        q = slice(32 * v, 32 * v + 2 * NCMP)
                        last = nc.tensor.transpose(bank(3 - 2 * v)[:, c * 30:(c + 1) * 30],
                                                   hid[q, c * P:(c + 1) * P], ident[q, q])
                last.then_inc(pe_hidT, 1)
                kv(1)
                pe.wait_ge(dve_hT, 1)
                pe.wait_ge(ld_misc, 64)
                for g in range(G):
                    for c in range(2):
                        mm(bank(2)[g * HD:(g + 1) * HD, 0:NCMP], w_c2[:, 0, c, :], hT[:, 0, c, g * NCMP:(g + 1) * NCMP],
                           start=(c == 0), stop=(c == 1))
                for g in range(G):
                    for c in range(2):
                        last = mm(bank(2)[0:NCMP, 128 + g * HD:128 + (g + 1) * HD], hT[:, 1, c, g * NCMP:(g + 1) * NCMP],
                                  w_c2[:, 1, c, :], start=(c == 0), stop=(c == 1))
                last.then_inc(pe_ckv, 1)
                kv(2)
                pe.wait_ge(dve_ckv, 2)
                pe.wait_ge(act_qkT, 3)
                for t in range(T):
                    for j in range(J):
                        for g in range(G):
                            gp = slice(g * HD, (g + 1) * HD)
                            last = mm(bank(4 + g)[:, t * 60 + j * 15:t * 60 + j * 15 + 15], qT[gp, j, t * P:(t + 1) * P],
                                      kcT[gp, :], start=True, stop=True)
                last.then_inc(pe_cs, 1)

                def scores(n):
                    t, j = n // J, n % J
                    nk = P * (t + 1)
                    if n >= 1:
                        pe.wait_ge(dve_sm, n)
                    else:
                        pe.wait_ge(act_kv, 2)
                        pe.wait_ge(dve_blk, 16)
                    for g in range(G):
                        gp = slice(g * HD, (g + 1) * HD)
                        last = mm(bank(g).rearrange("p (k n) -> p k n", k=2)[:, :, 0:nk],
                                  qT[gp, j, t * P:(t + 1) * P], kT[gp, :, 0:nk], start=True, stop=True)
                    last.then_inc(pe_sc, 1)

                scores(0)
                kv(3)
                pe.wait_ge(dve_cp, 1)
                for t in range(T):
                    for g in range(G):
                        for j in range(J):
                            last = tr(bank(4 + 2 * t + g)[0:NCMP, j * P:(j + 1) * P], Pc[:, g, t, j, :])
                last.then_inc(pe_cpt, 1)

                def p_transposes(n):
                    t = n // J
                    pe.wait_ge(dve_p, n + 1)
                    pe.wait_ge(act_cpt, 4)
                    if n >= 1:
                        pe.wait_ge(act_pt, 2 * n)
                    for g in range(G):
                        for k in range(2):
                            for b in range(t + 1):
                                i = k * (t + 1) + b
                                last = tr(bank(4 + g)[:, i * P:(i + 1) * P], Pb[:, n % 2, g, k, b * P:(b + 1) * P])
                    last.then_inc(pe_pt, 1)

                def mix_out(t, part):
                    src = (oT, convT)[part]
                    for n in range(2):
                        for c in range(4):
                            last = mm(bank(4 * t + 2 * part + n), src[:, c, t * P:(t + 1) * P],
                                      w_out[:, 4 * part + c, n * BANK:(n + 1) * BANK], start=(c == 0), stop=(c == 3))
                    return last

                for n in range(T * J):
                    if n + 1 < T * J:
                        scores(n + 1)
                    if n in KV_AT:
                        u = KV_AT[n]
                        if u == 4:
                            pe.wait_ge(ld_xk, 16)
                            pe.wait_ge(act_kv, 3)
                        if u == 5:
                            pe.wait_ge(act_cpt, 4)
                        if u == 6:
                            pe.wait_ge(act_kv, 4)
                        if u == 7:
                            pe.wait_ge(act_kv, 5)
                        kv(u)
                    if n == T * J - 1:
                        pe.wait_ge(ld_out, 16 * 9)
                        pe.wait_ge(dve_csq, 1)
                        pe.wait_ge(act_kv, 8)
                        mix_out(0, 1)
                    p_transposes(n)
                    if n % J == J - 1:
                        t = n // J
                        pe.wait_ge(act_pt, 2 * (n + 1))
                        if t == 1:
                            pe.wait_ge(act_kv, 6)
                        nb = 2 * (t + 1)
                        for i in range(nb + 1):
                            for g in range(G):
                                o = bank(6 + t)[g * HD:(g + 1) * HD, :]
                                if i < nb:
                                    k, b = i // (t + 1), i % (t + 1)
                                    last = mm(o, vrow[:, b, 1 + k, g * HD:(g + 1) * HD], PT[g][:, i, :, :],
                                              start=(i == 0), stop=False)
                                else:
                                    last = mm(o, vc[:, g, :], PTc[:, g, t, :], start=False, stop=True)
                        last.then_inc(pe_pv, 1)

                pe.wait_ge(dve_sm, T * J)
                mix_out(0, 0).then_inc(pe_mo, 1)
                pe.wait_ge(dve_osq, 1)
                pe.wait_ge(pool_cst, 4)
                for t in range(T):
                    for part in range(2):
                        last = mm(bank(4)[:, 2 * t + part:2 * t + part + 1], sqs[:, part, t * P:(t + 1) * P],
                                  ones[:, 0:1], start=True, stop=True)
                last.then_inc(pe_ss, 1)
                mix_out(1, 1)

                def halves(t):
                    return bank(4 * t), bank(4 * t + 1)

                def eight_transposes(what, t, src):
                    for c in range(KC):
                        last = tr(bank(4 * t + c // 4)[:, (c % 4) * P:(c % 4 + 1) * P], src[:, c * P:(c + 1) * P])
                    last.then_inc(pe_two, 1)

                def ready(what, t):
                    pe.wait_ge(dve_two, TWO[what, t])
                    pe.wait_ge(act_two, TWO[what, t])

                def half_rows(t, n, lhs, w):
                    for c in range(KC):
                        last = mm(bank(4 * t + 2 + n), lhs(c), w[:, c, n * BANK:(n + 1) * BANK], start=(c == 0), stop=(c == KC - 1))
                    return last

                def ht(t):
                    return lambda c: XT[:, c, t * P:(t + 1) * P]

                def ot(t):
                    return lambda c: qo2[:, t, c, :]

                pe.wait_ge(act_sst, 1)
                mix_out(1, 0).then_inc(pe_mo, 1)
                pe.wait_ge(dve_h1, 1)
                eight_transposes("h1T", 0, H[:, 0, :])
                ready("h1T", 0)
                pe.wait_ge(ld_q2, 16)
                half_rows(0, 0, ht(0), w_a)
                pe.wait_ge(dve_h1, 2)
                eight_transposes("h1T", 1, H[:, 1, :])
                half_rows(0, 1, ht(0), w_a).then_inc(pe_two, 1)
                ready("h1T", 1)
                half_rows(1, 0, ht(1), w_a)
                ready("q", 0)
                eight_transposes("qT", 0, XS[:, 0, :])
                half_rows(1, 1, ht(1), w_a).then_inc(pe_two, 1)

                def scores2(t):
                    ready("qT", t)
                    for h in range(XH):
                        for c in range(2):
                            last = mm(bank(4 * t + 2, 2)[:, h * S:(h + 1) * S], qo2[:, t, 2 * h + c, :], MK[:, 2 * h + c, :],
                                      start=(c == 0), stop=(c == 1))
                    last.then_inc(pe_s2, 1)

                scores2(0)
                ready("q", 1)
                eight_transposes("qT", 1, XS[:, 1, :])
                scores2(1)
                for t in range(T):
                    pe.wait_ge(act_e2, XH * (t + 1))
                    for h in range(XH):
                        for m in range(2):
                            c = 2 * h + m
                            last = tr(bank(4 * t + c // 4)[:, (c % 4) * P:(c % 4 + 1) * P], P2[:, t, h, m * P:(m + 1) * P])
                    last.then_inc(pe_two, 1)
                for t in range(T):
                    ready("pT", t)
                    for h in range(XH):
                        for m in range(2):
                            last = mm(bank(4 * t + 2, 2)[:, h * XD:(h + 1) * XD], P2T[:, t, h, m, :],
                                      MV[:, m, h * XD:(h + 1) * XD], start=(m == 0), stop=(m == 1))
                    last.then_inc(pe_two, 1)
                ready("pv", 0)
                eight_transposes("oT", 0, XS[:, 0, :])
                ready("pv", 1)
                eight_transposes("oT", 1, XS[:, 1, :])
                pe.wait_ge(ld_o2, 16)
                ready("oT", 0)
                half_rows(0, 0, ot(0), w_o2).then_inc(pe_xo, 1)
                half_rows(0, 1, ot(0), w_o2).then_inc(pe_xo, 1)
                ready("oT", 1)
                half_rows(1, 0, ot(1), w_o2).then_inc(pe_xo, 1)
                pe.wait_ge(dve_h2, 2)
                eight_transposes("h2T", 0, H[:, 0, :])
                half_rows(1, 1, ot(1), w_o2).then_inc(pe_xo, 1)

                def router(t):
                    ready("h2T", t)
                    for kc in range(KC):
                        last = mm(bank(4 * t + 2)[:, 0:E], XT[:, kc, t * P:(t + 1) * P], w_rt[:, kc, :],
                                  start=(kc == 0), stop=(kc == KC - 1))
                    last.then_inc(pe_lg, 1)

                router(0)
                pe.wait_ge(dve_h2, 4)
                eight_transposes("h2T", 1, H[:, 1, :])
                router(1)
                pe.wait_ge(dve_g, 1)
                pe.wait_ge(pool_moe, 10)
                mm(bank(3)[:, 0:E], tri, gt[:, 0, :], start=True, stop=True)
                mm(bank(3)[:, E:2 * E], tri, gt[:, 1, :], start=True, stop=False)
                mm(bank(3)[:, E:2 * E], ones[:, 0:1].to_broadcast([P, P]), gt[:, 0, :], start=False, stop=True)
                for t in range(T):
                    last = mm(bank(3)[0:1, 2 * E:3 * E], ones[:, 0:1], gt[:, t, :], start=(t == 0), stop=(t == 1))
                last.then_inc(pe_cnt, 1)

                def gather():
                    for c in range(KC):
                        for t in range(T):
                            last = mm(bank(6 + c // 4)[:, (c % 4) * P:(c % 4 + 1) * P], XS[:, t, c * P:(c + 1) * P],
                                      sel1[:, t, :], start=(t == 0), stop=(t == 1))
                    return last

                def slot(h, j):
                    return (FILLS * h + j) % RING

                def at(r, p, h, j):
                    per = 32 * (HALF * FILLS // RING)
                    return r * (PAIRS // HALF * per) + p * per + 32 * ((FILLS * h + j) // RING + 1)

                pe.wait_ge(m_sel, 2)
                pe.wait_ge(act_xs, 2)
                gather().then_inc(m_gath, 1)
                pe.wait_ge(pool_bias, 1)
                with pe.Fori(0, ROUNDS) as r:
                    on = pe.value_load(flg[0:1, bass.ds(r, 1)], min_val=0, max_val=1)
                    with pe.If(on > 0):
                        with pe.Fori(0, PAIRS // HALF) as p:
                            for h in range(HALF):
                                k = r * PAIRS + p * HALF + h
                                pe.wait_ge(m_bsel, k + 1)
                                for n in range(4):
                                    last = mm(bank(n), bsel, b_prt[:, n * BANK:(n + 1) * BANK], start=True, stop=False,
                                              skip_group_check=True)
                                pe.wait_ge(m_xg, k + 1)
                                for j in range(KC):
                                    pe.wait_ge(arrived[slot(h, j)], at(r, p, h, j))
                                    for n in range(4):
                                        for s in range(2):
                                            last = mm(bank(n)[s * SLOTS:(s + 1) * SLOTS, :], xgT[:, j, s * SLOTS:(s + 1) * SLOTS],
                                                      ring[slot(h, j)][s][:, n * BANK:(n + 1) * BANK], start=False,
                                                      stop=(j == KC - 1), skip_group_check=True)
                                    last.then_inc(freed, 1)
                                pe.wait_ge(m_sel, 2 * k + 4)
                                pe.wait_ge(m_add, k * 4 + 1)
                                gather().then_inc(m_gath, 1)
                                pe.wait_ge(m_h, k + 1)
                                for f in range(KC):
                                    last = tr(bank(4 + f // 4)[:, (f % 4) * P:(f % 4 + 1) * P], ucl[:, f * P:(f + 1) * P])
                                last.then_inc(m_tr, 1)
                                pe.wait_ge(m_selg, 2 * k + 2)
                                pe.wait_ge(m_xg, k + 2)
                                for t in range(T):
                                    last = tr(bank(6)[:, t * P:(t + 1) * P], selg[:, t, :])
                                last.then_inc(m_sgT, 1)
                                pe.wait_ge(m_trD, k + 1)
                                pe.wait_ge(m_trA, k + 1)
                                for n in range(2):
                                    last = mm(bank(4 + n), bsel, b_prt[:, 2 * FF + n * BANK:2 * FF + (n + 1) * BANK],
                                              start=True, stop=False, skip_group_check=True)
                                last.then_inc(m_bias, 1)
                                for j in range(KC, FILLS):
                                    pe.wait_ge(arrived[slot(h, j)], at(r, p, h, j))
                                    for c in range(2):
                                        f = 2 * (j - KC) + c
                                        for n in range(2):
                                            for s in range(2):
                                                last = mm(bank(4 + n)[s * SLOTS:(s + 1) * SLOTS, :],
                                                          hTm[:, f, s * SLOTS:(s + 1) * SLOTS],
                                                          ring[slot(h, j)][s][:, c * D + n * BANK:c * D + (n + 1) * BANK],
                                                          start=False, stop=(f == KC - 1), skip_group_check=True)
                                    last.then_inc(freed, 1)
                                pe.wait_ge(m_oD, k + 1)
                                pe.wait_ge(m_oA, k + 1)
                                pe.wait_ge(m_sgTc, k + 1)
                                for q in range(4):
                                    t, n = q // 2, q % 2
                                    if q >= 2:
                                        pe.wait_ge(m_add, k * 4 + q)
                                    mm(bank(6 + n), selgT[:, t, :], orow[:, n * BANK:(n + 1) * BANK],
                                       start=True, stop=True).then_inc(m_y, 1)


_INS = ['x', 'mem', 'positions', 'g_mix_norm', 'w_mix_in', 'cmp_pos_k', 'cmp_pos_v', 'cmp_w1_k', 'cmp_b1_k',
        'cmp_w2_k', 'cmp_w1_v', 'cmp_b1_v', 'cmp_w2_v', 'conv_w', 'g_nsa_out', 'g_conv_out', 'w_mix_out',
        'g_xattn_norm', 'g_mem_norm', 'w_xq', 'w_xkv', 'w_xo', 'g_moe_norm', 'w_router', 'b_router', 'w_gate_up',
        'b_gate_up', 'w_down', 'b_down', 'g_final']


def kernel(**inputs):
    import concourse.bacc as _bacc
    from concourse.bass_utils import run_bass_kernel_spmd as _run

    nc = _bacc.Bacc("TRN2", target_bir_lowering=False, num_devices=1)
    arrays, args = {}, []
    half = HD // 2
    freq = (10000.0 ** (-np.arange(half) / half)).astype(np.float32).reshape(1, half)
    for name in _INS + ['inv_freq']:
        a = freq if name == 'inv_freq' else np.ascontiguousarray(inputs[name])
        arrays[f"in_{name}"] = a
        args.append(nc.dram_tensor(f"in_{name}", a.shape, mybir.dt.from_np(a.dtype), kind="ExternalInput").ap())
    args.append(nc.dram_tensor("out_0", (1, S, D), F32, kind="ExternalOutput").ap())
    trunk(nc, *args)
    r = _run(nc, [arrays], core_ids=[0])
    return r.results[0]["out_0"]
```

```python
import numpy as np
import concourse.bass as bass
from concourse import mybir
from contextlib import ExitStack

F32 = mybir.dt.float32
F32R = mybir.dt.float32r
BF16 = mybir.dt.bfloat16
I32 = mybir.dt.int32
ALU = mybir.AluOpType
ACT = mybir.ActivationFunctionType
AX = mybir.AxisListType.X

P = 128
BANK = 512
D = 1024
S = 256
T = S // P
KC = D // P
HD = 64
G, J = 2, 4
NSA = G * J * HD
ROWC = 1304
CONVW = 512
CC = CONVW // P
NCMP, CSTR, CLEN, CHID = 15, 16, 32, 256
MC = CLEN * HD // P
XH, XD = 4, 256
E = 32
FF = 1024
LIM, ALPHA = 7.0, 1.702
SLOTS = 64
PAIRS = E // 2
ROUNDS = S // SLOTS
FILLS = 12
RING = 8
HALF = 2
EPS = 1e-5
NEG = -1e30
R_MIX, R_XA, R_MEM, R_MOE, R_NSA, R_CNV, R_B1, R_CW, R_POS, R_END = 0, 8, 16, 24, 32, 36, 40, 44, 56, 88


def links(eng, default):
    count = {}

    def link(ins, sem=None):
        sem = default if sem is None else sem
        key = id(sem)
        count[key] = count.get(key, 0) + 1
        ins.then_inc(sem, 1)
        eng.wait_ge(sem, count[key])

    return link

def trunk(nc, x, mem, positions, g_mix_norm, w_mix_in, cmp_pos_k, cmp_pos_v, cmp_w1_k, cmp_b1_k,
          cmp_w2_k, cmp_w1_v, cmp_b1_v, cmp_w2_v, conv_w, g_nsa_out, g_conv_out, w_mix_out,
          g_xattn_norm, g_mem_norm, w_xq, w_xkv, w_xo, g_moe_norm, w_router, b_router, w_gate_up,
          b_gate_up, w_down, b_down, g_final, inv_freq, out):
    ctx = ExitStack()
    with ctx:
        def sb(name, shape, dt=F32):
            return ctx.enter_context(nc.sbuf_tensor(name, shape, dt))

        def sem(name):
            return ctx.enter_context(nc.semaphore(name))

        with ExitStack() as early:
            def parts(name, shape):
                return early.enter_context(nc.sbuf_tensor(name, shape, F32R))

            R_p = parts("R_p", [P, 24576])
            XS_p, MK_p, MV_p = parts("XS_p", [P, 2048]), parts("MK_p", [P, 2048]), parts("MV_p", [P, 2048])
            convT_p = parts("convT_p", [P, 1024])
        R = sb("R", [P, 24576])
        XS = sb("XS", [P, T, D])
        MK = sb("MK", [P, KC, S])
        MV = sb("MV", [P, T, D])
        convT = sb("convT", [P, CC, S])
        for part, whole in ((R_p, R), (XS_p, XS), (MK_p, MK), (MV_p, MV), (convT_p, convT)):
            assert nc.lookup_mloc(part).addr == nc.lookup_mloc(whole).addr
        A = sb("A", [P, 8192])
        H = sb("H", [P, T, D])
        XT = sb("XT", [P, KC, S])
        MT = sb("MT", [P, KC, S])
        w_row = R[:, 0:KC * ROWC].rearrange("p (k n) -> p k n", k=KC)
        w_cnv = R[:, KC * ROWC:KC * (ROWC + 3 * CONVW)].rearrange("p (k n) -> p k n", k=KC)
        w_out = R[:, 8192:16384].rearrange("p (k n) -> p k n", k=KC)
        w_xv = R[:, 0:8192].rearrange("p (k n) -> p k n", k=KC)
        w_o2 = R[:, 16384:24576].rearrange("p (h k n) -> p h k n", h=2, k=KC)
        tail = R[:, 16384:24576]
        w_a = A[:, :].rearrange("p (k n) -> p k n", k=KC)
        w_c1 = A[:, :].rearrange("p (v m n) -> p v m n", v=2, m=MC)

        ident = sb("ident", [P, P])
        prm_rows = sb("prm_rows", [R_END, P])
        prm = sb("prm", [P, R_END])
        ones = sb("ones", [P, 1])
        eps = sb("eps", [P, 1])
        ss = sb("ss", [P, 4])
        rst = sb("rst", [P, 4])
        pos_i = sb("pos_i", [P, T], I32)
        pos_f = sb("pos_f", [P, T])
        invf = sb("invf", [P, 32])
        ang = sb("ang", [P, T, 32])
        turn = sb("turn", [P, T, 32])
        rem = sb("rem", [P, 2, T, 32])
        trig = sb("trig", [P, 2, T, 32])
        QA = sb("QA", [P, 2048])
        KA = sb("KA", [P, 2048])
        qrot = QA[:, 0:1024].rearrange("p (t n) -> p t n", t=T)
        krot = KA[:, 0:768].rearrange("p (t k n) -> p t k n", t=T, k=3)
        vrow = KA[:, 768:1536].rearrange("p (t k n) -> p t k n", t=T, k=3)
        gates = sb("gates", [P, T, 24])
        ra = sb("ra", [P, 256])
        rb = sb("rb", [P, 256])
        qT = QA[:, 1024:2048].rearrange("p (j n) -> p j n", j=J)
        kT = KA[:, 1536:2048].rearrange("p (k n) -> p k n", k=2)
        mask = sb("mask", [P, S])
        cmask = sb("cmask", [P, T, NCMP])
        valid = sb("valid", [P, T])
        w_c2 = sb("w_c2", [P, 2, 2, HD])
        kcT = sb("kcT", [P, NCMP])
        vc = sb("vc", [NCMP, G, HD])
        nmx = sb("nmx", [P, 2, 4])
        smx = sb("smx", [P, 2, 4])
        cof = sb("cof", [P, 2, 4])
        cnm = sb("cnm", [P, 16])
        csm = sb("csm", [P, 16])
        w_rt = sb("w_rt", [P, KC, E])
        b_rt = sb("b_rt", [P, E])

        xsf = XS[:, :, :].rearrange("p t n -> p (t n)")
        mvf = MV[:, :, :].rearrange("p t n -> p (t n)")
        mkf = MK[:, :, :].rearrange("p a b -> p (a b)")
        mtf = MT[:, :, :].rearrange("p a b -> p (a b)")
        xtf = XT[:, :, :].rearrange("p a b -> p (a b)")
        ch_sb = xtf[:, 0:512].rearrange("p (b n) -> p b n", b=2)
        u_pad = xtf[:, 512:512 + S + 2]
        cy = xtf[:, 800:800 + S]
        cy2 = xtf[:, 1056:1056 + S]
        x_hi = XS_p[:, :].rearrange("p (k n) -> p k n", k=KC)
        x_lo = MV_p[:, :].rearrange("p (k n) -> p k n", k=KC)
        w_lo = R_p[:, KC * ROWC:KC * (ROWC + 3 * CONVW)].rearrange("p (k n) -> p k n", k=KC)
        last_r = R_p[:, 22720:23744]
        w_hi = [[t.rearrange("p (k n) -> p k n", k=KC) for t in unit] for unit in (
            [last_r, MK_p[:, 1024:2048], convT_p[:, :]],
            [R_p[:, 0:1024], R_p[:, 1024:2048], R_p[:, 2048:3072]],
            [R_p[:, 3072:4096], R_p[:, 4096:5120], R_p[:, 5120:6144]],
            [R_p[:, 8192:9216], R_p[:, 9216:10240], last_r])]

        def w_conv(w, i, which):
            return w[:, :, which * CONVW + i * P:which * CONVW + (i + 1) * P]

        kraw = mkf[:, 0:384].rearrange("p (k n) -> p k n", k=3)
        blk = mkf[:, 0:960].rearrange("p (v m g c) -> p v m g c", v=2, m=MC, g=G)
        hid = mkf[0:64, 960:960 + CHID]
        hx = mkf[:, 1472:1592]
        hy = mkf[:, 1592:1712]
        hTf = mkf[:, 1712:1832]
        hT = hTf.rearrange("p (v c n) -> p v c n", v=2, c=2)
        Pb = tail[:, 0:2048].rearrange("p (b g k n) -> p b g k n", b=2, g=2, k=2)
        oT = tail[:, 2048:3072].rearrange("p (j n) -> p j n", j=J)
        sqn = tail[:, 3072:4096].rearrange("p (t j n) -> p t j n", t=T, j=J)
        PTc = tail[0:NCMP, 3072:5120].rearrange("p (g t n) -> p g t n", g=G, t=T)
        Pcf = tail[:, 7168:7408]
        Pc = Pcf.rearrange("p (g t j c) -> p g t j c", g=G, t=T, j=J)
        PT = [tail[:, 5120:7168].rearrange("p (b j n) -> p b j n", b=4, j=J),
              xtf.rearrange("p (b j n) -> p b j n", b=4, j=J)]
        gsr = sb("gsr", [P, 4])
        sqs = sb("sqs", [P, 2, S])
        wo_hi = R_p[:, 0:8192].rearrange("p (k n) -> p k n", k=KC)
        wo_lo = R_p[:, 8192:16384].rearrange("p (k n) -> p k n", k=KC)
        mix_hi = [XS_p[:, (1 - part) * 1024:(2 - part) * 1024].rearrange("p (c n) -> p c n", c=4) for part in range(2)]
        mix_lo = [R_p[:, 16384 + 2048:16384 + 3072].rearrange("p (c n) -> p c n", c=4),
                  convT_p[:, :].rearrange("p (c n) -> p c n", c=4)]

        def of_tile(a, t):
            return a[:, :, t * P:(t + 1) * P]

        MIX_PARTS = {"conv": (convT[:], mix_hi[1], mix_lo[1])}
        for c in range(4, 8):
            MIX_PARTS["w", c] = (w_out[:, c, :], wo_hi[:, c, :], wo_lo[:, c, :])
        MIX_PARTS["o", 0] = tuple(of_tile(a, 0) for a in (oT, mix_hi[0], mix_lo[0]))
        for c in range(4):
            MIX_PARTS["w", c] = (w_out[:, c, :], wo_hi[:, c, :], wo_lo[:, c, :])
        MIX_PARTS["o", 1] = tuple(of_tile(a, 1) for a in (oT, mix_hi[0], mix_lo[0]))
        MIX_COUNT = {key: n + 1 for n, key in enumerate(MIX_PARTS)}
        MIX_AT = {1: ["conv", ("w", 4)], 2: [("w", 5)], 3: [("w", 6)], 4: [("w", 7)], 5: [("o", 0), ("w", 0)],
                  6: [("w", 1), ("w", 2)], 7: [("w", 3)]}
        P2 = xsf.rearrange("p (t h n) -> p t h n", t=T, h=XH)
        qo2 = mtf.rearrange("p (t c n) -> p t c n", t=T, c=KC)
        P2T = xtf.rearrange("p (t h m n) -> p t h m n", t=T, h=XH, m=2)
        ring = [[R[:, (2 * f + h) * 2048:(2 * f + h + 1) * 2048] for h in range(2)] for f in range(6)]
        ring = ring[0:4] + [[QA[:, :], KA[:, :]]] + ring[4:6] + [[mtf, xtf]]
        xgT = A[:, 0:1024].rearrange("p (k n) -> p k n", k=KC)
        gcl = A[:, 1024:2048]
        ucl = A[:, 2048:3072]
        sgm = A[:, 3072:4096]
        hTm = A[:, 4096:5120].rearrange("p (k n) -> p k n", k=KC)
        orow = A[:, 5120:6144]
        BW = 2 * FF + D
        b_raw = A[0:96, 0:BW]
        b_res = A[0:96, BW:2 * BW]
        b_prt = A[0:96, 2 * BW:2 * BW + BW // 2].bitcast(BF16)
        ROW = ROUNDS * E
        keys = mkf[:, 0:T * (ROW + 2)].rearrange("p (t c) -> p t c", t=T)
        gtab = mkf[:, 260:260 + T * (ROW + 2)].rearrange("p (t c) -> p t c", t=T)
        sel1 = mkf[:, 520:776].rearrange("p (t n) -> p t n", t=T)
        selg = mkf[:, 776:1032].rearrange("p (t n) -> p t n", t=T)
        selgT = mkf[:, 1032:1288].rearrange("p (t n) -> p t n", t=T)
        iot = mkf[:, 1288:1288 + SLOTS]
        bdiff = mkf[0:96, 1352:1352 + P]
        bsel = mkf[0:96, 1480:1480 + P // 2].bitcast(BF16)
        lg = mkf[:, 1552:1616].rearrange("p (t e) -> p t e", t=T)
        top = mkf[:, 1616:1632].rearrange("p (t e) -> p t e", t=T)
        gt = mkf[:, 1632:1696].rearrange("p (t e) -> p t e", t=T)
        eq = mkf[:, 1696:1760].rearrange("p (t e) -> p t e", t=T)
        cum = mkf[:, 1760:1824].rearrange("p (t e) -> p t e", t=T)
        need = mkf[:, 1824:1826]
        gex = mkf[:, 1826:1890].rearrange("p (t e) -> p t e", t=T)
        gsum = mkf[:, 1890:1892]
        gneg = mkf[:, 1892:1894]
        zer = mkf[:, 1894:1926]
        lead = mkf[0:96, 1959:1959 + ROUNDS * PAIRS + 1]
        cmx = mkf[0:1, 1958:1959]
        koff = mkf[:, 2030:2030 + ROUNDS]
        flg = sb("flg", [1, ROUNDS], I32)
        tri = ra[:, 0:P]
        gfin = mvf[:, 0:D]

        ps = ctx.enter_context(nc.psum_tensor("ps", [P, 8 * BANK], F32))

        def bank(i, n=1):
            return ps[:, i * BANK:(i + n) * BANK]

        ld_x, ld_mem, ld_prm, ld_misc, ld_pos = [sem(f"ld_x{i}") for i in range(T)], sem("ld_mem"), sem("ld_prm"), sem("ld_misc"), sem("ld_pos")
        ld_row = [sem(f"ld_row{i}") for i in range(KC)]
        ld_cnv, ld_c1, ld_out, ld_xv, ld_xk, ld_q2, ld_o2 = (sem("ld_cnv"), sem("ld_c1"), sem("ld_out"), sem("ld_xv"),
                                                            sem("ld_xk"), sem("ld_q2"), sem("ld_o2"))
        ld_bias, ld_end = sem("ld_bias"), sem("ld_end")
        pool_seq, pool_id, pool_cst, pool_moe = sem("pool_seq"), sem("pool_id"), sem("pool_cst"), sem("pool_moe")
        act_part, pool_res = sem("act_part"), sem("pool_res")
        dve_seq, act_seq = sem("dve_seq"), sem("act_seq")
        act_sqrt, dve_rstd, dve_norm = sem("act_sqrt"), sem("dve_rstd"), sem("dve_norm")
        pe_prm, dve_prm, dve_eps = sem("pe_prm"), sem("dve_prm"), sem("dve_eps")
        pe_tr, dve_tr = sem("pe_tr"), sem("dve_tr")
        dve_q = sem("dve_q")
        pe_row, dve_rope, act_rows = sem("pe_row"), sem("dve_rope"), sem("act_rows")
        dve_rem, act_trig = sem("dve_rem"), sem("act_trig")
        pe_cnv, act_ch, dve_cnv, dve_csq = sem("pe_cnv"), sem("act_ch"), sem("dve_cnv"), sem("dve_csq")
        act_hi, pool_xlo, pool_lo = sem("act_hi"), sem("pool_xlo"), sem("pool_lo")
        act_mhi, pool_mlo = sem("act_mhi"), sem("pool_mlo")
        pe_qkT, act_qkT = sem("pe_qkT"), sem("act_qkT")
        pe_cT, dve_blk = sem("pe_cT"), sem("dve_blk")
        pe_hid, act_hid, pe_hidT, dve_hx, act_hs, dve_hT = (sem("pe_hid"), sem("act_hid"), sem("pe_hidT"),
                                                           sem("dve_hx"), sem("act_hs"), sem("dve_hT"))
        pe_ckv, dve_ckv = sem("pe_ckv"), sem("dve_ckv")
        pe_cs, dve_cx, act_ce, dve_cp, pe_cpt, act_cpt = (sem("pe_cs"), sem("dve_cx"), sem("act_ce"),
                                                         sem("dve_cp"), sem("pe_cpt"), sem("act_cpt"))
        pe_kv, act_kv = sem("pe_kv"), sem("act_kv")
        pe_sc, dve_sx, act_e, dve_p, pe_pt, act_pt = (sem("pe_sc"), sem("dve_sx"), sem("act_e"), sem("dve_p"),
                                                     sem("pe_pt"), sem("act_pt"))
        dve_sm = sem("dve_sm")
        pe_pv, dve_o, act_osq, dve_osq = sem("pe_pv"), sem("dve_o"), sem("act_osq"), sem("dve_osq")
        pe_ss, act_sst, pe_mo, dve_h1 = sem("pe_ss"), sem("act_sst"), sem("pe_mo"), sem("dve_h1")
        pe_two, dve_two, act_two = sem("pe_two"), sem("dve_two"), sem("act_two")
        act_rt, dve_rt = sem("act_rt"), sem("dve_rt")
        pe_s2, dve_m2, act_e2, dve_sum2 = sem("pe_s2"), sem("dve_m2"), sem("act_e2"), sem("dve_sum2")
        pe_xo, dve_h2, act_xs = sem("pe_xo"), sem("dve_h2"), sem("act_xs")
        pe_lg, dve_ng, act_gx, dve_g, pe_cnt, dve_flg = (sem("pe_lg"), sem("dve_ng"), sem("act_gx"), sem("dve_g"),
                                                        sem("pe_cnt"), sem("dve_flg"))
        arrived = [sem(f"arrived{i}") for i in range(RING)]
        freed = sem("freed")
        m_swi = sem("m_swi")
        m_sel, m_selg, m_gath, m_xg = sem("m_sel"), sem("m_selg"), sem("m_gath"), sem("m_xg")
        m_bsel, m_bias, m_half = sem("m_bsel"), sem("m_bias"), sem("m_half")
        m_gcl, m_sg, m_h = sem("m_gcl"), sem("m_sg"), sem("m_h")
        m_tr, m_trD, m_trA, m_sgT, m_sgTc = sem("m_tr"), sem("m_trD"), sem("m_trA"), sem("m_sgT"), sem("m_sgTc")
        m_oA, m_oD, m_y, m_add = sem("m_oA"), sem("m_oD"), sem("m_y"), sem("m_add")
        f_go = sem("f_go")
        f_ss, f_root, f_rst, f_out, st_out = sem("f_ss"), sem("f_root"), sem("f_rst"), sem("f_out"), sem("st_out")

        x_v = x.rearrange("o (t p) n -> p (o t) n", p=P)
        mem_v = mem.rearrange("o (t p) n -> p (o t) n", p=P)
        out_v = out.rearrange("o (t p) n -> p (o t) n", p=P)

        KV_BANK = [7, 0, 3, 2, 3, 7, 2, 3]
        KV_AT = {0: [(3, 1), (4, 0)], 1: [(4, 1)], 2: [(5, 0)], 3: [(5, 1)], 4: [(6, 0)], 5: [(6, 1), (7, 0)], 6: [(7, 1)]}
        KV_DONE = {n: u for n, halves in KV_AT.items() for u, half in halves if half == 1}

        TWO = {x: n + 1 for n, x in enumerate([
            ("h1T", 0), ("h1T", 1), ("q", 0), ("qT", 0), ("q", 1), ("qT", 1), ("pT", 0), ("pv", 0),
            ("pT", 1), ("oT", 0), ("pv", 1), ("oT", 1), ("h2T", 0), ("h2T", 1)])}

        def chunked(w):
            return w.rearrange("(k p) n -> p k n", p=P)

        with nc.Block() as block:

            @block.sync
            def _(sp):
                def load_row(kc):
                    sp.dma_start(w_row[:, kc, :], w_mix_in[0, kc * P:(kc + 1) * P, 0:ROWC]).then_inc(ld_row[kc], 16)

                for t in range(T):
                    sp.dma_start(H[:, t, :], x_v[:, t, :]).then_inc(ld_x[t], 16)
                load_row(0)
                rows = [(R_MIX, g_mix_norm[0]), (R_XA, g_xattn_norm[0]), (R_MEM, g_mem_norm[0]),
                        (R_MOE, g_moe_norm[0]), (R_CNV, g_conv_out[0]), (R_B1, cmp_b1_k[0]), (R_B1 + 2, cmp_b1_v[0])]
                for r, v in rows:
                    n = v.shape[0] // P
                    sp.dma_start(prm_rows[r:r + n, :], v.rearrange("(r n) -> r n", n=P)).then_inc(ld_prm, 16)
                for g in range(G):
                    sp.dma_start(prm_rows[R_NSA:R_NSA + J, g * HD:(g + 1) * HD],
                                  g_nsa_out[0, g * J * HD:(g + 1) * J * HD].rearrange("(j d) -> j d", j=J)
                                  ).then_inc(ld_prm, 16)
                sp.dma_start(prm_rows[R_CW:R_CW + 12, :], conv_w[0].rearrange("k (c n) -> (k c) n", n=P)
                              ).then_inc(ld_prm, 16)
                for v, w in enumerate((cmp_pos_k, cmp_pos_v)):
                    sp.dma_start(prm_rows[R_POS + 16 * v:R_POS + 16 * (v + 1), :],
                                  w[0].rearrange("(m i) d -> m (i d)", i=2)).then_inc(ld_prm, 16)
                for kc in range(1, KC):
                    load_row(kc)
                for t in range(T):
                    sp.dma_start(MV[:, t, :], mem_v[:, t, :]).then_inc(ld_mem, 16)
                for kc in range(KC):
                    sp.dma_start(w_cnv[:, kc, :], w_mix_in[0, kc * P:(kc + 1) * P, ROWC:ROWC + 3 * CONVW]
                                 ).then_inc(ld_cnv, 16)
                for v, w in enumerate((cmp_w1_k, cmp_w1_v)):
                    sp.dma_start(w_c1[:, v, :, :], w[0].rearrange("(m p) n -> p m n", p=P)).then_inc(ld_c1, 16)
                sp.wait_ge(pe_cnv, CC - 1)
                sp.dma_start(w_xv, chunked(w_xkv[0, :, D:2 * D])).then_inc(ld_xv, 16)
                sp.wait_ge(pe_hid, 1)
                sp.dma_start(w_a, chunked(w_xkv[0, :, 0:D])).then_inc(ld_xk, 16)
                sp.wait_ge(pe_cnv, CC)
                nsa = w_mix_out[0, 0:NSA, :].rearrange("(g j d) n -> g j d n", g=G, j=J)
                for g in range(G):
                    for j in range(J):
                        sp.dma_start(w_out[g * HD:(g + 1) * HD, j, :], nsa[g, j]).then_inc(ld_out, 16)
                sp.dma_start(w_out[:, J:J + CC, :], chunked(w_mix_out[0, NSA:D, :])).then_inc(ld_out, 16)
                sp.wait_ge(pe_kv, 8)
                sp.dma_start(w_a, chunked(w_xq[0])).then_inc(ld_q2, 16)
                sp.wait_ge(pe_ss, 1)
                sp.wait_ge(pe_mo, T)
                for n in range(2):
                    sp.dma_start(w_o2[:, n], chunked(w_xo[0, :, n * BANK:(n + 1) * BANK])).then_inc(ld_o2, 16)
                sp.wait_ge(pe_two, TWO["q", 1])
                for part in range(3):
                    sp.dma_start(A[part * E:(part + 1) * E, 0:2 * FF], b_gate_up[0]).then_inc(ld_bias, 16)
                    sp.dma_start(A[part * E:(part + 1) * E, 2 * FF:BW], b_down[0]).then_inc(ld_bias, 16)

                def fill(p, h, j):
                    slot = (FILLS * h + j) % RING
                    for side in range(2):
                        e = p * (2 * HALF) + (2 * h + side)
                        if j < KC:
                            src = w_gate_up[0, bass.ds(e, 1), j * P:(j + 1) * P, :].rearrange("o p n -> p (o n)")
                            dst = ring[slot][side]
                        else:
                            f = (j - KC) * 2 * P
                            src = w_down[0, bass.ds(e, 1), f:f + 2 * P, :].rearrange("o (c p) n -> p (o c) n", p=P)
                            dst = ring[slot][side].rearrange("p (c n) -> p c n", c=2)
                        sp.dma_start(dst, src).then_inc(arrived[slot], 16)

                for h in range(HALF):
                    for j in range(FILLS):
                        n = FILLS * h + j
                        if n in (5, 6):
                            sp.wait_ge(pe_xo, n - 2)
                        if n == 7:
                            sp.wait_ge(pe_lg, T)
                        if n >= RING:
                            sp.wait_ge(freed, n - RING + 1)
                        fill(0, h, j)
                with sp.Fori(1, PAIRS // HALF) as p:
                    for h in range(HALF):
                        for j in range(FILLS):
                            sp.wait_ge(freed, p * (HALF * FILLS) + (FILLS * h + j - RING + 1))
                            fill(p, h, j)
                sp.wait_ge(dve_flg, 1)
                more = sp.value_load(flg[0:1, 1:2], min_val=0, max_val=1)
                with sp.If(more > 0):
                    with sp.Fori(1, ROUNDS) as r:
                        on = sp.value_load(flg[0:1, bass.ds(r, 1)], min_val=0, max_val=1)
                        with sp.If(on > 0):
                            with sp.Fori(0, PAIRS // HALF) as p:
                                for h in range(HALF):
                                    for j in range(FILLS):
                                        sp.wait_ge(freed, r * (PAIRS * FILLS) + p * (HALF * FILLS) + (FILLS * h + j - RING + 1))
                                        fill(p, h, j)
                for t in range(T):
                    sp.wait_ge(f_out, t + 1)
                    sp.dma_start(out_v[:, t, :], H[:, t, :]).then_inc(st_out, 16)
                sp.wait_ge(st_out, 16 * T)

            @block.gpsimd
            def _(pool):
                link = links(pool, pool_seq)
                link(nc.gpsimd.memset(ident[:], 0.0))
                nc.gpsimd.affine_select(out=ident[:], in_=ident[:], compare_op=ALU.not_equal, fill=1.0, base=0,
                                        pattern=[[-1, P]], channel_multiplier=1).then_inc(pool_id, 1)
                nc.gpsimd.memset(ones[:], 1.0).then_inc(pool_cst, 1)
                link(nc.gpsimd.memset(mask[:], 0.0))
                nc.gpsimd.affine_select(out=mask[:], in_=mask[:], compare_op=ALU.is_ge, fill=NEG, base=P,
                                        pattern=[[-1, S]], channel_multiplier=1).then_inc(pool_cst, 1)
                link(nc.gpsimd.memset(cmask[:], 0.0))
                nc.gpsimd.affine_select(out=cmask[:], in_=cmask[:], compare_op=ALU.is_ge, fill=NEG,
                                        base=-(CLEN - 1), pattern=[[P, T], [-CSTR, NCMP]],
                                        channel_multiplier=1).then_inc(pool_cst, 1)
                link(nc.gpsimd.memset(valid[:], 1.0))
                nc.gpsimd.affine_select(out=valid[:], in_=valid[:], compare_op=ALU.is_ge, fill=0.0,
                                        base=-(CLEN - 1), pattern=[[P, T]], channel_multiplier=1).then_inc(pool_cst, 1)
                pool.wait_ge(pe_tr, 8)
                pool.wait_ge(act_hi, 1)
                nc.gpsimd.tensor_tensor(x_lo, XT[:], x_hi, ALU.subtract).then_inc(pool_xlo, 1)
                for i in range(CC):
                    for which in range(3):
                        pool.wait_ge(act_hi, 3 * i + which + 2)
                        nc.gpsimd.tensor_tensor(w_conv(w_lo, i, which), w_conv(w_cnv, i, which), w_hi[i][which], ALU.subtract).then_inc(pool_lo, 1)
                for key, (whole, high, low) in MIX_PARTS.items():
                    pool.wait_ge(act_mhi, MIX_COUNT[key])
                    nc.gpsimd.tensor_tensor(low, whole, high, ALU.subtract).then_inc(pool_mlo, 1)
                pool.wait_ge(pe_s2, T)
                link(nc.gpsimd.iota(iot, pattern=[[1, SLOTS]], base=0, channel_multiplier=0,
                               allow_small_or_imprecise_dtypes=True), pool_moe)
                for part in range(3):
                    link(nc.gpsimd.iota(mkf[part * E:(part + 1) * E, 1352:1352 + P].rearrange("p (s n) -> p s n", s=2),
                                   pattern=[[-1, 2], [0, SLOTS]], base=0, channel_multiplier=1,
                                   allow_small_or_imprecise_dtypes=True), pool_moe)
                link(nc.gpsimd.iota(lead[:, 0:ROUNDS * PAIRS], pattern=[[0, ROUNDS], [2, PAIRS]], base=0, channel_multiplier=0,
                               allow_small_or_imprecise_dtypes=True), pool_moe)
                link(nc.gpsimd.memset(lead[:, ROUNDS * PAIRS:ROUNDS * PAIRS + 1], 0.0), pool_moe)
                link(nc.gpsimd.memset(zer, 0.0), pool_moe)
                link(nc.gpsimd.iota(koff, pattern=[[-SLOTS, ROUNDS]], base=-1, channel_multiplier=0,
                                    allow_small_or_imprecise_dtypes=True), pool_moe)
                link(nc.gpsimd.memset(mkf[:, 0:520], -1.0), pool_moe)
                link(nc.gpsimd.memset(tri, 0.0))
                link(nc.gpsimd.affine_select(out=tri, in_=tri, compare_op=ALU.is_ge, fill=1.0, base=0,
                                             pattern=[[-1, P]], channel_multiplier=1), pool_moe)
                for part, src in ((1, b_raw), (2, b_res)):
                    for q in range(part * E, 96, E):
                        pool.wait_ge(act_part, 1 if part == 1 else 3)
                        link(nc.gpsimd.tensor_tensor(b_res[q:q + E], src[q:q + E], b_prt[q:q + E], ALU.subtract),
                             pool_res)

            @block.scalar
            def _(act):
                link = links(act, act_seq)
                def root(t, src, junk):
                    link(nc.scalar.activation(junk, src, ACT.Square, accum_out=ss[:, t:t + 1]))
                    return nc.scalar.activation(rst[:, t:t + 1], ss[:, t:t + 1], ACT.Sqrt, bias=eps[:], scale=1.0 / D)

                act.wait_ge(dve_eps, 1)
                link(nc.scalar.activation(rst[:, 0:1], eps[:], ACT.Sqrt))
                for t in range(T):
                    act.wait_ge(ld_x[t], 16)
                    root(t, H[:, t, :], XS[:, t, :]).then_inc(act_sqrt, 1)
                act.dma_start(pos_i[:], positions.rearrange("o (t p) -> p (o t)", p=P), allow_slow_non_contiguous=True).then_inc(ld_pos, 16)
                act.dma_start(invf[:], inv_freq.to_broadcast([P, 32])).then_inc(ld_pos, 16)
                act.wait_ge(dve_rem, 1)
                nc.scalar.activation(trig[:].rearrange("p a t n -> p (a t n)"), rem[:].rearrange("p a t n -> p (a t n)"),
                                     ACT.Sin).then_inc(act_trig, 1)
                act.wait_ge(dve_tr, 4)
                nc.scalar.copy(x_hi, XT[:]).then_inc(act_hi, 1)
                act.wait_ge(dve_norm, 2)
                act.wait_ge(ld_mem, 32)
                for t in range(T):
                    root(t, MV[:, t, :], mkf[:, t * D:(t + 1) * D]).then_inc(act_sqrt, 1)
                act.dma_start(b_rt[:], b_router.to_broadcast([P, E])).then_inc(ld_misc, 16)
                act.dma_start(w_rt[:], chunked(w_router[0])).then_inc(ld_misc, 16)
                for v, w in enumerate((cmp_w2_k, cmp_w2_v)):
                    act.dma_start(w_c2[:, v, :, :], w[0].rearrange("(c p) n -> p c n", p=P)).then_inc(ld_misc, 16)
                def high_parts(i):
                    for which in range(3):
                        nc.scalar.copy(w_hi[i][which], w_conv(w_cnv, i, which)).then_inc(act_hi, 1)

                for t in range(T):
                    if t == 1:
                        act.wait_ge(ld_cnv, 16 * KC)
                        high_parts(0)
                    act.wait_ge(pe_row, t + 1)
                    if t == 1:
                        act.wait_ge(dve_rope, 1)
                    pr = bank(4, 3)
                    nc.scalar.copy(kraw, pr[:, NSA:NSA + 768].rearrange("p (k n) -> p k n", k=3)[:, :, 0:P]).then_inc(act_rows, 1)
                    nc.scalar.copy(vrow[:, t, :, :],
                                   pr[:, 640:1408].rearrange("p (k n) -> p k n", k=3)[:, :, 0:P]).then_inc(act_rows, 1)
                    nc.scalar.activation(gates[:, t, :], pr[:, 1280:ROWC], ACT.Sigmoid).then_inc(act_rows, 1)

                def conv_h(i):
                    act.wait_ge(pe_cnv, i + 1)
                    if i >= 2:
                        act.wait_ge(dve_cnv, i - 1)
                    nc.scalar.copy(ch_sb[:, i % 2, :], bank(2 * (i % 2))[:, 0:S]).then_inc(act_ch, 1)

                for i in range(CC - 1):
                    high_parts(i + 1)
                    conv_h(i)
                act.wait_ge(pe_qkT, 1)
                nc.scalar.copy(qT[:, 0:2, :].rearrange("p a n -> p (a n)"), bank(4)).then_inc(act_qkT, 1)
                nc.scalar.copy(qT[:, 2:4, :].rearrange("p a n -> p (a n)"), bank(5)).then_inc(act_qkT, 1)
                nc.scalar.copy(kT.rearrange("p a n -> p (a n)"), bank(6)).then_inc(act_qkT, 1)
                conv_h(CC - 1)

                def kv_out(i):
                    act.wait_ge(pe_kv, i + 1)
                    dst = MV[:, i // 2, (i % 2) * BANK:(i % 2 + 1) * BANK] if i < 4 else mkf[:, (i - 4) * BANK:(i - 3) * BANK]
                    nc.scalar.copy(dst, bank(KV_BANK[i])).then_inc(act_kv, 1)

                act.wait_ge(pe_hid, 1)
                for v in range(2):
                    nc.scalar.copy(hid[32 * v:32 * v + 2 * NCMP, :], bank(1 + v)[32 * v:32 * v + 2 * NCMP, 0:CHID]
                                   ).then_inc(act_hid, 1)
                kv_out(0)
                act.wait_ge(dve_hx, 1)
                nc.scalar.activation(hy, hy, ACT.Sigmoid, scale=2.0 * 0.7978845608028654).then_inc(act_hs, 1)
                kv_out(1)
                act.wait_ge(dve_cx, 1)
                nc.scalar.activation(Pcf, Pcf, ACT.Exp).then_inc(act_ce, 1)
                kv_out(2)

                def exps(n):
                    t = n // J
                    nk = P * (t + 1)
                    act.wait_ge(dve_sx, n + 1)
                    for g in range(G):
                        for k in range(2):
                            nc.scalar.activation(Pb[:, n % 2, g, k, 0:nk], Pb[:, n % 2, g, k, 0:nk], ACT.Exp,
                                                 bias=nmx[:, n % 2, 2 * g + k:2 * g + k + 1],
                                                 accum_out=smx[:, n % 2, 2 * g + k:2 * g + k + 1]).then_inc(act_e, 1)

                def pt_out(n):
                    t, j = n // J, n % J
                    act.wait_ge(pe_pt, n + 1)
                    if t == 1:
                        act.wait_ge(pe_pv, 1)
                    for g in range(G):
                        nb = 2 * (t + 1)
                        nc.scalar.copy(PT[g][:, 0:nb, j, :], bank(4 + g)[:, 0:nb * P].rearrange("p (b n) -> p b n", b=nb)
                                       ).then_inc(act_pt, 1)

                exps(0)
                for i in range(4):
                    act.wait_ge(pe_cpt, 1)
                    nc.scalar.copy(PTc[:, i % 2, i // 2, :], bank(4 + i)[0:NCMP, :]).then_inc(act_cpt, 1)

                def o_squares(t):
                    act.wait_ge(dve_o, t + 1)
                    act.wait_ge(pe_pv, T)
                    nc.scalar.activation(sqn[:, t].rearrange("p j n -> p (j n)"), bank(6 if t == 0 else 7), ACT.Square
                                         ).then_inc(act_osq, 1)

                def mix_high(key):
                    if key == "conv":
                        act.wait_ge(dve_csq, 1)
                    if key == ("w", 4):
                        act.wait_ge(ld_out, 16 * 9)
                    if key[0] == "o":
                        act.wait_ge(dve_o, key[1] + 1)
                    whole, high, low = MIX_PARTS[key]
                    nc.scalar.copy(high, whole).then_inc(act_mhi, 1)

                for n in range(T * J):
                    if n >= 1:
                        exps(n)
                        pt_out(n - 1)
                    if n in KV_DONE:
                        kv_out(KV_DONE[n])
                    for key in MIX_AT.get(n, []):
                        mix_high(key)
                pt_out(T * J - 1)
                mix_high(("o", 1))
                for t in range(T):
                    o_squares(t)
                act.wait_ge(pe_ss, 1)
                nc.scalar.activation(gsr[:], bank(4)[:, 0:4], ACT.Sqrt, bias=eps[:], scale=1.0 / NSA).then_inc(act_sst, 1)

                def second(what, t, b, dst, scale=None):
                    act.wait_ge(pe_two, TWO[what, t])
                    nc.scalar.activation(dst, bank(b), ACT.Copy, scale=1.0 if scale is None else scale).then_inc(act_two, 1)

                def second_gain(what, t, row):
                    act.wait_ge(pe_two, TWO[what, t])
                    for c in range(4, KC):
                        ins = nc.scalar.activation(XT[:, c, t * P:(t + 1) * P], bank(4 * t + 1)[:, (c - 4) * P:(c - 3) * P],
                                                   ACT.Copy, scale=prm[:, row + c:row + c + 1])
                    ins.then_inc(act_two, 1)

                def qo_second(t):
                    return qo2[:, t, 4:8, :].rearrange("p c n -> p (c n)")

                for t in range(T):
                    act.wait_ge(dve_h1, t + 1)
                    root(t, H[:, t, :], mtf[:, t * D:(t + 1) * D]).then_inc(act_rt, 1)
                    second_gain("h1T", t, R_XA)
                act.wait_ge(dve_rt, 1)
                second("q", 0, 3, XS[:, 0, BANK:D], rst[:, 0:1])
                second("qT", 0, 1, qo_second(0))
                act.wait_ge(dve_rt, 2)
                second("q", 1, 7, XS[:, 1, BANK:D], rst[:, 1:2])

                def exps2(t):
                    act.wait_ge(dve_m2, t + 1)
                    act.wait_ge(pe_two, TWO["qT", t])
                    for h in range(XH):
                        nc.scalar.activation(P2[:, t, h, :], bank(4 * t + 2, 2)[:, h * S:(h + 1) * S], ACT.Exp,
                                             bias=cnm[:, XH * t + h:XH * t + h + 1], scale=XD ** -0.5,
                                             accum_out=csm[:, XH * t + h:XH * t + h + 1]).then_inc(act_e2, 1)

                second("qT", 1, 5, qo_second(1))
                def pv_second(t):
                    act.wait_ge(pe_two, TWO["pv", t])
                    act.wait_ge(dve_sum2, t + 1)
                    for h in (2, 3):
                        ins = nc.scalar.activation(XS[:, t, h * XD:(h + 1) * XD], bank(4 * t + 3)[:, (h - 2) * XD:(h - 1) * XD],
                                                   ACT.Copy, scale=csm[:, XH * t + h:XH * t + h + 1])
                    ins.then_inc(act_two, 1)

                exps2(0)
                second("pT", 0, 1, P2T[:, 0, 2:4].rearrange("p h m n -> p (h m n)"))
                exps2(1)
                act.wait_ge(ld_bias, 16 * 6)
                nc.scalar.copy(b_prt, b_raw).then_inc(act_part, 1)
                pv_second(0)
                second("pT", 1, 5, P2T[:, 1, 2:4].rearrange("p h m n -> p (h m n)"))
                second("oT", 0, 1, qo_second(0))
                pv_second(1)
                second("oT", 1, 5, qo_second(1))
                act.wait_ge(pe_two, TWO["pv", 1])
                act.dma_start(gfin, g_final.rearrange("(a n) -> a n", a=1).to_broadcast([P, D])).then_inc(ld_end, 16)
                for i, q in enumerate((E, 2 * E, 2 * E)):
                    act.wait_ge(pool_res, i + 1)
                    nc.scalar.copy(b_prt[q:q + E], b_res[q:q + E]).then_inc(act_part, 1)
                for t in range(T):
                    act.wait_ge(dve_h2, 2 * t + 2)
                    act.wait_ge(pe_two, TWO["oT", t])
                    root(t, H[:, t, :], XS[:, t, :]).then_inc(act_rt, 1)
                    second_gain("h2T", t, R_MOE)
                    act.wait_ge(dve_rt, T + t + 1)
                    nc.scalar.activation(XS[:, t, :], H[:, t, :], ACT.Copy, scale=rst[:, t:t + 1]).then_inc(act_xs, 1)
                for t in range(T):
                    act.wait_ge(dve_ng, t + 1)
                    nc.scalar.activation(gex[:, t, :], lg[:, t, :], ACT.Exp, bias=gneg[:, t:t + 1]).then_inc(act_gx, 1)

                def pair(r, p, h, k):
                    act.wait_ge(m_gcl, k + 1)
                    nc.scalar.activation(sgm, gcl, ACT.Sigmoid, scale=ALPHA).then_inc(m_sg, 1)
                    act.wait_ge(m_tr, k + 1)
                    nc.scalar.copy(hTm[:, 4:8, :].rearrange("p k n -> p (k n)"), bank(5)).then_inc(m_trA, 1)
                    act.wait_ge(freed, k * FILLS + FILLS)
                    nc.scalar.copy(orow[:, BANK:D], bank(5)).then_inc(m_oA, 1)

                with act.Fori(0, PAIRS // HALF) as p:
                    for h in range(HALF):
                        pair(0, p, h, p * HALF + h)
                act.wait_ge(dve_flg, 1)
                more = act.value_load(flg[0:1, 1:2], min_val=0, max_val=1)
                with act.If(more > 0):
                    with act.Fori(1, ROUNDS) as r:
                        on = act.value_load(flg[0:1, bass.ds(r, 1)], min_val=0, max_val=1)
                        with act.If(on > 0):
                            with act.Fori(0, PAIRS // HALF) as p:
                                for h in range(HALF):
                                    pair(r, p, h, r * PAIRS + p * HALF + h)
                link(nc.scalar.activation(rst[:, 2:3], eps[:], ACT.Sqrt))
                act.wait_ge(f_go, 1)
                for t in range(T):
                    link(nc.scalar.activation(XS[:, t, :], H[:, t, :], ACT.Square, accum_out=ss[:, t:t + 1]), f_ss)
                    nc.scalar.activation(rst[:, t:t + 1], ss[:, t:t + 1], ACT.Sqrt, bias=eps[:], scale=1.0 / D
                                         ).then_inc(f_root, 1)

            @block.vector
            def _(dve):
                V = nc.vector
                link = links(dve, dve_seq)
                V.memset(eps[:], EPS).then_inc(dve_eps, 1)

                def tr_out(i, dst, b0, row):
                    for b in range(4):
                        dve.wait_ge(pe_tr, 4 * i + b + 1)
                        V.tensor_tensor(dst[:, 2 * b:2 * b + 2, :], bank(b0 + b).rearrange("p (a n) -> p a n", a=2),
                                        prm[:, row + 2 * b:row + 2 * b + 2].unsqueeze(2).to_broadcast([P, 2, S]),
                                        ALU.mult).then_inc(dve_tr, 1)

                def norm(src, dst, i):
                    for t in range(T):
                        dve.wait_ge(act_sqrt, T * i + t + 1)
                        link(V.reciprocal(rst[:, t:t + 1], rst[:, t:t + 1]), dve_rstd)
                        link(V.tensor_scalar(dst[:, t, :], src[:, t, :], rst[:, t:t + 1], None, ALU.mult), dve_norm)

                norm(H, XS, 0)
                dve.wait_ge(pe_prm, 1)
                link(V.tensor_copy(prm[:], bank(7)[:, 0:R_END]), dve_prm)
                tr_out(0, XT, 0, R_MIX)
                dve.wait_ge(ld_pos, 32)
                link(V.tensor_copy(pos_f[:], pos_i[:]))
                for t in range(T):
                    link(V.tensor_scalar(ang[:, t, :], invf[:], pos_f[:, t:t + 1], None, ALU.mult))
                big = 12582912.0
                link(V.tensor_scalar(turn[:], ang[:], 0.15915494309189535, None, ALU.mult))
                link(V.tensor_scalar(turn[:], turn[:], big, None, ALU.add))
                link(V.tensor_scalar(turn[:], turn[:], big, None, ALU.subtract))
                c1, c2 = 6.28125, 0.0019350051879882812
                c3 = 2.0 * np.pi - c1 - c2
                for c in (c1, c2, c3):
                    link(V.scalar_tensor_tensor(ang[:].rearrange("p t n -> p (t n)"), turn[:].rearrange("p t n -> p (t n)"),
                                                -float(c), ang[:].rearrange("p t n -> p (t n)"), ALU.mult, ALU.add))
                pi = 3.1415925
                link(V.tensor_scalar(rem[:, 0], ang[:], pi, -pi, ALU.min, ALU.max))
                link(V.tensor_scalar(ang[:], ang[:], float(np.pi / 2), None, ALU.add))
                link(V.tensor_scalar(turn[:], ang[:], pi, 2.0 * float(np.pi), ALU.is_gt, ALU.mult))
                link(V.tensor_tensor(ang[:], ang[:], turn[:], ALU.subtract))
                link(V.tensor_scalar(rem[:, 1], ang[:], pi, -pi, ALU.min, ALU.max), dve_rem)
                norm(MV, MV, 1)
                dve.wait_ge(act_trig, 1)

                def rope(a1, a2, o1, o2, t, n, shape, sem_last):
                    sin, cos = trig[:, 0, t, :], trig[:, 1, t, :]
                    def bc(w):
                        return w.unsqueeze(1).unsqueeze(1).to_broadcast([P] + shape + [32])
                    def tmp(b):
                        return b[:, 0:n].rearrange("p (a b d) -> p a b d", a=shape[0], b=shape[1])
                    V.tensor_tensor(tmp(ra), a1, bc(cos), ALU.mult)
                    link(V.tensor_tensor(tmp(rb), a2, bc(sin), ALU.mult))
                    link(V.tensor_tensor(o1, tmp(ra), tmp(rb), ALU.subtract))
                    V.tensor_tensor(tmp(ra), a2, bc(cos), ALU.mult)
                    link(V.tensor_tensor(tmp(rb), a1, bc(sin), ALU.mult))
                    link(V.tensor_tensor(o2, tmp(ra), tmp(rb), ALU.add), sem_last)

                for t in range(T):
                    if t == 1:
                        tr_out(1, MT, 0, R_MEM)
                    dve.wait_ge(pe_row, t + 1)
                    pr = bank(4, 3)
                    q4 = pr[:, 0:NSA].rearrange("p (g j d) -> p g j d", g=G, j=J)
                    o4 = qrot[:, t, :].rearrange("p (j g d) -> p g j d", g=G, j=J)
                    rope(q4[:, :, :, 0:32], q4[:, :, :, 32:64], o4[:, :, :, 0:32], o4[:, :, :, 32:64], t, 256, [G, J], dve_q)
                    dve.wait_ge(act_rows, 3 * t + 1)
                    k4 = kraw.rearrange("p k (g d) -> p k g d", g=G)
                    r4 = krot[:, t, :, :].rearrange("p k (g d) -> p k g d", g=G)
                    rope(k4[:, :, :, 0:32], k4[:, :, :, 32:64], r4[:, :, :, 0:32], r4[:, :, :, 32:64], t, 192, [3, G], dve_rope)

                dve.wait_ge(pool_xlo, 1)
                link(V.memset(u_pad[:, 0:2], 0.0))
                def conv(i):
                    dve.wait_ge(act_ch, i + 1)
                    b0 = 2 * (i % 2)
                    link(V.tensor_tensor(u_pad[:, 2:S + 2], bank(b0)[:, S:2 * S], ch_sb[:, i % 2, :], ALU.mult))
                    tap = [prm[:, R_CW + 4 * w + i:R_CW + 4 * w + i + 1] for w in range(3)]
                    link(V.tensor_scalar(cy, u_pad[:, 0:S], tap[0], None, ALU.mult))
                    link(V.scalar_tensor_tensor(cy2, u_pad[:, 1:S + 1], tap[1], cy, ALU.mult, ALU.add))
                    link(V.scalar_tensor_tensor(cy, u_pad[:, 2:S + 2], tap[2], cy2, ALU.mult, ALU.add))
                    link(V.tensor_tensor(convT[:, i, :], bank(b0 + 1)[:, 0:S], cy, ALU.mult), dve_cnv)

                def conv_end():
                    sqc = xtf[:, 0:1024].rearrange("p (c n) -> p c n", c=CC)
                    link(V.tensor_tensor(sqc, convT[:], convT[:], ALU.mult))
                    link(V.tensor_reduce(sqs[:, 1, :], sqc.rearrange("p c n -> p n c"), AX, ALU.add))
                    link(V.tensor_tensor(convT[:], convT[:], prm[:, R_CNV:R_CNV + CC].unsqueeze(2).to_broadcast([P, CC, S]),
                                         ALU.mult), dve_csq)

                for i in range(CC - 1):
                    conv(i)
                for v in range(2):
                    dve.wait_ge(pe_cT, v + 1)
                    for i in range(2):
                        src = (bank(7) if v == 0 else bank(0))[i * HD:(i + 1) * HD, :].rearrange(
                            "p (g c m i) -> p g c m i", g=G, m=8, i=2)
                        for mh in range(2):
                            for g in range(G):
                                link(V.tensor_tensor(
                                    blk[i * HD:(i + 1) * HD, v, 8 * mh:8 * mh + 8, g, :].rearrange("p m c -> p c m"),
                                    src[:, g, mh:mh + NCMP, :, i],
                                    prm[i * HD:(i + 1) * HD, R_POS + 16 * v + 8 * mh:R_POS + 16 * v + 8 * mh + 8
                                        ].unsqueeze(1).to_broadcast([HD, NCMP, 8]), ALU.add), dve_blk)
                conv(CC - 1)

                dve.wait_ge(pe_hidT, 1)
                for v in range(2):
                    link(V.tensor_tensor(hx[:, 60 * v:60 * v + 60].rearrange("p (a n) -> p a n", a=2),
                                         bank(3 - 2 * v)[:, 0:60].rearrange("p (a n) -> p a n", a=2),
                                         prm[:, R_B1 + 2 * v:R_B1 + 2 * v + 2].unsqueeze(2).to_broadcast([P, 2, 2 * NCMP]),
                                         ALU.add))
                link(V.tensor_tensor(hy, hx, hx, ALU.mult))
                link(V.tensor_scalar(hy, hy, 0.044715, 1.0, ALU.mult, ALU.add))
                link(V.tensor_tensor(hy, hy, hx, ALU.mult), dve_hx)
                dve.wait_ge(act_hs, 1)
                link(V.tensor_tensor(hTf, hx, hy, ALU.mult), dve_hT)
                conv_end()
                dve.wait_ge(pe_ckv, 1)
                link(V.tensor_copy(kcT[:], bank(2)[:, 0:NCMP]), dve_ckv)
                link(V.tensor_copy(vc[:].rearrange("p g d -> p (g d)"), bank(2)[0:NCMP, 128:256]), dve_ckv)

                dve.wait_ge(pe_cs, 1)
                dve.wait_ge(pool_cst, 4)
                for g in range(G):
                    for t in range(T):
                        link(V.scalar_tensor_tensor(Pc[:, g, t], bank(4 + g)[:, t * 60:t * 60 + 60].rearrange(
                            "p (j c) -> p j c", j=J), HD ** -0.5,
                            cmask[:, t, :].unsqueeze(1).to_broadcast([P, J, NCMP]), ALU.mult, ALU.add))
                pc16 = Pcf.rearrange("p (a c) -> p a c", c=NCMP)
                link(V.tensor_reduce(cnm[:], pc16, AX, ALU.max))
                link(V.tensor_tensor(pc16, pc16, cnm[:].unsqueeze(2).to_broadcast([P, 16, NCMP]), ALU.subtract), dve_cx)
                dve.wait_ge(act_ce, 1)
                link(V.tensor_reduce(csm[:], pc16, AX, ALU.add))
                link(V.reciprocal(csm[:], csm[:]))
                c4 = csm[:].rearrange("p (g t j) -> p g t j", g=G, t=T)
                for t in range(T):
                    gt0 = gates[:, t, :].rearrange("p (g j b) -> p g j b", g=G, j=J)[:, :, :, 0]
                    link(V.tensor_tensor(c4[:, :, t, :], c4[:, :, t, :], gt0, ALU.mult))
                    link(V.tensor_scalar(c4[:, :, t, :], c4[:, :, t, :], valid[:, t:t + 1], None, ALU.mult))
                link(V.tensor_tensor(pc16, pc16, csm[:].unsqueeze(2).to_broadcast([P, 16, NCMP]), ALU.mult), dve_cp)

                def mask_max(n):
                    t, b = n // J, n % 2
                    nk = P * (t + 1)
                    dve.wait_ge(pe_sc, n + 1)
                    if n >= 2:
                        dve.wait_ge(pe_pt, n - 1)
                    sc = bank(0, 2).rearrange("p (a n) -> p a n", a=4)[:, :, 0:nk]
                    pb = Pb[:, b].rearrange("p g k n -> p (g k) n")[:, :, 0:nk]
                    mk = mask[:, S - nk:S].unsqueeze(1).to_broadcast([P, 4, nk])
                    link(V.scalar_tensor_tensor(pb, sc, HD ** -0.5, mk, ALU.mult, ALU.add), dve_sm)
                    link(V.tensor_reduce(nmx[:, b, :], pb, AX, ALU.max, negate=True), dve_sx)

                def weigh(n):
                    t, j, b = n // J, n % J, n % 2
                    nk = P * (t + 1)
                    dve.wait_ge(act_e, 4 * (n + 1))
                    link(V.reciprocal(cof[:, b, :], smx[:, b, :]))
                    gt2 = gates[:, t, :].rearrange("p (g j b) -> p g j b", g=G, j=J)[:, :, j, 1:3]
                    c2 = cof[:, b, :].rearrange("p (g k) -> p g k", g=G)
                    link(V.tensor_tensor(c2, c2, gt2, ALU.mult))
                    pb = Pb[:, b].rearrange("p g k n -> p (g k) n")[:, :, 0:nk]
                    link(V.tensor_tensor(pb, pb, cof[:, b, :].unsqueeze(2).to_broadcast([P, 4, nk]), ALU.mult), dve_p)

                def o_out(t):
                    dve.wait_ge(pe_pv, t + 1)
                    link(V.tensor_tensor(oT[:, :, t * P:(t + 1) * P], bank(6 if t == 0 else 7).rearrange("p (j n) -> p j n", j=J),
                                         prm[:, R_NSA:R_NSA + J].unsqueeze(2).to_broadcast([P, J, P]), ALU.mult), dve_o)

                for n in range(T * J):
                    mask_max(n)
                    if n >= 1:
                        weigh(n - 1)
                    if n == J + 1:
                        o_out(0)
                weigh(T * J - 1)
                o_out(1)
                dve.wait_ge(act_osq, T)
                link(V.tensor_reduce(sqs[:, 0, :].rearrange("p (t n) -> p t n", t=T), sqn.rearrange("p t j n -> p t n j"),
                                     AX, ALU.add), dve_osq)
                dve.wait_ge(act_sst, 1)
                link(V.reciprocal(gsr[:], gsr[:]))

                def first_gain(what, t, row):
                    dve.wait_ge(pe_two, TWO[what, t])
                    V.tensor_tensor(XT[:, 0:4, t * P:(t + 1) * P], bank(4 * t).rearrange("p (c n) -> p c n", c=4),
                                    prm[:, row:row + 4].unsqueeze(2).to_broadcast([P, 4, P]), ALU.mult).then_inc(dve_two, 1)

                def first(what, t, b, dst):
                    dve.wait_ge(pe_two, TWO[what, t])
                    V.tensor_copy(dst, bank(b)).then_inc(dve_two, 1)

                def reciprocal_root(t, i):
                    dve.wait_ge(act_rt, T * i + t + 1)
                    link(V.reciprocal(rst[:, t:t + 1], rst[:, t:t + 1]), dve_rt)

                def qo_first(t):
                    return qo2[:, t, 0:4, :].rearrange("p c n -> p (c n)")

                def q_rows(t):
                    dve.wait_ge(pe_two, TWO["q", t])
                    V.tensor_scalar(XS[:, t, 0:BANK], bank(4 * t + 2), rst[:, t:t + 1], None, ALU.mult).then_inc(dve_two, 1)

                def max2(t):
                    dve.wait_ge(pe_s2, t + 1)
                    c = slice(XH * t, XH * (t + 1))
                    link(V.tensor_reduce(cnm[:, c], bank(4 * t + 2, 2).rearrange("p (h n) -> p h n", h=XH), AX, ALU.max,
                                         negate=True))
                    link(V.tensor_scalar(cnm[:, c], cnm[:, c], XD ** -0.5, None, ALU.mult), dve_m2)

                for t in range(T):
                    dve.wait_ge(pe_mo, t + 1)
                    for part in range(2):
                        link(V.scalar_tensor_tensor(H[:, t, :], bank(4 * t + 2 * part, 2), gsr[:, 2 * t + part:2 * t + part + 1],
                                                    H[:, t, :], ALU.mult, ALU.add), dve_h1 if part == 1 else None)
                    first_gain("h1T", t, R_XA)
                    reciprocal_root(t, 0)
                q_rows(0)
                first("qT", 0, 0, qo_first(0))
                q_rows(1)
                first("qT", 1, 4, qo_first(1))
                max2(0)
                max2(1)

                def pv_first(t):
                    dve.wait_ge(act_e2, XH * (t + 1))
                    c = slice(XH * t, XH * (t + 1))
                    link(V.reciprocal(csm[:, c], csm[:, c]), dve_sum2)
                    dve.wait_ge(pe_two, TWO["pv", t])
                    V.tensor_tensor(XS[:, t, 0:BANK].rearrange("p (h n) -> p h n", h=2),
                                    bank(4 * t + 2).rearrange("p (h n) -> p h n", h=2),
                                    csm[:, XH * t:XH * t + 2].unsqueeze(2).to_broadcast([P, 2, XD]), ALU.mult
                                    ).then_inc(dve_two, 1)

                first("pT", 0, 0, P2T[:, 0, 0:2].rearrange("p h m n -> p (h m n)"))
                pv_first(0)
                first("pT", 1, 4, P2T[:, 1, 0:2].rearrange("p h m n -> p (h m n)"))
                first("oT", 0, 0, qo_first(0))
                pv_first(1)
                first("oT", 1, 4, qo_first(1))
                for t in range(T):
                    for n in range(2):
                        dve.wait_ge(pe_xo, 2 * t + n + 1)
                        hn = H[:, t, n * BANK:(n + 1) * BANK]
                        link(V.tensor_tensor(hn, hn, bank(4 * t + 2 + n), ALU.add), dve_h2)
                    first_gain("h2T", t, R_MOE)
                    reciprocal_root(t, 1)

                dve.wait_ge(pool_moe, 10)
                dve.wait_ge(ld_misc, 64)
                for t in range(T):
                    dve.wait_ge(pe_lg, t + 1)
                    link(V.scalar_tensor_tensor(lg[:, t, :], bank(4 * t + 2)[:, 0:E], rst[:, t:t + 1], b_rt[:], ALU.mult, ALU.add))
                    link(V.max(top[:, t, :], lg[:, t, :]))
                    fourth = top[:, t, 3:4]
                    V.tensor_scalar(gt[:, t, :], lg[:, t, :], fourth, None, ALU.is_gt)
                    link(V.tensor_scalar(eq[:, t, :], lg[:, t, :], fourth, None, ALU.is_equal))
                    V.tensor_tensor_scan(cum[:, t, :], eq[:, t, :], zer, 0.0, ALU.add, ALU.add)
                    link(V.tensor_reduce(need[:, t:t + 1], gt[:, t, :], AX, ALU.add))
                    link(V.tensor_scalar(cum[:, t, :], cum[:, t, :], need[:, t:t + 1], 4.0, ALU.add, ALU.is_le))
                    link(V.tensor_tensor(eq[:, t, :], eq[:, t, :], cum[:, t, :], ALU.mult))
                    link(V.tensor_tensor(gt[:, t, :], gt[:, t, :], eq[:, t, :], ALU.add), dve_g)
                    link(V.tensor_scalar(gneg[:, t:t + 1], top[:, t, 0:1], -1.0, None, ALU.mult), dve_ng)

                def make_keys(t):
                    dve.wait_ge(pe_cnt, t + 1)
                    link(V.scalar_tensor_tensor(lg[:, t, :], bank(3 + 4 * t)[:, 0:E], 1.0, gt[:, t, :], ALU.add, ALU.mult))
                    link(V.tensor_tensor(keys[:, t, 0:ROW].rearrange("p (r e) -> p r e", r=ROUNDS),
                                         lg[:, t, :].unsqueeze(1).to_broadcast([P, ROUNDS, E]),
                                         koff.unsqueeze(2).to_broadcast([P, ROUNDS, E]), ALU.add))

                def build_sel(c):
                    for t in range(T):
                        yield V.tensor_tensor(sel1[:, t, :].rearrange("p (s n) -> p s n", s=2),
                                              iot.unsqueeze(1).to_broadcast([P, 2, SLOTS]),
                                              keys[:, t, bass.ds(c, 2)].unsqueeze(2).to_broadcast([P, 2, SLOTS]),
                                              ALU.is_equal)

                def build_selg(c):
                    for t in range(T):
                        yield V.tensor_tensor(selg[:, t, :].rearrange("p (s n) -> p s n", s=2),
                                              sel1[:, t, :].rearrange("p (s n) -> p s n", s=2),
                                              gtab[:, t, bass.ds(c, 2)].unsqueeze(2).to_broadcast([P, 2, SLOTS]),
                                              ALU.mult)

                def build_bsel(i):
                    return V.tensor_tensor(bsel, bdiff, lead[:, bass.ds(i, 1)].to_broadcast([96, P]), ALU.is_equal)

                def xg_out(i, n=1):
                    c = slice(4 * i, 4 * (i + n))
                    return V.tensor_tensor(xgT[:, c, :], bank(6 + i, n).rearrange("p (k n) -> p k n", k=4 * n),
                                           prm[:, R_MOE + 4 * i:R_MOE + 4 * (i + n)].unsqueeze(2).to_broadcast([P, 4 * n, P]),
                                           ALU.mult)

                dve.wait_ge(act_gx, 2)
                make_keys(0)
                make_keys(1)
                for ins in build_sel(0):
                    link(ins, m_sel)
                link(V.tensor_tensor(gex, gex, gt, ALU.mult))
                link(V.tensor_reduce(gsum, gex, AX, ALU.add))
                link(V.reciprocal(gsum, gsum))
                for t in range(T):
                    link(V.tensor_scalar(gtab[:, t, 0:ROW].rearrange("p (r e) -> p r e", r=ROUNDS),
                                         gex[:, t, :].unsqueeze(1).to_broadcast([P, ROUNDS, E]), gsum[:, t:t + 1], None, ALU.mult))
                dve.wait_ge(pe_cnt, T + 1)
                link(V.tensor_reduce(cmx, bank(2)[0:1, E:2 * E], AX, ALU.max))
                for r in range(ROUNDS):
                    link(V.tensor_scalar(flg[0:1, r:r + 1], cmx, float(SLOTS * r), None, ALU.is_gt),
                         dve_flg if r == ROUNDS - 1 else None)
                for ins in build_selg(0):
                    link(ins, m_selg)
                link(build_bsel(0), m_bsel)
                link(V.memset(cmx, 0.0), m_add)
                dve.wait_ge(pool_res, 3)
                for i in range(2):
                    dve.wait_ge((m_half, m_gath)[i], 1)
                    link(xg_out(i), m_xg)
                def pair(r, p, h, k):
                    dve.wait_ge(m_gath, k + 1)
                    dve.wait_ge(m_selg, 2 * k + 2)
                    for ins in build_sel(k * 2 + 2):
                        ins.then_inc(m_sel, 1)
                    dve.wait_ge(freed, k * FILLS + KC)
                    V.tensor_scalar(gcl, bank(0, 2), LIM, None, ALU.min).then_inc(m_gcl, 1)
                    V.tensor_scalar(ucl, bank(2, 2), LIM, -LIM, ALU.min, ALU.max).then_inc(m_swi, 1)
                    dve.wait_ge(m_gcl, k + 1)
                    dve.wait_ge(m_swi, k * 2 + 1)
                    V.scalar_tensor_tensor(ucl, ucl, 1.0, gcl, ALU.add, ALU.mult).then_inc(m_swi, 1)
                    dve.wait_ge(m_swi, k * 2 + 2)
                    dve.wait_ge(m_sg, k + 1)
                    V.tensor_tensor(ucl, ucl, sgm, ALU.mult).then_inc(m_h, 1)
                    dve.wait_ge(m_gath, k + 2)
                    xg_out(0, 2).then_inc(m_xg, 1)
                    dve.wait_ge(m_tr, k + 1)
                    V.tensor_copy(hTm[:, 0:4, :].rearrange("p k n -> p (k n)"), bank(4)).then_inc(m_trD, 1)
                    dve.wait_ge(m_sgT, k + 1)
                    V.tensor_copy(selgT.rearrange("p t n -> p (t n)"), bank(6)[:, 0:S]).then_inc(m_sgTc, 1)
                    dve.wait_ge(freed, k * FILLS + FILLS)
                    V.tensor_copy(orow[:, 0:BANK], bank(4)).then_inc(m_oD, 1)
                    dve.wait_ge(m_bias, k + 1)
                    build_bsel(k + 1).then_inc(m_bsel, 1)
                    dve.wait_ge(m_sel, 2 * k + 4)
                    for ins in build_selg(k * 2 + 2):
                        ins.then_inc(m_selg, 1)
                    for q in range(4):
                        t, n = q // 2, q % 2
                        hh = H[:, t, n * BANK:(n + 1) * BANK]
                        dve.wait_ge(m_y, k * 4 + q + 1)
                        V.tensor_tensor(hh, hh, bank(6 + n), ALU.add).then_inc(m_add, 1)
                    dve.wait_ge(m_add, k * 4 + 5)

                with dve.Fori(0, PAIRS // HALF) as p:
                    for h in range(HALF):
                        pair(0, p, h, p * HALF + h)
                more = dve.value_load(flg[0:1, 1:2], min_val=0, max_val=1)
                with dve.If(more > 0):
                    with dve.Fori(1, ROUNDS) as r:
                        on = dve.value_load(flg[0:1, bass.ds(r, 1)], min_val=0, max_val=1)
                        with dve.If(on > 0):
                            with dve.Fori(0, PAIRS // HALF) as p:
                                for h in range(HALF):
                                    pair(r, p, h, r * PAIRS + p * HALF + h)
                V.memset(cmx, 0.0).then_inc(f_go, 1)
                dve.wait_ge(ld_end, 16)
                for t in range(T):
                    dve.wait_ge(f_root, t + 1)
                    link(V.reciprocal(rst[:, t:t + 1], rst[:, t:t + 1]), f_rst)
                    V.scalar_tensor_tensor(H[:, t, :], H[:, t, :], rst[:, t:t + 1], gfin, ALU.mult, ALU.mult
                                           ).then_inc(f_out, 1)

            @block.tensor
            def _(pe):
                mm = nc.tensor.matmul

                def tr(dst, src):
                    k = src.shape[0]
                    return nc.tensor.transpose(dst, src, ident[0:k, 0:k])

                def keep_warm(n):
                    for _ in range(n):
                        mm(bank(0)[:, 0:P], ident[:], ident[:], start=True, stop=True)

                def transpose_rows(i, src, b0):
                    for t in range(T):
                        if i == 0 and t == 1:
                            pe.wait_ge(ld_prm, 16 * 12)
                            tr(bank(7)[:, 0:R_END], prm_rows[:]).then_inc(pe_prm, 1)
                        pe.wait_ge(dve_norm, 2 * i + t + 1)
                        for b in range(4):
                            for a in range(2):
                                c = 2 * b + a
                                last = tr(bank(b0 + b)[:, a * S + t * P:a * S + (t + 1) * P], src[:, t, c * P:(c + 1) * P])
                            if t == T - 1:
                                last.then_inc(pe_tr, 1)

                pe.wait_ge(pool_id, 1)
                transpose_rows(0, XS, 0)

                def rows(t):
                    for kc in range(KC):
                        pe.wait_ge(ld_row[kc], 16)
                        pe.wait_ge(dve_tr, kc // 2 + 1)
                        for n, w in ((0, BANK), (1, BANK), (2, ROWC - 2 * BANK)):
                            last = mm(bank(4 + n)[:, 0:w], XT[:, kc, t * P:(t + 1) * P], w_row[:, kc, n * BANK:n * BANK + w],
                                      start=(kc == 0), stop=(kc == KC - 1))
                    last.then_inc(pe_row, 1)

                rows(0)
                transpose_rows(1, MV, 0)
                pe.wait_ge(dve_q, 1)
                pe.wait_ge(act_rows, 3)
                rows(1)

                pe.wait_ge(dve_tr, 8)
                pe.wait_ge(pool_xlo, 1)

                def conv(i):
                    if i >= 2:
                        pe.wait_ge(dve_cnv, i - 1)
                    for which, (b, half) in enumerate(((0, 0), (1, 0), (0, 1))):
                        pe.wait_ge(pool_lo, 3 * i + which + 1)
                        hi, lo = w_hi[i][which], w_conv(w_lo, i, which)
                        for kc in range(KC):
                            for part, (w, xp) in enumerate(((hi, x_hi), (hi, x_lo), (lo, x_hi))):
                                last = mm(bank(2 * (i % 2) + b)[:, half * S:(half + 1) * S], w[:, kc, :], xp[:, kc, :],
                                          start=(kc == 0 and part == 0), stop=(kc == KC - 1 and part == 2))
                    last.then_inc(pe_cnv, 1)

                for i in range(CC - 1):
                    conv(i)
                pe.wait_ge(dve_rope, 2)
                pe.wait_ge(act_rows, 6)
                for j in range(J):
                    for t in range(T):
                        tr(bank(4 + j // 2)[:, (j % 2) * S + t * P:(j % 2) * S + (t + 1) * P], qrot[:, t, j * P:(j + 1) * P])
                for kd in range(2):
                    for t in range(T):
                        last = tr(bank(6)[:, kd * S + t * P:kd * S + (t + 1) * P], krot[:, t, 1 + kd, :])
                last.then_inc(pe_qkT, 1)
                for v, src in enumerate((krot, vrow)):
                    if v == 1:
                        pe.wait_ge(dve_cnv, CC - 1)
                    for g in range(G):
                        for t in range(T):
                            for i in range(2):
                                last = mm((bank(7) if v == 0 else bank(0))[i * HD:(i + 1) * HD, g * S + t * P:g * S + (t + 1) * P],
                                          src[:, t, 0, g * HD:(g + 1) * HD], ident[:], start=True, stop=True)
                    last.then_inc(pe_cT, 1)
                conv(CC - 1)
                def kv(i, half):
                    o = bank(KV_BANK[i])
                    if half == 0:
                        if i == 4:
                            pe.wait_ge(ld_xk, 16)
                            pe.wait_ge(act_kv, 3)
                        if i == 5:
                            pe.wait_ge(act_cpt, 4)
                        if i >= 6:
                            pe.wait_ge(act_kv, i - 2)
                    if i < 4:
                        t, n = i // 2, i % 2
                        for kc in range(4 * half, 4 * half + 4):
                            last = mm(o, MT[:, kc, t * P:(t + 1) * P], w_xv[:, kc, n * BANK:(n + 1) * BANK],
                                      start=(kc == 0), stop=(kc == KC - 1))
                    else:
                        m = 2 * (i - 4) + half
                        for kc in range(KC):
                            last = mm(o[:, half * S:(half + 1) * S], w_a[:, kc, m * P:(m + 1) * P], MT[:, kc, :],
                                      start=(kc == 0), stop=(kc == KC - 1))
                    if half == 1:
                        last.then_inc(pe_kv, 1)

                pe.wait_ge(ld_xv, 16)
                pe.wait_ge(dve_blk, 8)
                kv(0, 0)
                pe.wait_ge(ld_c1, 32)
                pe.wait_ge(dve_cnv, CC - 1)
                pe.wait_ge(dve_blk, 16)
                pe.wait_ge(dve_cnv, CC)
                for m in range(MC):
                    for v in range(2):
                        last = mm(bank(1 + v)[32 * v:32 * v + 2 * NCMP, 0:CHID], blk[:, v, m].rearrange("p g c -> p (g c)"),
                                  w_c1[:, v, m, :], start=(m == 0), stop=(m == MC - 1))
                last.then_inc(pe_hid, 1)

                kv(0, 1)
                for v in range(2):
                    pe.wait_ge(act_hid, v + 1)
                    for c in range(2):
                        q = slice(32 * v, 32 * v + 2 * NCMP)
                        last = nc.tensor.transpose(bank(3 - 2 * v)[:, c * 30:(c + 1) * 30],
                                                   hid[q, c * P:(c + 1) * P], ident[q, q])
                last.then_inc(pe_hidT, 1)
                kv(1, 0)
                kv(1, 1)
                pe.wait_ge(dve_hT, 1)
                pe.wait_ge(ld_misc, 64)
                for g in range(G):
                    for c in range(2):
                        mm(bank(2)[g * HD:(g + 1) * HD, 0:NCMP], w_c2[:, 0, c, :], hT[:, 0, c, g * NCMP:(g + 1) * NCMP],
                           start=(c == 0), stop=(c == 1))
                for g in range(G):
                    for c in range(2):
                        last = mm(bank(2)[0:NCMP, 128 + g * HD:128 + (g + 1) * HD], hT[:, 1, c, g * NCMP:(g + 1) * NCMP],
                                  w_c2[:, 1, c, :], start=(c == 0), stop=(c == 1))
                last.then_inc(pe_ckv, 1)
                kv(2, 0)
                pe.wait_ge(dve_ckv, 2)
                pe.wait_ge(act_qkT, 3)
                for t in range(T):
                    for j in range(J):
                        for g in range(G):
                            gp = slice(g * HD, (g + 1) * HD)
                            last = mm(bank(4 + g)[:, t * 60 + j * 15:t * 60 + j * 15 + 15], qT[gp, j, t * P:(t + 1) * P],
                                      kcT[gp, :], start=True, stop=True)
                last.then_inc(pe_cs, 1)

                def scores(n):
                    t, j = n // J, n % J
                    nk = P * (t + 1)
                    if n >= 1:
                        pe.wait_ge(dve_sm, n)
                    else:
                        pe.wait_ge(act_kv, 2)
                        pe.wait_ge(dve_blk, 16)
                    for g in range(G):
                        gp = slice(g * HD, (g + 1) * HD)
                        last = mm(bank(g).rearrange("p (k n) -> p k n", k=2)[:, :, 0:nk],
                                  qT[gp, j, t * P:(t + 1) * P], kT[gp, :, 0:nk], start=True, stop=True)
                    last.then_inc(pe_sc, 1)

                scores(0)
                kv(2, 1)
                kv(3, 0)
                pe.wait_ge(dve_cp, 1)
                for t in range(T):
                    for g in range(G):
                        for j in range(J):
                            last = tr(bank(4 + 2 * t + g)[0:NCMP, j * P:(j + 1) * P], Pc[:, g, t, j, :])
                last.then_inc(pe_cpt, 1)

                def p_transposes(n):
                    t = n // J
                    pe.wait_ge(dve_p, n + 1)
                    pe.wait_ge(act_cpt, 4)
                    if n >= 1:
                        pe.wait_ge(act_pt, 2 * n)
                    for g in range(G):
                        for k in range(2):
                            for b in range(t + 1):
                                i = k * (t + 1) + b
                                last = tr(bank(4 + g)[:, i * P:(i + 1) * P], Pb[:, n % 2, g, k, b * P:(b + 1) * P])
                    last.then_inc(pe_pt, 1)

                def mix_out(t, part, banks=(0, 1)):
                    pe.wait_ge(pool_mlo, MIX_COUNT["w", 7] if part == 1 else MIX_COUNT["o" if t else "w", 1 if t else 3])
                    high, low = mix_hi[part], mix_lo[part]
                    for n in banks:
                        for c in range(4):
                            for i, (a, w) in enumerate(((high, wo_hi), (high, wo_lo), (low, wo_hi))):
                                last = mm(bank(4 * t + 2 * part + n), a[:, c, t * P:(t + 1) * P],
                                          w[:, 4 * part + c, n * BANK:(n + 1) * BANK],
                                          start=(c == 0 and i == 0), stop=(c == 3 and i == 2))
                    return last

                def pv(t):
                    pe.wait_ge(act_pt, 2 * J * (t + 1))
                    if t == 1:
                        pe.wait_ge(act_kv, 6)
                    nb = 2 * (t + 1)
                    for i in range(nb + 1):
                        for g in range(G):
                            o = bank(6 + t)[g * HD:(g + 1) * HD, :]
                            if i < nb:
                                k, b = i // (t + 1), i % (t + 1)
                                last = mm(o, vrow[:, b, 1 + k, g * HD:(g + 1) * HD], PT[g][:, i, :, :],
                                          start=(i == 0), stop=False)
                            else:
                                last = mm(o, vc[:, g, :], PTc[:, g, t, :], start=False, stop=True)
                    last.then_inc(pe_pv, 1)

                for n in range(T * J):
                    if n + 1 < T * J:
                        scores(n + 1)
                    for unit, half in KV_AT.get(n, []):
                        kv(unit, half)
                    if n == T * J - 1:
                        pe.wait_ge(ld_out, 16 * 9)
                        pe.wait_ge(dve_csq, 1)
                        pe.wait_ge(act_kv, 8)
                        mix_out(0, 1, [0])
                    if n == J:
                        pv(0)
                    p_transposes(n)
                mix_out(0, 1, [1])
                pv(1)

                pe.wait_ge(dve_sm, T * J)
                mix_out(0, 0).then_inc(pe_mo, 1)
                pe.wait_ge(dve_osq, 1)
                pe.wait_ge(pool_cst, 4)
                for t in range(T):
                    for part in range(2):
                        last = mm(bank(4)[:, 2 * t + part:2 * t + part + 1], sqs[:, part, t * P:(t + 1) * P],
                                  ones[:, 0:1], start=True, stop=True)
                last.then_inc(pe_ss, 1)
                mix_out(1, 1)

                def halves(t):
                    return bank(4 * t), bank(4 * t + 1)

                def eight_transposes(what, t, src):
                    for c in range(KC):
                        last = tr(bank(4 * t + c // 4)[:, (c % 4) * P:(c % 4 + 1) * P], src[:, c * P:(c + 1) * P])
                    last.then_inc(pe_two, 1)

                def ready(what, t):
                    pe.wait_ge(dve_two, TWO[what, t])
                    pe.wait_ge(act_two, TWO[what, t])

                def half_rows(t, n, lhs, w):
                    for c in range(KC):
                        last = mm(bank(4 * t + 2 + n), lhs(c), w(c, n), start=(c == 0), stop=(c == KC - 1))
                    return last

                def wq(c, n):
                    return w_a[:, c, n * BANK:(n + 1) * BANK]

                def wo(c, n):
                    return w_o2[:, n, c, :]

                def ht(t):
                    return lambda c: XT[:, c, t * P:(t + 1) * P]

                def ot(t):
                    return lambda c: qo2[:, t, c, :]

                pe.wait_ge(act_sst, 1)
                mix_out(1, 0).then_inc(pe_mo, 1)
                pe.wait_ge(dve_h1, 1)
                eight_transposes("h1T", 0, H[:, 0, :])
                ready("h1T", 0)
                pe.wait_ge(ld_q2, 16)
                half_rows(0, 0, ht(0), wq)
                pe.wait_ge(dve_h1, 2)
                eight_transposes("h1T", 1, H[:, 1, :])
                half_rows(0, 1, ht(0), wq).then_inc(pe_two, 1)
                ready("h1T", 1)
                half_rows(1, 0, ht(1), wq)
                ready("q", 0)
                eight_transposes("qT", 0, XS[:, 0, :])
                half_rows(1, 1, ht(1), wq).then_inc(pe_two, 1)

                def scores2(t):
                    ready("qT", t)
                    for h in range(XH):
                        for c in range(2):
                            last = mm(bank(4 * t + 2, 2)[:, h * S:(h + 1) * S], qo2[:, t, 2 * h + c, :], MK[:, 2 * h + c, :],
                                      start=(c == 0), stop=(c == 1))
                    last.then_inc(pe_s2, 1)

                scores2(0)
                ready("q", 1)
                eight_transposes("qT", 1, XS[:, 1, :])
                scores2(1)

                def p2_transposes(t):
                    pe.wait_ge(act_e2, XH * (t + 1))
                    for h in range(XH):
                        for m in range(2):
                            c = 2 * h + m
                            last = tr(bank(4 * t + c // 4)[:, (c % 4) * P:(c % 4 + 1) * P], P2[:, t, h, m * P:(m + 1) * P])
                    last.then_inc(pe_two, 1)

                def pv2(t):
                    ready("pT", t)
                    for h in range(XH):
                        for m in range(2):
                            last = mm(bank(4 * t + 2, 2)[:, h * XD:(h + 1) * XD], P2T[:, t, h, m, :],
                                      MV[:, m, h * XD:(h + 1) * XD], start=(m == 0), stop=(m == 1))
                    last.then_inc(pe_two, 1)

                p2_transposes(0)
                pv2(0)
                p2_transposes(1)
                ready("pv", 0)
                eight_transposes("oT", 0, XS[:, 0, :])
                pv2(1)
                pe.wait_ge(ld_o2, 32)
                ready("oT", 0)
                half_rows(0, 0, ot(0), wo).then_inc(pe_xo, 1)
                ready("pv", 1)
                eight_transposes("oT", 1, XS[:, 1, :])
                half_rows(0, 1, ot(0), wo).then_inc(pe_xo, 1)
                ready("oT", 1)
                half_rows(1, 0, ot(1), wo).then_inc(pe_xo, 1)
                pe.wait_ge(dve_h2, 2)
                eight_transposes("h2T", 0, H[:, 0, :])
                half_rows(1, 1, ot(1), wo).then_inc(pe_xo, 1)

                def router(t):
                    ready("h2T", t)
                    for kc in range(KC):
                        last = mm(bank(4 * t + 2)[:, 0:E], XT[:, kc, t * P:(t + 1) * P], w_rt[:, kc, :],
                                  start=(kc == 0), stop=(kc == KC - 1))
                    last.then_inc(pe_lg, 1)

                router(0)
                pe.wait_ge(dve_h2, 4)
                eight_transposes("h2T", 1, H[:, 1, :])
                keep_warm(4)
                router(1)
                keep_warm(6)
                pe.wait_ge(dve_g, 1)
                pe.wait_ge(pool_moe, 10)
                mm(bank(3)[:, 0:E], tri, gt[:, 0, :], start=True, stop=True).then_inc(pe_cnt, 1)
                mm(bank(7)[:, 0:E], ones[:, 0:1].to_broadcast([P, P]), gt[:, 0, :], start=True, stop=False)
                pe.wait_ge(dve_g, 2)
                mm(bank(7)[:, 0:E], tri, gt[:, 1, :], start=False, stop=True).then_inc(pe_cnt, 1)
                for t in range(T):
                    last = mm(bank(2)[0:1, E:2 * E], ones[:, 0:1], gt[:, t, :], start=(t == 0), stop=(t == 1))
                last.then_inc(pe_cnt, 1)

                def gather():
                    for c in range(KC):
                        for t in range(T):
                            last = mm(bank(6 + c // 4)[:, (c % 4) * P:(c % 4 + 1) * P], XS[:, t, c * P:(c + 1) * P],
                                      sel1[:, t, :], start=(t == 0), stop=(t == 1))
                        if c == KC // 2 - 1:
                            last.then_inc(m_half, 1)
                    return last

                def slot(h, j):
                    return (FILLS * h + j) % RING

                def at(r, p, h, j):
                    per = 32 * (HALF * FILLS // RING)
                    return r * (PAIRS // HALF * per) + p * per + 32 * ((FILLS * h + j) // RING + 1)

                keep_warm(6)
                pe.wait_ge(m_sel, 2)
                pe.wait_ge(act_xs, 2)
                gather().then_inc(m_gath, 1)
                pe.wait_ge(act_part, 4)
                def pair(r, p, h, k):
                    pe.wait_ge(m_bsel, k + 1)
                    for n in range(4):
                        last = mm(bank(n), bsel, b_prt[:, n * BANK:(n + 1) * BANK], start=True, stop=False,
                                  skip_group_check=True)
                    pe.wait_ge(m_xg, k + 2)
                    for j in range(KC):
                        pe.wait_ge(arrived[slot(h, j)], at(r, p, h, j))
                        for n in range(4):
                            for s in range(2):
                                last = mm(bank(n)[s * SLOTS:(s + 1) * SLOTS, :], xgT[:, j, s * SLOTS:(s + 1) * SLOTS],
                                          ring[slot(h, j)][s][:, n * BANK:(n + 1) * BANK], start=False,
                                          stop=(j == KC - 1), skip_group_check=True)
                        last.then_inc(freed, 1)
                    pe.wait_ge(m_sel, 2 * k + 4)
                    pe.wait_ge(m_add, k * 4 + 1)
                    gather().then_inc(m_gath, 1)
                    pe.wait_ge(m_h, k + 1)
                    for f in range(KC):
                        last = tr(bank(4 + f // 4)[:, (f % 4) * P:(f % 4 + 1) * P], ucl[:, f * P:(f + 1) * P])
                    last.then_inc(m_tr, 1)
                    pe.wait_ge(m_selg, 2 * k + 2)
                    pe.wait_ge(m_xg, k + 3)
                    for t in range(T):
                        last = tr(bank(6)[:, t * P:(t + 1) * P], selg[:, t, :])
                    last.then_inc(m_sgT, 1)
                    pe.wait_ge(m_trD, k + 1)
                    pe.wait_ge(m_trA, k + 1)
                    for n in range(2):
                        last = mm(bank(4 + n), bsel, b_prt[:, 2 * FF + n * BANK:2 * FF + (n + 1) * BANK],
                                  start=True, stop=False, skip_group_check=True)
                    last.then_inc(m_bias, 1)
                    for j in range(KC, FILLS):
                        pe.wait_ge(arrived[slot(h, j)], at(r, p, h, j))
                        for c in range(2):
                            f = 2 * (j - KC) + c
                            for n in range(2):
                                for s in range(2):
                                    last = mm(bank(4 + n)[s * SLOTS:(s + 1) * SLOTS, :],
                                              hTm[:, f, s * SLOTS:(s + 1) * SLOTS],
                                              ring[slot(h, j)][s][:, c * D + n * BANK:c * D + (n + 1) * BANK],
                                              start=False, stop=(f == KC - 1), skip_group_check=True)
                        last.then_inc(freed, 1)
                    pe.wait_ge(m_oD, k + 1)
                    pe.wait_ge(m_oA, k + 1)
                    pe.wait_ge(m_sgTc, k + 1)
                    for q in range(4):
                        t, n = q // 2, q % 2
                        if q >= 2:
                            pe.wait_ge(m_add, k * 4 + q)
                        mm(bank(6 + n), selgT[:, t, :], orow[:, n * BANK:(n + 1) * BANK],
                           start=True, stop=True).then_inc(m_y, 1)

                with pe.Fori(0, PAIRS // HALF) as p:
                    for h in range(HALF):
                        pair(0, p, h, p * HALF + h)
                pe.wait_ge(dve_flg, 1)
                more = pe.value_load(flg[0:1, 1:2], min_val=0, max_val=1)
                with pe.If(more > 0):
                    with pe.Fori(1, ROUNDS) as r:
                        on = pe.value_load(flg[0:1, bass.ds(r, 1)], min_val=0, max_val=1)
                        with pe.If(on > 0):
                            with pe.Fori(0, PAIRS // HALF) as p:
                                for h in range(HALF):
                                    pair(r, p, h, r * PAIRS + p * HALF + h)


_INS = ['x', 'mem', 'positions', 'g_mix_norm', 'w_mix_in', 'cmp_pos_k', 'cmp_pos_v', 'cmp_w1_k', 'cmp_b1_k',
        'cmp_w2_k', 'cmp_w1_v', 'cmp_b1_v', 'cmp_w2_v', 'conv_w', 'g_nsa_out', 'g_conv_out', 'w_mix_out',
        'g_xattn_norm', 'g_mem_norm', 'w_xq', 'w_xkv', 'w_xo', 'g_moe_norm', 'w_router', 'b_router', 'w_gate_up',
        'b_gate_up', 'w_down', 'b_down', 'g_final']


def kernel(**inputs):
    import concourse.bacc as _bacc
    from concourse.bass_utils import run_bass_kernel_spmd as _run

    nc = _bacc.Bacc("TRN2", target_bir_lowering=False, num_devices=1)
    arrays, args = {}, []
    half = HD // 2
    freq = (10000.0 ** (-np.arange(half) / half)).astype(np.float32).reshape(1, half)
    for name in _INS + ['inv_freq']:
        a = freq if name == 'inv_freq' else np.ascontiguousarray(inputs[name])
        arrays[f"in_{name}"] = a
        args.append(nc.dram_tensor(f"in_{name}", a.shape, mybir.dt.from_np(a.dtype), kind="ExternalInput").ap())
    args.append(nc.dram_tensor("out_0", (1, S, D), F32, kind="ExternalOutput").ap())
    trunk(nc, *args)
    r = _run(nc, [arrays], core_ids=[0])
    return r.results[0]["out_0"]
```
